# Optimizing a Trainium2 kernel written in Bass

```python
import math
import jax, jax.numpy as jnp
from jax import lax
import numpy as np

D_MODEL = 1024
BATCH = 1
SEQ = 512
DEPTH = 2

DEEPNORM_ALPHA = (2 * DEPTH) ** 0.25
DEEPNORM_BETA = (8 * DEPTH) ** -0.25
LN_EPS = 1e-5
ROPE_THETA = 500000.0
ROPE_FRACTION = 4
RWKV_HEAD_DIM = 64
RWKV_DIM = D_MODEL // 2
RWKV_HEADS = RWKV_DIM // RWKV_HEAD_DIM
DECAY_LORA = max(32, int(round(1.8 * D_MODEL ** 0.5 / 32)) * 32)
ICLR_LORA = max(32, int(round(1.8 * D_MODEL ** 0.5 / 32)) * 32)
GATE_LORA = max(32, int(round(0.6 * D_MODEL ** 0.8 / 32)) * 32)
RWKV_GN_EPS = 64e-5
RWKV_PROJ_COLS = 3 * RWKV_DIM + DECAY_LORA + ICLR_LORA + GATE_LORA
MOBA_HEAD_DIM = 128
MOBA_WIDTH = D_MODEL - RWKV_DIM
MOBA_HEADS = MOBA_WIDTH // MOBA_HEAD_DIM
MOBA_BLOCK = 256
MOBA_TOPK = 3
MOBA_Q_CHUNK = 16
AB_IN_COLS = RWKV_PROJ_COLS + 3 * MOBA_WIDTH
AB_OUT_COLS = RWKV_DIM + MOBA_WIDTH
DIL_PAIRS = ((128, 1), (512, 4), (2048, 16))
DIL_GROUPS = len(DIL_PAIRS)
DIL_HEAD_DIM = 128
DIL_HEADS = D_MODEL // DIL_HEAD_DIM
C_WIDTH = DIL_HEADS * DIL_HEAD_DIM
C_IN_COLS = DIL_GROUPS * C_WIDTH + 2 * C_WIDTH
MLP_HIDDEN = 4 * D_MODEL
NEG_INF = -1e30


def _layer_norm(x, g, b):
    xf = x.astype(jnp.float32)
    mu = jnp.mean(xf, -1, keepdims=True)
    var = jnp.mean(jnp.square(xf - mu), -1, keepdims=True)
    return ((xf - mu) * lax.rsqrt(var + LN_EPS) * g + b).astype(x.dtype)

def _partial_rotary(x, pos):
    rot = x.shape[-1] // ROPE_FRACTION
    half = rot // 2
    inv_freq = ROPE_THETA ** (-jnp.arange(half, dtype=jnp.float32) / half)
    ang = pos.astype(jnp.float32)[:, None] * inv_freq[None, :]
    cos = jnp.cos(ang).astype(x.dtype)
    sin = jnp.sin(ang).astype(x.dtype)
    x1, x2, rest = x[..., :half], x[..., half:rot], x[..., rot:]
    return jnp.concatenate([x1 * cos - x2 * sin, x2 * cos + x1 * sin, rest], axis=-1)

def _token_shift(z):
    return jnp.pad(z, ((0, 0), (1, 0), (0, 0)))[:, :-1]

def _rwkv7_time_mix(z, shift_mix, w0, w_up, a0, a_up, g_up, k_k, k_a, r_k, lnx_g, lnx_b):
    B, T, _ = z.shape
    H, N = RWKV_HEADS, RWKV_HEAD_DIM
    f32 = jnp.float32
    z = z + (_token_shift(z) - z) * shift_mix
    o1, o2, o3 = RWKV_DIM, 2 * RWKV_DIM, 3 * RWKV_DIM
    o4 = o3 + DECAY_LORA
    o5 = o4 + ICLR_LORA
    r, k, v = z[..., :o1], z[..., o1:o2], z[..., o2:o3]
    w_d, a_d, g_d = z[..., o3:o4], z[..., o4:o5], z[..., o5:]
    w = -jax.nn.softplus(-(w0 + jnp.tanh(w_d) @ w_up)) - 0.5
    decay = jnp.exp(-jnp.exp(w.astype(f32)))
    a = jax.nn.sigmoid(a0 + a_d @ a_up).astype(f32)
    g = jax.nn.sigmoid(g_d) @ g_up
    heads = lambda t: t.astype(f32).reshape(B, T, H, N)
    kk = heads(k * k_k)
    kk = kk / jnp.maximum(jnp.linalg.norm(kk, axis=-1, keepdims=True), 1e-12)
    k = k.astype(f32) * (1.0 + (a - 1.0) * k_a)
    r, k, v, a, decay = heads(r), heads(k), heads(v), heads(a), heads(decay)

    def step(S, inp):
        r_t, w_t, k_t, v_t, a_t, b_t = inp
        sa = jnp.einsum('bhvk,bhk->bhv', S, a_t)
        S = S * w_t[:, :, None, :] + sa[..., None] * b_t[:, :, None, :] + v_t[..., None] * k_t[:, :, None, :]
        return S, jnp.einsum('bhvk,bhk->bhv', S, r_t)

    seq_first = lambda t: jnp.moveaxis(t, 1, 0)
    xs = (seq_first(r), seq_first(decay), seq_first(k), seq_first(v), seq_first(-kk), seq_first(kk * a))
    _, y = lax.scan(step, jnp.zeros((B, H, N, N), f32), xs)
    y = jnp.moveaxis(y, 0, 1)
    mu = jnp.mean(y, -1, keepdims=True)
    var = jnp.mean(jnp.square(y - mu), -1, keepdims=True)
    y = ((y - mu) * lax.rsqrt(var + RWKV_GN_EPS)).reshape(B, T, RWKV_DIM) * lnx_g + lnx_b
    bonus = jnp.sum(r * k * r_k, -1, keepdims=True) * v
    y = y + bonus.reshape(B, T, RWKV_DIM)
    return y * g

def _moba_attention(q, k, v):
    B, H, T, Dh = q.shape
    f32 = jnp.float32
    nb = -(-T // MOBA_BLOCK)
    Tp = nb * MOBA_BLOCK
    pad = ((0, 0), (0, 0), (0, Tp - T), (0, 0))
    q, k, v = jnp.pad(q, pad), jnp.pad(k, pad), jnp.pad(v, pad)
    scale = Dh ** -0.5
    kb = k.reshape(B, H, nb, MOBA_BLOCK, Dh)
    vb = v.reshape(B, H, nb, MOBA_BLOCK, Dh)
    n_sel = min(MOBA_TOPK, nb - 1)
    sel = None
    if n_sel > 0:
        k_mean = jnp.mean(kb.astype(f32), axis=3)
        gate = jnp.einsum('bhtd,bhnd->bhtn', q.astype(f32), k_mean)
        q_blk = jnp.arange(Tp) // MOBA_BLOCK
        past = jnp.arange(nb)[None, :] < q_blk[:, None]
        gate = jnp.where(past, gate, NEG_INF)
        _, sel = lax.top_k(gate, n_sel)
    bi = jnp.arange(B)[:, None, None, None]
    hi = jnp.arange(H)[None, :, None, None]

    def chunk(c):
        t0 = c * MOBA_Q_CHUNK
        i = t0 // MOBA_BLOCK
        qc = lax.dynamic_slice_in_dim(q, t0, MOBA_Q_CHUNK, axis=2)
        k_own = lax.dynamic_slice_in_dim(k, i * MOBA_BLOCK, MOBA_BLOCK, axis=2)
        v_own = lax.dynamic_slice_in_dim(v, i * MOBA_BLOCK, MOBA_BLOCK, axis=2)
        s_own = jnp.einsum('bhqd,bhkd->bhqk', qc, k_own).astype(f32) * scale
        causal = (i * MOBA_BLOCK + jnp.arange(MOBA_BLOCK))[None, :] <= (t0 + jnp.arange(MOBA_Q_CHUNK))[:, None]
        s_own = jnp.where(causal, s_own, NEG_INF)
        if n_sel == 0:
            p = jax.nn.softmax(s_own, axis=-1).astype(v.dtype)
            return jnp.einsum('bhqk,bhkd->bhqd', p, v_own)
        idx = lax.dynamic_slice_in_dim(sel, t0, MOBA_Q_CHUNK, axis=2)
        k_sel = kb[bi, hi, idx]
        v_sel = vb[bi, hi, idx]
        s_sel = jnp.einsum('bhqd,bhqskd->bhqsk', qc, k_sel).astype(f32) * scale
        valid = jnp.arange(n_sel) < i
        s_sel = jnp.where(valid[:, None], s_sel, NEG_INF)
        n_k = n_sel * MOBA_BLOCK
        s_all = jnp.concatenate([s_sel.reshape(B, H, MOBA_Q_CHUNK, n_k), s_own], axis=-1)
        p = jax.nn.softmax(s_all, axis=-1).astype(v.dtype)
        p_sel = p[..., :n_k].reshape(B, H, MOBA_Q_CHUNK, n_sel, MOBA_BLOCK)
        return (jnp.einsum('bhqsk,bhqskd->bhqd', p_sel, v_sel)
                + jnp.einsum('bhqk,bhkd->bhqd', p[..., n_k:], v_own))

    out = lax.map(chunk, jnp.arange(Tp // MOBA_Q_CHUNK))
    out = jnp.moveaxis(out, 0, 2).reshape(B, H, Tp, Dh)
    return out[:, :, :T]

def _dilated_window_branch(q, k, v, span, dilation):
    B, H, T, Dh = q.shape
    f32 = jnp.float32
    L = T // dilation
    W = span // dilation
    nblk = -(-L // W)
    Lp = nblk * W

    def strided(t):
        t = t.reshape(B, H, L, dilation, Dh).transpose(0, 1, 3, 2, 4)
        return jnp.pad(t, ((0, 0), (0, 0), (0, 0), (0, Lp - L), (0, 0)))

    qb = strided(q).reshape(B, H, dilation, nblk, W, Dh)
    kb = strided(k).reshape(B, H, dilation, nblk, W, Dh)
    vb = strided(v).reshape(B, H, dilation, nblk, W, Dh)
    prev = lambda t: jnp.pad(t, ((0, 0), (0, 0), (0, 0), (1, 0), (0, 0), (0, 0)))[:, :, :, :-1]
    k_band = jnp.concatenate([prev(kb), kb], axis=4)
    v_band = jnp.concatenate([prev(vb), vb], axis=4)
    s = jnp.einsum('bhrnqd,bhrnkd->bhrnqk', qb, k_band).astype(f32) * (Dh ** -0.5)
    qi = jnp.arange(W)[:, None]
    kj = jnp.arange(2 * W)[None, :]
    dist = W + qi - kj
    blk = jnp.arange(nblk)[:, None, None]
    mask = (dist >= 0) & (dist <= W) & ((blk > 0) | (kj >= W))
    s = jnp.where(mask, s, NEG_INF)
    lse = jax.nn.logsumexp(s, axis=-1)
    p = jnp.exp(s - lse[..., None]).astype(v.dtype)
    o = jnp.einsum('bhrnqk,bhrnkd->bhrnqd', p, v_band)
    o = o.reshape(B, H, dilation, Lp, Dh)[:, :, :, :L].transpose(0, 1, 3, 2, 4).reshape(B, H, T, Dh)
    lse = lse.reshape(B, H, dilation, Lp)[..., :L].transpose(0, 1, 3, 2).reshape(B, H, T)
    return o, lse

def _rwkv_moba_mixer(x, w_in, shift_mix, w0, w_up, a0, a_up, g_up, k_k, k_a, r_k, lnx_g, lnx_b, w_out, pos):
    B, T, _ = x.shape
    z = x @ w_in
    y_a = _rwkv7_time_mix(z[..., :RWKV_PROJ_COLS], shift_mix, w0, w_up, a0, a_up, g_up,
                          k_k, k_a, r_k, lnx_g, lnx_b)
    qkv = z[..., RWKV_PROJ_COLS:].reshape(B, T, 3, MOBA_HEADS, MOBA_HEAD_DIM).transpose(2, 0, 3, 1, 4)
    q = _partial_rotary(qkv[0], pos)
    k = _partial_rotary(qkv[1], pos)
    y_b = _moba_attention(q, k, qkv[2]).transpose(0, 2, 1, 3).reshape(B, T, MOBA_WIDTH)
    y = jnp.concatenate([y_a.astype(x.dtype), y_b.astype(x.dtype)], axis=-1)
    return (y @ w_out).astype(x.dtype)

def _dilated_mixer(x, w_in, w_out, pos):
    B, T, _ = x.shape
    z = x @ w_in
    nq = DIL_GROUPS * C_WIDTH
    q = z[..., :nq].reshape(B, T, DIL_GROUPS, DIL_HEADS, DIL_HEAD_DIM).transpose(0, 2, 3, 1, 4)
    kv = z[..., nq:].reshape(B, T, 2, DIL_HEADS, DIL_HEAD_DIM).transpose(2, 0, 3, 1, 4)
    q = _partial_rotary(q, pos)
    k = _partial_rotary(kv[0], pos)
    v = kv[1]
    outs, lses = [], []
    for g, (span, dilation) in enumerate(DIL_PAIRS):
        o, l = _dilated_window_branch(q[:, g], k, v, span, dilation)
        outs.append(o)
        lses.append(l)
    wts = jax.nn.softmax(jnp.stack(lses, axis=0), axis=0).astype(v.dtype)
    o = jnp.einsum('gbht,gbhtd->bhtd', wts, jnp.stack(outs, axis=0))
    o = o.transpose(0, 2, 1, 3).reshape(B, T, C_WIDTH)
    return (o @ w_out).astype(x.dtype)

def _sq_relu_mlp(x, w1, w2):
    return jnp.square(jax.nn.relu(x @ w1)) @ w2

def first_inputs(seed: int = 0) -> dict:
    key = jax.random.key(seed)
    ks = iter(jax.random.split(key, 24))
    f32 = jnp.float32
    nrm = lambda shape, scale: jax.random.normal(next(ks), shape, f32) * scale
    D = D_MODEL
    NE = (DEPTH + 1) // 2
    NO = DEPTH // 2
    x = nrm((BATCH, SEQ, D), 1.0)
    ab_w_in = nrm((NE, D, AB_IN_COLS), D ** -0.5)
    ab_shift_mix = jax.random.uniform(next(ks), (NE, RWKV_PROJ_COLS), f32)
    ab_w0 = jax.random.uniform(next(ks), (NE, RWKV_DIM), f32, minval=-6.0, maxval=0.0)
    ab_w_up = nrm((NE, DECAY_LORA, RWKV_DIM), 0.5 * DECAY_LORA ** -0.5)
    ab_a0 = nrm((NE, RWKV_DIM), 0.1)
    ab_a_up = nrm((NE, ICLR_LORA, RWKV_DIM), 0.5 * ICLR_LORA ** -0.5)
    ab_g_up = nrm((NE, GATE_LORA, RWKV_DIM), GATE_LORA ** -0.5)
    ab_k_k = 0.85 + nrm((NE, RWKV_DIM), 0.02)
    ab_k_a = 1.0 + nrm((NE, RWKV_DIM), 0.02)
    ab_r_k = nrm((NE, RWKV_HEADS, RWKV_HEAD_DIM), 0.1)
    ab_lnx_g = 1.0 + nrm((NE, RWKV_DIM), 0.02)
    ab_lnx_b = nrm((NE, RWKV_DIM), 0.02)
    ab_w_out = nrm((NE, AB_OUT_COLS, D), DEEPNORM_BETA * AB_OUT_COLS ** -0.5)
    c_w_in = nrm((NO, D, C_IN_COLS), D ** -0.5)
    c_w_out = nrm((NO, C_WIDTH, D), DEEPNORM_BETA * C_WIDTH ** -0.5)
    ln1_g = 1.0 + nrm((DEPTH, D), 0.02)
    ln1_b = nrm((DEPTH, D), 0.02)
    mlp_w1 = nrm((DEPTH, D, MLP_HIDDEN), D ** -0.5)
    mlp_w2 = nrm((DEPTH, MLP_HIDDEN, D), DEEPNORM_BETA * MLP_HIDDEN ** -0.5)
    ln2_g = 1.0 + nrm((DEPTH, D), 0.02)
    ln2_b = nrm((DEPTH, D), 0.02)
    return {'x': x, 'ab_w_in': ab_w_in, 'ab_shift_mix': ab_shift_mix, 'ab_w0': ab_w0,
            'ab_w_up': ab_w_up, 'ab_a0': ab_a0, 'ab_a_up': ab_a_up, 'ab_g_up': ab_g_up,
            'ab_k_k': ab_k_k, 'ab_k_a': ab_k_a, 'ab_r_k': ab_r_k, 'ab_lnx_g': ab_lnx_g,
            'ab_lnx_b': ab_lnx_b, 'ab_w_out': ab_w_out, 'c_w_in': c_w_in, 'c_w_out': c_w_out,
            'ln1_g': ln1_g, 'ln1_b': ln1_b, 'mlp_w1': mlp_w1, 'mlp_w2': mlp_w2,
            'ln2_g': ln2_g, 'ln2_b': ln2_b}

def first_block(x, ab_w_in, ab_shift_mix, ab_w0, ab_w_up, ab_a0, ab_a_up, ab_g_up, ab_k_k, ab_k_a,
              ab_r_k, ab_lnx_g, ab_lnx_b, ab_w_out, c_w_in, c_w_out, ln1_g, ln1_b, mlp_w1, mlp_w2,
              ln2_g, ln2_b):
    T = x.shape[1]
    pos = jnp.arange(T)
    for layer in range(DEPTH):
        j = layer // 2
        if layer % 2 == 0:
            h = _rwkv_moba_mixer(x, ab_w_in[j], ab_shift_mix[j], ab_w0[j], ab_w_up[j], ab_a0[j],
                                 ab_a_up[j], ab_g_up[j], ab_k_k[j], ab_k_a[j], ab_r_k[j],
                                 ab_lnx_g[j], ab_lnx_b[j], ab_w_out[j], pos)
        else:
            h = _dilated_mixer(x, c_w_in[j], c_w_out[j], pos)
        x = _layer_norm(DEEPNORM_ALPHA * x + h, ln1_g[layer], ln1_b[layer])
        x = _layer_norm(DEEPNORM_ALPHA * x + _sq_relu_mlp(x, mlp_w1[layer], mlp_w2[layer]),
                        ln2_g[layer], ln2_b[layer])
    return x


DA_HEADS = 4
DA_QK_DIM = 64
DA_V_DIM = 2 * DA_QK_DIM
RET_HEADS = 4
RET_QK_DIM = 64
RET_V_DIM = 64
RET_CHUNK = 128
SC_WIDTH = 256
SC_GROUPS = 4
CONV_W = 3
D_FF = 2816
REL_BUCKETS = 32
REL_MAX_DIST = 128
ROPE_THETA_2 = 10000.0
Q_BLOCK = 128
EPS = 1e-6
N_BRANCH = 3

DA_QK_W = DA_HEADS * 2 * DA_QK_DIM
DA_V_W = DA_HEADS * DA_V_DIM
RET_QK_W = RET_HEADS * RET_QK_DIM
RET_V_W = RET_HEADS * RET_V_DIM
IN_SPLITS = (DA_QK_W, DA_QK_W, DA_V_W,
             RET_QK_W, RET_QK_W, RET_V_W, RET_V_W,
             SC_WIDTH, SC_WIDTH, SC_WIDTH,
             N_BRANCH * D_MODEL)
IN_WIDTH = 2 * DA_QK_W + DA_V_W + 2 * RET_QK_W + 2 * RET_V_W + 3 * SC_WIDTH + N_BRANCH * D_MODEL


def rmsnorm(x, g):
    xf = x.astype(jnp.float32)
    y = xf * lax.rsqrt(jnp.mean(xf * xf, axis=-1, keepdims=True) + EPS)
    return (y * g.astype(jnp.float32)).astype(x.dtype)

def causal_dwconv(x, w, b):
    S = x.shape[1]
    K = w.shape[0]
    xp = jnp.pad(x, ((0, 0), (K - 1, 0), (0, 0)))
    y = b + xp[:, 0:S] * w[0]
    for k in range(1, K):
        y = y + xp[:, k:k + S] * w[k]
    return y

def rel_bucket(n):
    max_exact = REL_BUCKETS // 2
    nf = jnp.maximum(n, 1).astype(jnp.float32)
    large = max_exact + (jnp.log(nf / max_exact) / math.log(REL_MAX_DIST / max_exact)
                         * (REL_BUCKETS - max_exact)).astype(jnp.int32)
    large = jnp.minimum(large, REL_BUCKETS - 1)
    return jnp.where(n < max_exact, n, large)

def rotary(x, pos):
    d = x.shape[-1]
    half = d // 2
    inv = ROPE_THETA_2 ** (-jnp.arange(half, dtype=jnp.float32) / half)
    ang = pos.astype(jnp.float32)[:, None] * inv[None, :]
    cos = jnp.cos(ang)[None, :, None, :]
    sin = jnp.sin(ang)[None, :, None, :]
    xf = x.astype(jnp.float32)
    x1, x2 = xf[..., :half], xf[..., half:]
    return jnp.concatenate([x1 * cos - x2 * sin, x2 * cos + x1 * sin], axis=-1)

def diff_attention(q, k, v, lam, bias_dist):
    B, S, H = q.shape[0], q.shape[1], q.shape[2]
    qh = jnp.transpose(q, (0, 2, 3, 1, 4)).astype(jnp.float32)
    kh = jnp.transpose(k, (0, 2, 3, 1, 4)).astype(jnp.float32)
    vh = jnp.transpose(v, (0, 2, 1, 3)).astype(jnp.float32)
    kpos = jnp.arange(S)
    neg = jnp.finfo(jnp.float32).min

    def block(i):
        start = i * Q_BLOCK
        qb = lax.dynamic_slice_in_dim(qh, start, Q_BLOCK, axis=3)
        dist = (start + jnp.arange(Q_BLOCK))[:, None] - kpos[None, :]
        bias = jnp.transpose(bias_dist[jnp.maximum(dist, 0)], (2, 0, 1)).astype(jnp.float32)
        s = jnp.einsum('bhmqd,bhmkd->bhmqk', qb, kh) + bias[None, :, None]
        s = jnp.where(dist >= 0, s, neg)
        p = jax.nn.softmax(s, axis=-1)
        a = p[:, :, 0] - lam * p[:, :, 1]
        return jnp.einsum('bhqk,bhke->bhqe', a, vh)

    out = lax.map(block, jnp.arange(S // Q_BLOCK))
    return jnp.transpose(out, (1, 0, 3, 2, 4)).reshape(B, S, H, -1)

def retention(q, k, v):
    B, S, H, dk = q.shape
    dv = v.shape[-1]
    C = RET_CHUNK
    N = S // C
    lg = jnp.log(1.0 - 2.0 ** (-5.0 - jnp.arange(H, dtype=jnp.float32)))
    to_chunks = lambda t: jnp.transpose(t.astype(jnp.float32).reshape(B, N, C, H, t.shape[-1]), (0, 3, 1, 2, 4))
    qc, kc, vc = to_chunks(q), to_chunks(k), to_chunks(v)
    idx = jnp.arange(C, dtype=jnp.float32)
    diff = idx[:, None] - idx[None, :]
    d_intra = jnp.where(diff[None] >= 0, jnp.exp(lg[:, None, None] * jnp.maximum(diff, 0.0)[None]), 0.0)
    inner = jnp.einsum('bhncd,bhnjd->bhncj', qc, kc) * d_intra[None, :, None]
    inner = jnp.einsum('bhncj,bhnje->bhnce', inner, vc)
    k_dec = kc * jnp.exp(lg[:, None] * (C - 1 - idx)[None])[None, :, None, :, None]
    kv = jnp.einsum('bhncd,bhnce->nbhde', k_dec, vc)
    chunk_decay = jnp.exp(lg * C)[None, :, None, None]

    def step(R, kv_n):
        return R * chunk_decay + kv_n, R

    _, R_prev = lax.scan(step, jnp.zeros((B, H, dk, dv), jnp.float32), kv)
    q_dec = qc * jnp.exp(lg[:, None] * (idx + 1.0)[None])[None, :, None, :, None]
    cross = jnp.einsum('bhncd,nbhde->bhnce', q_dec, R_prev)
    o = inner + cross
    return jnp.transpose(o, (0, 2, 3, 1, 4)).reshape(B, S, H, dv)

def second_inputs(seed: int = 0) -> dict:
    key = jax.random.key(seed)
    ks = jax.random.split(key, 24)
    f32 = jnp.float32
    nrm = lambda k, shape, s: jax.random.normal(k, shape, f32) * s
    gain = lambda k, shape: 1.0 + 0.05 * jax.random.normal(k, shape, f32)
    return {
        "x": nrm(ks[0], (BATCH, SEQ, D_MODEL), 1.0),
        "rel_bias": nrm(ks[1], (REL_BUCKETS, DA_HEADS), 0.5),
        "norm_mix_g": gain(ks[2], (DEPTH, D_MODEL)),
        "w_in": nrm(ks[3], (DEPTH, D_MODEL, IN_WIDTH), D_MODEL ** -0.5),
        "b_gate": nrm(ks[4], (DEPTH, N_BRANCH * D_MODEL), 0.02),
        "da_q_norm_g": gain(ks[5], (DEPTH, DA_QK_DIM)),
        "da_k_norm_g": gain(ks[6], (DEPTH, DA_QK_DIM)),
        "da_lambda": nrm(ks[7], (DEPTH, 4, DA_QK_DIM), 0.1),
        "da_subln_g": gain(ks[8], (DEPTH, DA_V_DIM)),
        "ret_norm_g": gain(ks[9], (DEPTH, RET_V_DIM)),
        "sc_conv_w": nrm(ks[10], (DEPTH, CONV_W, SC_WIDTH), CONV_W ** -0.5),
        "sc_conv_b": nrm(ks[11], (DEPTH, SC_WIDTH), 0.02),
        "w_branch_da": nrm(ks[12], (DEPTH, DA_V_W, D_MODEL), DA_V_W ** -0.5),
        "w_branch_ret": nrm(ks[13], (DEPTH, RET_V_W, D_MODEL), RET_V_W ** -0.5),
        "w_branch_sc": nrm(ks[14], (DEPTH, SC_WIDTH, D_MODEL), SC_WIDTH ** -0.5),
        "w_out": nrm(ks[15], (DEPTH, D_MODEL, D_MODEL), 0.5 * D_MODEL ** -0.5),
        "norm_ffn_g": gain(ks[16], (DEPTH, D_MODEL)),
        "w_ffn_in": nrm(ks[17], (DEPTH, D_MODEL, 2 * D_FF), D_MODEL ** -0.5),
        "ffn_conv_w": nrm(ks[18], (DEPTH, CONV_W, D_FF), CONV_W ** -0.5),
        "ffn_conv_b": nrm(ks[19], (DEPTH, D_FF), 0.02),
        "w_ffn_out": nrm(ks[20], (DEPTH, D_FF, D_MODEL), 0.5 * D_FF ** -0.5),
    }

def second_block(x, rel_bias, norm_mix_g, w_in, b_gate, da_q_norm_g, da_k_norm_g, da_lambda,
              da_subln_g, ret_norm_g, sc_conv_w, sc_conv_b, w_branch_da, w_branch_ret,
              w_branch_sc, w_out, norm_ffn_g, w_ffn_in, ffn_conv_w, ffn_conv_b, w_ffn_out):
    B, S, D = x.shape
    pos = jnp.arange(S)
    bias_dist = rel_bias[rel_bucket(pos)]
    offs = np.cumsum(IN_SPLITS)[:-1].tolist()
    for l in range(DEPTH):
        h = rmsnorm(x, norm_mix_g[l])
        proj = jnp.einsum('bsd,de->bse', h, w_in[l])
        (da_q, da_k, da_v, r_q, r_k, r_v, r_g,
         sc_b, sc_c, sc_x, gate_pre) = jnp.split(proj, offs, axis=-1)

        lam_init = 0.8 - 0.6 * math.exp(-0.3 * l)
        lp = da_lambda[l].astype(jnp.float32)
        lam = jnp.exp(jnp.sum(lp[0] * lp[1])) - jnp.exp(jnp.sum(lp[2] * lp[3])) + lam_init
        q = rmsnorm(da_q.reshape(B, S, DA_HEADS, 2, DA_QK_DIM), da_q_norm_g[l]) * (DA_QK_DIM ** -0.5)
        k = rmsnorm(da_k.reshape(B, S, DA_HEADS, 2, DA_QK_DIM), da_k_norm_g[l])
        v = da_v.reshape(B, S, DA_HEADS, DA_V_DIM)
        o_da = diff_attention(q, k, v, lam, bias_dist)
        o_da = (rmsnorm(o_da, da_subln_g[l]) * (1.0 - lam_init)).astype(x.dtype).reshape(B, S, DA_V_W)

        rq = rotary(r_q.reshape(B, S, RET_HEADS, RET_QK_DIM), pos)
        rk = rotary(r_k.reshape(B, S, RET_HEADS, RET_QK_DIM), pos) * (RET_QK_DIM ** -0.5)
        rv = r_v.reshape(B, S, RET_HEADS, RET_V_DIM)
        o_ret = rmsnorm(retention(rq, rk, rv), ret_norm_g[l]).reshape(B, S, RET_V_W)
        o_ret = (o_ret * jax.nn.silu(r_g.astype(jnp.float32))).astype(x.dtype)

        o_sc = sc_b * causal_dwconv(sc_c * sc_x, sc_conv_w[l], sc_conv_b[l])

        gates = jax.nn.sigmoid((gate_pre + b_gate[l]).astype(jnp.float32)).astype(x.dtype)
        gates = gates.reshape(B, S, N_BRANCH, D)
        y = (gates[:, :, 0] * jnp.einsum('bse,ed->bsd', o_da, w_branch_da[l])
             + gates[:, :, 1] * jnp.einsum('bse,ed->bsd', o_ret, w_branch_ret[l])
             + gates[:, :, 2] * jnp.einsum('bse,ed->bsd', o_sc, w_branch_sc[l]))
        x = x + jnp.einsum('bsd,de->bse', y, w_out[l])

        h = rmsnorm(x, norm_ffn_g[l])
        gu = jnp.einsum('bsd,df->bsf', h, w_ffn_in[l])
        g_ff, u_ff = gu[..., :D_FF], gu[..., D_FF:]
        g_ff = causal_dwconv(g_ff, ffn_conv_w[l], ffn_conv_b[l])
        x = x + jnp.einsum('bsf,fd->bsd', jax.nn.silu(g_ff) * u_ff, w_ffn_out[l])
    return x


def setup_inputs(seed=0):
    out = dict(first_inputs(seed))
    for name, value in second_inputs(seed + 1).items():
        if name != "x":
            out[name + "_2"] = value
    return out


def reference(
    x, ab_w_in, ab_shift_mix, ab_w0, ab_w_up, ab_a0, ab_a_up, ab_g_up, ab_k_k, ab_k_a, ab_r_k,
    ab_lnx_g, ab_lnx_b, ab_w_out, c_w_in, c_w_out, ln1_g, ln1_b, mlp_w1, mlp_w2, ln2_g, ln2_b,
    rel_bias_2, norm_mix_g_2, w_in_2, b_gate_2, da_q_norm_g_2, da_k_norm_g_2, da_lambda_2,
    da_subln_g_2, ret_norm_g_2, sc_conv_w_2, sc_conv_b_2, w_branch_da_2, w_branch_ret_2,
    w_branch_sc_2, w_out_2, norm_ffn_g_2, w_ffn_in_2, ffn_conv_w_2, ffn_conv_b_2, w_ffn_out_2,
):
    x = first_block(
        x, ab_w_in, ab_shift_mix, ab_w0, ab_w_up, ab_a0, ab_a_up, ab_g_up, ab_k_k, ab_k_a,
        ab_r_k, ab_lnx_g, ab_lnx_b, ab_w_out, c_w_in, c_w_out, ln1_g, ln1_b, mlp_w1, mlp_w2,
        ln2_g, ln2_b,
    )
    return second_block(
        x, rel_bias_2, norm_mix_g_2, w_in_2, b_gate_2, da_q_norm_g_2, da_k_norm_g_2,
        da_lambda_2, da_subln_g_2, ret_norm_g_2, sc_conv_w_2, sc_conv_b_2, w_branch_da_2,
        w_branch_ret_2, w_branch_sc_2, w_out_2, norm_ffn_g_2, w_ffn_in_2, ffn_conv_w_2,
        ffn_conv_b_2, w_ffn_out_2,
    )


_drawn_inputs = setup_inputs


def setup_inputs(seed=0):
    import zlib

    import numpy as np

    out = dict(_drawn_inputs(seed))
    spreads = {}
    factors = {'ab_w_up': 8.0,
     'ab_a0': 7.384,
     'ab_k_k': 8.0,
     'ab_k_a': 8.0,
     'ab_lnx_g': 8.0,
     'ab_lnx_b': 8.0,
     'b_gate_2': 8.0,
     'da_q_norm_g_2': 7.361,
     'da_k_norm_g_2': 8.0,
     'da_lambda_2': 3.134,
     'da_subln_g_2': 4.283,
     'ret_norm_g_2': 5.718,
     'sc_conv_b_2': 7.062,
     'ffn_conv_b_2': 7.151}
    for name, (base, spread) in spreads.items():
        noise = np.random.default_rng([zlib.crc32(name.encode()), seed]).standard_normal(out[name].shape)
        drawn = base * np.exp(spread * noise) if base else spread * noise
        out[name] = __import__('jax').numpy.asarray(drawn.astype(out[name].dtype))
    for name, factor in factors.items():
        out[name] = (out[name] * factor).astype(out[name].dtype)
    return out
```

```python
from contextlib import ExitStack

import numpy as np

import concourse.bass as bass
from concourse import mybir

F32 = mybir.dt.float32
F32R = mybir.dt.float32r
BF16 = mybir.dt.bfloat16
ACT = mybir.ActivationFunctionType
ALU = mybir.AluOpType
AX_X = mybir.AxisListType.X

P = 128
T = 512
TB = T // P
D = 1024
DT = D // P
DEPTH = 2
ALPHA = (2 * DEPTH) ** 0.25
ROPE_THETA, ROPE_THETA_2 = 500000.0, 10000.0
MLP_TILES = 4 * D // P
FFN_TILES = 2816 // P
CHUNK = 64
NCHUNK = T // CHUNK
LEVELS = 6
UNIT = DT * P
SLOT = 2 * UNIT
RING = 3
AHEAD = 3
LOW_TILES, MID_TILES, EXT_TILES = 24, 16, 16
NEG = -1.0e30
LAM_INIT = [0.8 - 0.6 * float(np.exp(-0.3 * l)) for l in range(DEPTH)]



def layout(entries):
    at, out = 0, {}
    for name, width in entries:
        out[name] = (at, width)
        at += width
    return out, at


CONSTS, CONST_W = layout([
    ("cos", T), ("sin", T), ("cos2", T), ("sin2", T), ("decay", 4 * T), ("reset", T),
    ("ident", P), ("turn", P), ("turn2", P), ("mean", P), ("mean128", P), ("mean64", P), ("sum64", P),
    ("flip", P), ("pair", P), ("low0", P)] + [(f"up{l}", P) for l in range(LEVELS)] +
    [("up", P), ("upincl", P), ("eps", 4)])
MASKS = ["ident", "causal", "band", "four", "fourcausal", "sixteen", "sixteencausal"]
EPS = [1e-5, 1e-6, 64e-6, 64e-5]


def constants():
    c = np.zeros((P, CONST_W), np.float32)

    def put(name, value):
        at, width = CONSTS[name]
        c[:, at:at + width] = value

    pos = np.arange(T, dtype=np.float32)

    def rope(cos, sin, turn, theta, half, period):
        inv = np.float32(theta) ** (-np.arange(half, dtype=np.float32) / np.float32(half))
        ang = pos[None, :] * inv[:, None].astype(np.float32)
        co, si, tu = np.ones((P, T)), np.zeros((P, T)), np.zeros((P, P))
        for b in range(0, P, period):
            co[b:b + half] = co[b + half:b + 2 * half] = np.cos(ang)
            si[b:b + half] = si[b + half:b + 2 * half] = np.sin(ang)
            for i in range(half):
                tu[b + half + i, b + i] = -1.0
                tu[b + i, b + half + i] = 1.0
        put(cos, co)
        put(sin, si)
        put(turn, tu)

    rope("cos", "sin", "turn", ROPE_THETA, 16, P)
    rope("cos2", "sin2", "turn2", ROPE_THETA_2, 32, 64)
    lg = np.log(1.0 - 2.0 ** (-5.0 - np.arange(4)))
    n = np.arange(T)[None, :] - np.arange(P)[:, None]
    put("decay", np.concatenate([np.where(n >= 0, np.exp(g * np.maximum(n, 0)), 0.0) / 8.0 for g in lg], 1))
    put("reset", np.broadcast_to((np.arange(T) % CHUNK != 0).astype(np.float32), (P, T)))
    a, b = np.arange(P)[:, None], np.arange(P)[None, :]
    block = a // 64 == b // 64
    put("ident", a == b)
    put("mean", 1.0 / D)
    put("mean128", 1.0 / P)
    put("mean64", block / 64.0)
    put("sum64", block)
    put("flip", a + b == P - 1)
    put("pair", block)
    for l in range(LEVELS):
        w = 1 << l
        low = (a // (2 * w) == b // (2 * w)) & (a % (2 * w) >= w) & (b % (2 * w) < w)
        if l == 0:
            put("low0", low)
        put(f"up{l}", low.T)
    put("up", block & (a < b))
    put("upincl", block & (a <= b))
    put("eps", np.broadcast_to(np.array(EPS, np.float32), (P, len(EPS))))
    d = a - b
    masks = {"ident": (d == 0) * 1.0, "causal": np.where(d >= 0, 0, NEG), "band": np.where(d <= 0, 0, NEG),
             "four": np.where(d % 4 == 0, 0, NEG), "fourcausal": np.where((d % 4 == 0) & (d >= 0), 0, NEG),
             "sixteen": np.where(d % 16 == 0, 0, NEG), "sixteencausal": np.where((d % 16 == 0) & (d >= 0), 0, NEG)}
    m = np.concatenate([masks[k] for k in MASKS], 1).astype(np.float32)
    dist = np.maximum(np.arange(T + P) - (P - 1), 0)
    nf = np.maximum(dist, 1).astype(np.float32)
    large = 16 + (np.log(nf / np.float32(16)) / np.float32(np.log(8.0)) * np.float32(16)).astype(np.int32)
    bucket = np.where(dist < 16, dist, np.minimum(large, 31))
    onehot = (bucket[None, :] == np.arange(32)[:, None]).astype(np.float32)
    return c, m, onehot



def vector_entries():
    e = [("w0", 4), ("a0", 4), ("b_gate", 24 * DEPTH)]
    e += [("mix", 15), ("k_k", 4), ("k_a", 4), ("r_k", 4), ("lnx_g", 4), ("lnx_b", 4)]
    e += [(n, DT * DEPTH) for n in ("ln1_g", "ln1_b", "ln2_g", "ln2_b", "norm_mix_g", "norm_ffn_g")]
    e += [(n, DEPTH) for n in ("da_q_g", "da_k_g", "subln_g", "ret_g")]
    e += [("conv_w", 6 * DEPTH), ("conv_b", 2 * DEPTH), ("ffn_w", 3 * FFN_TILES * DEPTH), ("ffn_b", FFN_TILES * DEPTH)]
    return e


VECTORS, VECTOR_W = layout(vector_entries())
HALVED = 8 + 24 * DEPTH

AB_TILES = [c * P for c in range(14)] + [1792] + [1824 + c * P for c in range(12)]
MLP_HALF, FFN_HALF = MLP_TILES // 2, FFN_TILES // 2
FFN_PARTS = [6, 5]


def unit_parts():
    mlp = ([8] * MLP_HALF + [8, 8] * DT) * 2
    u = [8] * (27 + DT) + mlp + [8] * (40 + DT) + mlp
    for _ in range(DEPTH):
        u += [8] * (26 + 4 * DT + DT) + ([8] * FFN_TILES + FFN_PARTS * DT) * 2
    return u


UNITS = unit_parts()


def group_units():
    groups, n = [], 0
    while n < len(UNITS):
        end = n + 1
        while end < len(UNITS) and sum(UNITS[n:end + 1]) * P <= SLOT and end - n < 2:
            end += 1
        groups.append((n, end))
        n = end
    return groups


GROUPS = group_units()
GROUP_OF = [g for g, (a, b) in enumerate(GROUPS) for _ in range(a, b)]
UNIT_AT = [P * sum(UNITS[:n]) for n in range(len(UNITS) + 1)]


class Halves:

    def __init__(self, hi, lo):
        self.hi_t, self.lo_t = hi, lo

    def hi(self, n):
        return self.hi_t[:, n, :]

    def lo(self, n):
        return self.lo_t[:, n, :]


class Core:

    def __init__(self, nc, ctx, wts):
        self.nc = nc
        self.ring = ctx.enter_context(nc.sbuf_tensor("ring", [P, RING, SLOT], F32))
        self.w_hi = ctx.enter_context(nc.sbuf_tensor("w_hi", [P, AHEAD, UNIT], F32R))
        self.w_lo = ctx.enter_context(nc.sbuf_tensor("w_lo", [P, AHEAD, UNIT], F32R))
        self.xT = ctx.enter_context(nc.sbuf_tensor("xT", [P, DT, T], F32))
        self.const = ctx.enter_context(nc.sbuf_tensor("const", [P, CONST_W], F32))
        self.mask = ctx.enter_context(nc.sbuf_tensor("mask", [P, len(MASKS) * P], BF16))
        self.vec = ctx.enter_context(nc.sbuf_tensor("vec", [P, VECTOR_W], F32))
        self.small = ctx.enter_context(nc.sbuf_tensor("small", [P, 64], F32))
        self.psum = ctx.enter_context(nc.psum_tensor("psum", [P, 8, T], F32))
        sem = lambda name: ctx.enter_context(nc.semaphore(name))
        self.slot_filled = [sem(f"slot_filled{i}") for i in range(RING)]
        self.hi_ready, self.lo_ready, self.unit_used = sem("hi_ready"), sem("lo_ready"), sem("unit_used")
        self.out_stored = sem("out_stored")
        self.pools = [[sem(f"stage{p}_{i}") for i in range(14)] for p in range(2)]
        self.parts = {}
        self.names = 0
        self.stage = 0
        self.next_sem = 0
        self.next_group = 0
        self.wts = wts

    def space(self, stack, tiles, dtype=F32):
        self.names += 1
        return stack.enter_context(self.nc.sbuf_tensor(f"space{self.names}", [P, tiles, T], dtype))

    def halves(self, stack, tiles):
        return Halves(self.space(stack, tiles, F32R), self.space(stack, tiles, F32R))

    def open_part(self, stack, first, tiles):
        self.parts[first] = (self.space(stack, tiles), tiles)

    def x(self, d):
        return self.xT[:, d, :]

    def tile(self, n, count=1):
        first = max(f for f in self.parts if f <= n)
        part, tiles = self.parts[first]
        assert n + count <= first + tiles, (n, count)
        return part[:, n - first:n - first + count, :].rearrange("p a t -> p (a t)")

    def bank(self, b):
        return self.psum[:, b, :]

    def c(self, name):
        at, width = CONSTS[name]
        return self.const[:, at:at + width]

    def m(self, name):
        n = MASKS.index(name)
        return self.mask[:, n * P:(n + 1) * P]

    def v(self, name, j):
        at, width = VECTORS[name]
        assert j < width
        return self.vec[:, at + j:at + j + 1]

    def eps(self, value):
        at = CONSTS["eps"][0] + EPS.index(value)
        return self.const[:, at:at + 1]

    def begin(self):
        self.stage += 1
        self.next_sem = 0

    def sem(self):
        self.next_sem += 1
        return self.pools[self.stage % 2][self.next_sem - 1]

    def fill(self, sp, stop):
        while self.next_group < len(GROUPS):
            g = self.next_group
            if g >= RING:
                split = GROUPS[g - RING][1]
                if split > stop:
                    break
                sp.wait_ge(self.lo_ready, split)
            a, b = UNIT_AT[GROUPS[g][0]], UNIT_AT[GROUPS[g][1]]
            sp.dma_start(self.ring[:, g % RING, 0:b - a], self.wts[:, a:b]).then_inc(self.slot_filled[g % RING], 16)
            self.next_group += 1

    def sync_work(self, sp, end=None):
        for s in self.pools[(self.stage + 1) % 2]:
            sp.sem_clear(s)
        if end is not None:
            self.fill(sp, end + AHEAD)

    def raw(self, n):
        g = GROUP_OF[n]
        at = UNIT_AT[n] - UNIT_AT[GROUPS[g][0]]
        return self.ring[:, g % RING, at:at + UNITS[n] * P]

    def split_hi(self, act, n):
        if n >= len(UNITS):
            return
        g = GROUP_OF[n]
        act.wait_ge(self.slot_filled[g % RING], 16 * (g // RING + 1))
        if n >= AHEAD:
            act.wait_ge(self.unit_used, n - AHEAD + 1)
        act.activation(self.w_hi[:, n % AHEAD, 0:UNITS[n] * P], self.raw(n), ACT.Copy).then_inc(self.hi_ready, 1)

    def split_lo(self, dve, n):
        if n >= len(UNITS):
            return
        w = slice(0, UNITS[n] * P)
        dve.wait_ge(self.hi_ready, n + 1)
        dve.tensor_tensor(self.w_lo[:, n % AHEAD, w], self.raw(n), self.w_hi[:, n % AHEAD, w].bitcast(F32),
                          ALU.subtract).then_inc(self.lo_ready, 1)

    def product(self, pe, out, n, rhs, first=0, units=1, rhs_ready=None):
        at, total = 0, sum(UNITS[n:n + units])
        for u in range(n, n + units):
            pe.wait_ge(self.lo_ready, u + 1)
            for i in range(UNITS[u]):
                w = slice(i * P, (i + 1) * P)
                hi, lo = self.w_hi[:, u % AHEAD, w], self.w_lo[:, u % AHEAD, w]
                if rhs_ready is not None:
                    pe.wait_ge(rhs_ready, at + 1)
                pe.matmul(out, hi, rhs.hi(first + at), start=(at == 0), stop=False)
                pe.matmul(out, hi, rhs.lo(first + at), start=False, stop=False)
                last = pe.matmul(out, lo, rhs.hi(first + at), start=False, stop=(at == total - 1))
                at += 1
            last.then_inc(self.unit_used, 1)


class Chain:

    def __init__(self, eng, sem):
        self.eng, self.sem, self.n = eng, sem, 0

    def __call__(self, ins):
        ins.then_inc(self.sem, 1)
        self.n += 1
        return self.n

    def sync(self):
        self.eng.wait_ge(self.sem, self.n)

    def then(self, ins):
        self(ins)
        self.sync()



def prologue(k, stack, x_in, const_in, mask_in, vec_in, onehot_in, relb_in, bias_dram):
    nc = k.nc
    loaded, halved, bias_done, bias_copied, stored, oh_loaded = (k.sem() for _ in range(6))
    k.open_part(stack, 0, 6)
    onehot = k.tile(0, 2)[0:32, 0:T + P]
    relb = k.tile(0, 2)[0:32, T + P:T + P + 4]
    row = k.tile(2, 2)[0:4, 0:T + P]
    masks = k.tile(4, 2)[:, 0:len(MASKS) * P]
    with nc.Block() as block:
        @block.sync
        def _(sp):
            sp.dma_start(k.xT[:, :, :], x_in).then_inc(loaded, 16)
            sp.dma_start(k.vec[:, :], vec_in).then_inc(loaded, 16)
            sp.dma_start(masks, mask_in).then_inc(loaded, 16)
            sp.dma_start(onehot, onehot_in).then_inc(oh_loaded, 16)
            sp.dma_start(relb, relb_in).then_inc(oh_loaded, 16)
            k.fill(sp, 0)
            sp.dma_start(k.const[:, :], const_in).then_inc(loaded, 16)
            sp.wait_ge(bias_copied, 2)
            sp.dma_start(bias_dram, row).then_inc(stored, 16)
            sp.wait_ge(stored, 16)
            sp.wait_ge(loaded, 64)

        @block.vector
        def _(dve):
            dve.wait_ge(loaded, 64)
            dve.tensor_scalar(k.vec[:, 0:HALVED], k.vec[:, 0:HALVED], 0.5, None, ALU.mult).then_inc(halved, 1)
            dve.tensor_copy(k.mask[:, :], masks).then_inc(halved, 1)
            for n in range(AHEAD):
                k.split_lo(dve, n)

        @block.tensor
        def _(pe):
            pe.wait_ge(oh_loaded, 32)
            for b, (lo, hi) in enumerate(((0, T), (T, T + P))):
                pe.matmul(k.psum[0:4, b, 0:hi - lo], relb, onehot[:, lo:hi], start=True, stop=True).then_inc(bias_done, 1)

        @block.scalar
        def _(act):
            for b, (lo, hi) in enumerate(((0, T), (T, T + P))):
                act.wait_ge(bias_done, b + 1)
                act.activation(row[:, lo:hi], k.psum[0:4, b, 0:hi - lo], ACT.Copy).then_inc(bias_copied, 1)
            for n in range(AHEAD):
                k.split_hi(act, n)


def split_tiles_hi(act, tiles, halves, ready):
    for n, v in enumerate(tiles):
        act.activation(halves.hi(n), v, ACT.Copy).then_inc(ready, 1)


def split_tiles_lo(dve, tiles, halves, hi_ready, ready):
    for n, v in enumerate(tiles):
        dve.wait_ge(hi_ready, n + 1)
        dve.tensor_tensor(halves.lo(n), v, halves.hi(n).bitcast(F32), ALU.subtract).then_inc(ready, 1)


def project(k, first, src, rhs, out, turned=(), cos="cos", sin="sin", turn="turn"):
    nc = k.nc
    k.begin()
    src_hi, src_lo, copied, turned_done, chain, roped = (k.sem() for _ in range(6))
    order = [t for t in range(len(out)) if t in turned]
    end = first + len(out)
    with nc.Block() as block:
        @block.sync
        def _(sp):
            k.sync_work(sp, end)

        @block.tensor
        def _(pe):
            def rotate(r):
                pe.wait_ge(copied, order[r] + 1)
                if r >= 2:
                    pe.wait_ge(roped, r - 1)
                pe.matmul(k.bank(6 + r % 2), k.c(turn), out[order[r]], start=True, stop=True).then_inc(turned_done, 1)

            r = 0
            for t in range(len(out)):
                if t >= 6:
                    pe.wait_ge(copied, t - 5)
                k.product(pe, k.bank(t % 6), first + t, rhs, rhs_ready=src_lo if src and t == 0 else None)
                if r < len(order) and order[r] < t:
                    rotate(r)
                    r += 1
            while r < len(order):
                rotate(r)
                r += 1

        @block.scalar
        def _(act):
            if src:
                split_tiles_hi(act, src, rhs, src_hi)
            for t in range(len(out)):
                act.wait_ge(k.unit_used, first + t + 1)
                act.activation(out[t], k.bank(t % 6), ACT.Copy).then_inc(copied, 1)
                k.split_hi(act, first + t + AHEAD)

        @block.vector
        def _(dve):
            ch = Chain(dve, chain)
            if src:
                split_tiles_lo(dve, src, rhs, src_hi, src_lo)

            def finish(r):
                bank, o = k.bank(6 + r % 2), out[order[r]]
                dve.wait_ge(turned_done, r + 1)
                ch(dve.tensor_tensor(bank, bank, k.c(sin), ALU.mult))
                ch.then(dve.tensor_tensor(o, o, k.c(cos), ALU.mult))
                dve.tensor_tensor(o, o, bank, ALU.add).then_inc(roped, 1)

            r = 0
            for t in range(len(out)):
                k.split_lo(dve, first + t + AHEAD)
                if r < len(order) and order[r] < t:
                    finish(r)
                    r += 1
            while r < len(order):
                finish(r)
                r += 1


def project_residual(k, first, src, rhs, scale, units=1):
    nc = k.nc
    k.begin()
    src_hi, src_lo, added = (k.sem() for _ in range(3))
    end = first + DT * units
    with nc.Block() as block:
        @block.sync
        def _(sp):
            k.sync_work(sp, end)

        @block.scalar
        def _(act):
            if src:
                split_tiles_hi(act, src, rhs, src_hi)
            for n in range(first, end):
                k.split_hi(act, n + AHEAD)

        @block.tensor
        def _(pe):
            for t in range(DT):
                k.product(pe, k.bank(t), first + t * units, rhs, units=units, rhs_ready=src_lo if src and t == 0 else None)

        @block.vector
        def _(dve):
            if src:
                split_tiles_lo(dve, src, rhs, src_hi, src_lo)
            for t in range(DT):
                for n in range(first + t * units, first + (t + 1) * units):
                    k.split_lo(dve, n + AHEAD)
                dve.wait_ge(k.unit_used, first + (t + 1) * units)
                dve.scalar_tensor_tensor(out=k.x(t), in0=k.x(t), scalar=scale, in1=k.bank(t),
                                         op0=ALU.mult, op1=ALU.add).then_inc(added, 1)


def layer_norm(k, g, b, j, scratch):
    nc = k.nc
    k.begin()
    mean_done, centred, squared, var_done, root, inverse, scaled, shifted = (k.sem() for _ in range(8))
    sq = [k.tile(scratch), k.tile(scratch + 1)]
    rstd = k.tile(scratch + 2)
    with nc.Block() as block:
        @block.sync
        def _(sp):
            k.sync_work(sp)

        @block.tensor
        def _(pe):
            for d in range(DT):
                last = pe.matmul(k.bank(0), k.c("mean"), k.x(d), start=(d == 0), stop=(d == DT - 1))
            last.then_inc(mean_done, 1)
            for d in range(DT):
                pe.wait_ge(squared, d + 1)
                pe.matmul(k.bank(1), k.c("mean"), sq[d % 2], start=(d == 0), stop=(d == DT - 1)).then_inc(var_done, 1)

        @block.vector
        def _(dve):
            dve.wait_ge(mean_done, 1)
            for d in range(DT):
                dve.tensor_tensor(k.x(d), k.x(d), k.bank(0), ALU.subtract).then_inc(centred, 1)
            dve.wait_ge(root, 1)
            dve.reciprocal(rstd, rstd).then_inc(inverse, 1)
            dve.wait_ge(inverse, 1)
            for d in range(DT):
                dve.tensor_tensor(k.x(d), k.x(d), rstd, ALU.mult).then_inc(scaled, 1)

        @block.scalar
        def _(act):
            for d in range(DT):
                act.wait_ge(centred, d + 1)
                if d >= 2:
                    act.wait_ge(var_done, d - 1)
                act.activation(sq[d % 2], k.x(d), ACT.Square).then_inc(squared, 1)
            act.wait_ge(var_done, DT)
            act.activation(rstd, k.bank(1), ACT.Sqrt, bias=k.eps(1e-5)).then_inc(root, 1)
            for d in range(DT):
                act.wait_ge(scaled, d + 1)
                act.activation(k.x(d), k.x(d), ACT.Identity, scale=k.v(g, j * DT + d),
                               bias=k.v(b, j * DT + d)).then_inc(shifted, 1)


def rms_norm(k, g, j, out, work):
    nc = k.nc
    k.begin()
    squared, mean_done, root, inverse, scaled, out_hi, out_lo = (k.sem() for _ in range(7))
    sq = [k.tile(work), k.tile(work + 1)]
    rstd = k.tile(work + 2)
    with nc.Block() as block:
        @block.sync
        def _(sp):
            k.sync_work(sp)

        @block.tensor
        def _(pe):
            for d in range(DT):
                pe.wait_ge(squared, d + 1)
                pe.matmul(k.bank(0), k.c("mean"), sq[d % 2], start=(d == 0), stop=(d == DT - 1)).then_inc(mean_done, 1)

        @block.scalar
        def _(act):
            for d in range(DT):
                if d >= 2:
                    act.wait_ge(mean_done, d - 1)
                act.activation(sq[d % 2], k.x(d), ACT.Square).then_inc(squared, 1)
            act.wait_ge(mean_done, DT)
            act.activation(rstd, k.bank(0), ACT.Sqrt, bias=k.eps(1e-6)).then_inc(root, 1)
            for d in range(DT):
                act.wait_ge(scaled, d + 1)
                act.activation(out.hi(d), sq[d % 2], ACT.Copy).then_inc(out_hi, 1)

        @block.vector
        def _(dve):
            dve.wait_ge(root, 1)
            dve.reciprocal(rstd, rstd).then_inc(inverse, 1)
            dve.wait_ge(inverse, 1)
            def lo(d):
                dve.wait_ge(out_hi, d + 1)
                dve.tensor_tensor(out.lo(d), sq[d % 2], out.hi(d).bitcast(F32), ALU.subtract).then_inc(out_lo, 1)

            for d in range(DT):
                if d >= 2:
                    dve.wait_ge(out_lo, d - 1)
                dve.scalar_tensor_tensor(out=sq[d % 2], in0=k.x(d), scalar=k.v(g, j * DT + d), in1=rstd,
                                         op0=ALU.mult, op1=ALU.mult).then_inc(scaled, 1)
                if d >= 1:
                    lo(d - 1)
            lo(DT - 1)


def turn_values(k, tiles):
    nc = k.nc
    k.begin()
    turned, copied = k.sem(), k.sem()
    with nc.Block() as block:
        @block.sync
        def _(sp):
            k.sync_work(sp)

        @block.tensor
        def _(pe):
            for t, v in enumerate(tiles):
                if t >= 8:
                    pe.wait_ge(copied, t - 7)
                for i in range(TB):
                    last = pe.transpose(k.bank(t % 8)[:, i * P:(i + 1) * P], v[:, i * P:(i + 1) * P], k.c("ident"))
                last.then_inc(turned, 1)

        @block.scalar
        def _(act):
            for t, v in enumerate(tiles):
                act.wait_ge(turned, t + 1)
                act.activation(v, k.bank(t % 8), ACT.Copy).then_inc(copied, 1)


def attention(k, heads, scale, work, difference=None):
    nc = k.nc
    k.begin()
    scores_done, maxima, exps_done, probs_ready, turned, turned_copied, out_done, out_copied, chain = \
        (k.sem() for _ in range(9))
    units = [(h, i) for h in range(len(heads)) for i in range(TB)]
    G = len(heads[0][0])
    prob = [[k.tile(work + G * b + g) for g in range(G)] for b in range(2)]
    probT = [k.tile(work + 2 * G + b) for b in range(2)]
    stat = [k.small[:, 16 * b:16 * b + 16] for b in range(2)]

    with nc.Block() as block:
        @block.sync
        def _(sp):
            k.sync_work(sp)

        @block.tensor
        def _(pe):
            def scores(u):
                h, i = units[u]
                if u >= 2:
                    pe.wait_ge(exps_done, G * (u - 1))
                for g, (q, key, first, terms) in enumerate(heads[h][0]):
                    lo, hi = first(i), (i + 1) * P
                    out = k.bank(3 * (u % 2) + g)
                    adds = [(j, a) for j in range(lo // P, i + 1) for a in terms(i, j)]
                    last = pe.matmul(out[:, lo:hi], q[:, i * P:(i + 1) * P], key[:, lo:hi], start=True, stop=not adds)
                    for n, (j, (lhsT, rhs)) in enumerate(adds):
                        last = pe.matmul(out[:, j * P:(j + 1) * P], lhsT, rhs, start=False, stop=(n == len(adds) - 1))
                last.then_inc(scores_done, 1)

            def apply(u):
                h, i = units[u]
                values = heads[h][1]
                pe.wait_ge(probs_ready, u + 1)
                if u >= 1:
                    pe.wait_ge(turned_copied, u)
                for j in range(i + 1):
                    last = pe.transpose(k.bank(6)[:, j * P:(j + 1) * P], prob[u % 2][0][:, j * P:(j + 1) * P], k.c("ident"))
                last.then_inc(turned, 1)
                pe.wait_ge(turned_copied, u + 1)
                if u >= 1:
                    pe.wait_ge(out_copied, u)
                for j in range(i + 1):
                    last = pe.matmul(k.bank(7)[:, 0:P], values[:, j * P:(j + 1) * P], probT[u % 2][:, j * P:(j + 1) * P],
                                     start=(j == 0), stop=(j == i))
                last.then_inc(out_done, 1)

            for u in range(len(units)):
                scores(u)
                if u >= 1:
                    apply(u - 1)
            apply(len(units) - 1)

        @block.vector
        def _(dve):
            ch = Chain(dve, chain)

            def shift(u):
                h, i = units[u]
                s = stat[u % 2]
                dve.wait_ge(scores_done, u + 1)
                for g, (q, key, first, terms) in enumerate(heads[h][0]):
                    ch(dve.reduce_max(s[:, g:g + 1], k.bank(3 * (u % 2) + g)[:, first(i):(i + 1) * P], AX_X))
                ch.sync()
                if difference is not None:
                    dve.tensor_scalar(s[:, 6:8], s[:, 0:2], -scale, None, ALU.mult).then_inc(maxima, 1)
                    return
                for g in range(1, G):
                    ch.then(dve.tensor_tensor(s[:, 0:1], s[:, 0:1], s[:, g:g + 1], ALU.max))
                dve.tensor_scalar(s[:, 6:7], s[:, 0:1], -scale, None, ALU.mult).then_inc(maxima, 1)

            def combine(u):
                h, i = units[u]
                s, p = stat[u % 2], prob[u % 2]
                hi = (i + 1) * P
                dve.wait_ge(exps_done, G * (u + 1))
                if difference is not None:
                    ch.then(dve.reciprocal(s[:, 8:10], s[:, 3:5]))
                    ch(dve.tensor_scalar(s[:, 9:10], s[:, 9:10], difference, None, ALU.mult))
                    ch(dve.tensor_scalar(p[0][:, 0:hi], p[0][:, 0:hi], s[:, 8:9], None, ALU.mult))
                    ch.sync()
                    dve.scalar_tensor_tensor(out=p[0][:, 0:hi], in0=p[1][:, 0:hi], scalar=s[:, 9:10], in1=p[0][:, 0:hi],
                                             op0=ALU.mult, op1=ALU.add).then_inc(probs_ready, 1)
                    return
                for g in range(1, G):
                    lo = heads[h][0][g][2](i)
                    ch(dve.tensor_tensor(s[:, 3:4], s[:, 3:4], s[:, 3 + g:4 + g], ALU.add))
                    ch.then(dve.tensor_tensor(p[0][:, lo:hi], p[0][:, lo:hi], p[g][:, lo:hi], ALU.add))
                ch.then(dve.reciprocal(s[:, 8:9], s[:, 3:4]))
                dve.tensor_scalar(p[0][:, 0:hi], p[0][:, 0:hi], s[:, 8:9], None, ALU.mult).then_inc(probs_ready, 1)

            def store(u):
                h, i = units[u]
                dve.wait_ge(out_done, u + 1)
                dve.tensor_copy(heads[h][2][:, i * P:(i + 1) * P], k.bank(7)[:, 0:P]).then_inc(out_copied, 1)

            for u in range(len(units) + 2):
                if u < len(units):
                    shift(u)
                if 1 <= u <= len(units):
                    combine(u - 1)
                if u >= 2:
                    store(u - 2)

        @block.scalar
        def _(act):
            def exps(u):
                h, i = units[u]
                s = stat[u % 2]
                act.wait_ge(maxima, u + 1)
                if u >= 2:
                    act.wait_ge(turned, u - 1)
                for g, (q, key, first, terms) in enumerate(heads[h][0]):
                    lo, hi = first(i), (i + 1) * P
                    nm = s[:, 6 + g:7 + g] if difference is not None else s[:, 6:7]
                    act.activation(prob[u % 2][g][:, lo:hi], k.bank(3 * (u % 2) + g)[:, lo:hi], ACT.Exp, bias=nm,
                                   scale=scale, accum_out=s[:, 3 + g:4 + g]).then_inc(exps_done, 1)

            def copy_turned(u):
                h, i = units[u]
                act.wait_ge(turned, u + 1)
                if u >= 2:
                    act.wait_ge(out_done, u - 1)
                act.activation(probT[u % 2][:, 0:(i + 1) * P], k.bank(6)[:, 0:(i + 1) * P], ACT.Copy).then_inc(turned_copied, 1)

            for u in range(len(units) + 1):
                if u < len(units):
                    exps(u)
                if u >= 1:
                    copy_turned(u - 1)



def rwkv_shift(k):
    nc = k.nc
    k.begin()
    stepped, edge, mixed = (k.sem() for _ in range(3))
    n = 15
    delta = [k.tile(31), k.tile(32)]
    with nc.Block() as block:
        @block.sync
        def _(sp):
            k.sync_work(sp)

        @block.gpsimd
        def _(pool):
            for t in range(n):
                z, d = k.tile(t), delta[t % 2]
                if t >= 2:
                    pool.wait_ge(mixed, t - 1)
                pool.tensor_tensor(d[:, 1:T], z[:, 0:T - 1], z[:, 1:T], ALU.subtract).then_inc(stepped, 1)
                pool.tensor_scalar(d[:, 0:1], z[:, 0:1], -1.0, None, ALU.mult).then_inc(edge, 1)

        @block.vector
        def _(dve):
            for t in range(n):
                z, d = k.tile(t), delta[t % 2]
                dve.wait_ge(stepped, t + 1)
                dve.wait_ge(edge, t + 1)
                dve.scalar_tensor_tensor(out=z, in0=d, scalar=k.v("mix", t), in1=z, op0=ALU.mult,
                                         op1=ALU.add).then_inc(mixed, 1)


def rwkv_loras(k, lora_in):
    nc = k.nc
    k.begin()
    loaded, tanh_done, gates_ready, s_done, a_done, g_done, s_tanh, a_tanh, g_copied, gate_tanh, finished = \
        (k.sem() for _ in range(11))
    wup, aup, gup1, gup2 = (k.tile(31 + n) for n in range(4))
    tw = k.tile(35)
    z_wa, z_g = k.tile(12), k.tile(13, 2)
    with nc.Block() as block:
        @block.sync
        def _(sp):
            sp.dma_start(k.tile(31, 4), lora_in).then_inc(loaded, 16)
            sp.wait_ge(loaded, 16)
            k.sync_work(sp)

        @block.scalar
        def _(act):
            act.activation(tw, z_wa, ACT.Tanh).then_inc(tanh_done, 1)
            act.activation(z_g, z_g, ACT.Tanh, scale=0.5).then_inc(gate_tanh, 1)
            for j in range(4):
                act.wait_ge(s_done, j + 1)
                act.activation(k.tile(19 + j), k.bank(j % 2), ACT.Tanh, scale=0.5, bias=k.v("w0", j)).then_inc(s_tanh, 1)
                act.wait_ge(a_done, j + 1)
                act.activation(k.tile(23 + j), k.bank(2 + j % 2), ACT.Tanh, scale=0.5, bias=k.v("a0", j)).then_inc(a_tanh, 1)
                act.wait_ge(g_done, j + 1)
                act.activation(k.tile(27 + j), k.bank(4 + j % 2), ACT.Copy).then_inc(g_copied, 1)

        @block.vector
        def _(dve):
            dve.wait_ge(gate_tanh, 1)
            dve.tensor_scalar(z_g, z_g, 0.5, 0.5, ALU.mult, ALU.add).then_inc(gates_ready, 1)
            half = 0.5 * float(np.exp(-0.5))
            for j in range(4):
                dve.wait_ge(s_tanh, j + 1)
                dve.tensor_scalar(k.tile(19 + j), k.tile(19 + j), -half, -half, ALU.mult, ALU.add).then_inc(finished, 1)
                dve.wait_ge(a_tanh, j + 1)
                dve.tensor_scalar(k.tile(23 + j), k.tile(23 + j), 0.5, 0.5, ALU.mult, ALU.add).then_inc(finished, 1)

        @block.tensor
        def _(pe):
            pe.wait_ge(loaded, 16)
            pe.wait_ge(tanh_done, 1)
            for j in range(4):
                cols = slice(j * P, (j + 1) * P)
                if j >= 2:
                    pe.wait_ge(s_tanh, j - 1)
                    pe.wait_ge(a_tanh, j - 1)
                    pe.wait_ge(g_copied, j - 1)
                pe.matmul(k.bank(j % 2), wup[:, cols], tw, start=True, stop=True).then_inc(s_done, 1)
                pe.matmul(k.bank(2 + j % 2), aup[:, cols], z_wa, start=True, stop=True).then_inc(a_done, 1)
                if j == 0:
                    pe.wait_ge(gates_ready, 1)
                pe.matmul(k.bank(4 + j % 2), gup1[:, cols], z_g[:, 0:T], start=True, stop=False)
                pe.matmul(k.bank(4 + j % 2), gup2[:, cols], z_g[:, T:2 * T], start=False, stop=True).then_inc(g_done, 1)


def blocks(tile):
    return tile.rearrange("p (i t) -> p i t", i=TB)


def spread(mask):
    return mask.unsqueeze(1).to_broadcast([P, TB, P])


def rwkv_pair(k, j):
    nc = k.nc
    W = [k.tile(31 + n) for n in range(17)] + [k.tile(12 + n) for n in range(3)]
    r, key, val, lw, rate, gate = k.tile(j), k.tile(4 + j), k.tile(8 + j), k.tile(19 + j), k.tile(23 + j), k.tile(27 + j)
    bonus = W[3]
    tokA, tokB, tokK, tokV = W[10:14]
    fsum, fexp, om = k.small[:, 0:7], k.small[:, 8:15], k.small[:, 16:17]

    k.begin()
    square_ready, square_sum, root, rk_ready, bonus_sum, sums_ready, exps_done, chain, read = (k.sem() for _ in range(9))
    kk, sq, t2, rk, cum, cen, prv, nrm, e_in, e_out = W[0], W[1], W[2], W[14], W[4], W[5], W[6], W[7], W[8], W[9]
    with nc.Block() as block:
        @block.sync
        def _(sp):
            k.sync_work(sp)

        @block.tensor
        def _(pe):
            pe.wait_ge(square_ready, 1)
            pe.matmul(k.bank(0), k.c("sum64"), sq, start=True, stop=True).then_inc(square_sum, 1)
            pe.wait_ge(rk_ready, 1)
            pe.matmul(k.bank(1), k.c("sum64"), rk, start=True, stop=True).then_inc(bonus_sum, 1)

        @block.scalar
        def _(act):
            act.wait_ge(square_sum, 1)
            act.activation(nrm, k.bank(0), ACT.Sqrt).then_inc(root, 1)
            act.wait_ge(sums_ready, 1)
            act.activation(e_in, cen, ACT.Exp).then_inc(exps_done, 1)
            act.activation(e_out, cen, ACT.Exp, scale=-1.0).then_inc(exps_done, 1)
            act.activation(prv, prv, ACT.Exp).then_inc(exps_done, 1)
            act.activation(fexp, fsum, ACT.Exp, scale=0.5).then_inc(exps_done, 1)

        @block.vector
        def _(dve):
            ch = Chain(dve, chain)
            ch(dve.tensor_scalar(om, k.v("k_a", j), -1.0, 1.0, ALU.mult, ALU.add))
            ch.then(dve.tensor_scalar(kk, key, k.v("k_k", j), None, ALU.mult))
            dve.tensor_tensor(sq, kk, kk, ALU.mult).then_inc(square_ready, 1)
            ch.then(dve.tensor_scalar(t2, rate, k.v("k_a", j), om, ALU.mult, ALU.add))
            ch.then(dve.tensor_tensor(key, key, t2, ALU.mult))
            dve.scalar_tensor_tensor(out=rk, in0=r, scalar=k.v("r_k", j), in1=key, op0=ALU.mult,
                                     op1=ALU.mult).then_inc(rk_ready, 1)
            ch.then(dve.tensor_tensor_scan(cum, k.c("reset"), lw, 0.0, ALU.mult, ALU.add))
            cum3 = cum.rearrange("p (n c) -> p n c", n=NCHUNK)
            total = cum3[:, :, CHUNK - 1:CHUNK]
            ch(dve.tensor_tensor(fsum.unsqueeze(2), total[:, 0:NCHUNK - 1, :], total[:, 1:NCHUNK, :], ALU.add))
            ch.then(dve.scalar_tensor_tensor(out=cen.rearrange("p (n c) -> p n c", n=NCHUNK),
                                             in0=total.to_broadcast([P, NCHUNK, CHUNK]), scalar=-0.5, in1=cum3,
                                             op0=ALU.mult, op1=ALU.add))
            dve.tensor_tensor(prv, cen, lw, ALU.subtract).then_inc(sums_ready, 1)
            dve.wait_ge(root, 1)
            ch.then(dve.tensor_scalar(nrm, nrm, 1e-12, None, ALU.max))
            ch.then(dve.reciprocal(nrm, nrm))
            ch.then(dve.tensor_tensor(kk, kk, nrm, ALU.mult))
            ch(dve.tensor_tensor(rate, rate, kk, ALU.mult))
            dve.wait_ge(bonus_sum, 1)
            ch(dve.tensor_tensor(bonus, val, k.bank(1), ALU.mult))
            dve.wait_ge(exps_done, 4)
            ch(dve.scalar_tensor_tensor(out=lw, in0=kk, scalar=-1.0, in1=prv, op0=ALU.mult, op1=ALU.mult))
            ch.sync()
            ch(dve.tensor_tensor(rate, rate, e_out, ALU.mult))
            ch(dve.tensor_tensor(key, key, e_out, ALU.mult))
            ch(dve.tensor_tensor(r, r, e_in, ALU.mult))
    at, bt, kt, rt = lw, rate, key, r

    X, XT, NT, AK = [W[0], W[1]], [W[2], W[4]], [W[5], W[6]], [W[7], W[8]]
    av = W[16]
    k.begin()
    made, act_done, x_half, x_ready, ak_ready, xt_half, xt_ready, av_done, av_copied = (k.sem() for _ in range(9))
    half = [slice(0, 64), slice(64, 128)]
    with nc.Block() as block:
        @block.sync
        def _(sp):
            k.sync_work(sp)

        @block.tensor
        def _(pe):
            for b, src in enumerate((at, bt, kt, val)):
                for i in range(TB):
                    last = pe.transpose(k.bank(b)[:, i * P:(i + 1) * P], src[:, i * P:(i + 1) * P], k.c("ident"))
                last.then_inc(made, 1)

            def outer(bank, left, right, h):
                for i in range(TB):
                    last = pe.matmul(k.bank(bank)[:, i * P:(i + 1) * P], left[half[h], i * P:(i + 1) * P],
                                     right[half[h], i * P:(i + 1) * P], start=True, stop=True)
                last.then_inc(made, 1)

            outer(4, at, bt, 0)
            outer(5, bt, at, 0)
            outer(6, kt, at, 0)
            outer(7, at, bt, 1)
            pe.wait_ge(act_done, 1)
            outer(0, bt, at, 1)
            pe.wait_ge(act_done, 2)
            outer(1, kt, at, 1)
            pe.wait_ge(act_done, 4)
            for h in range(2):
                pe.wait_ge(ak_ready, h + 1)
                for i in range(TB):
                    cols = slice(i * P + 64 * h, i * P + 64 * h + 64)
                    last = pe.matmul(k.bank(2)[:, cols], AK[h][:, i * P:(i + 1) * P], tokV[:, cols], start=True, stop=True)
            last.then_inc(av_done, 1)

        @block.scalar
        def _(act):
            for b, dst in enumerate((tokA, tokB, tokK, tokV)):
                act.wait_ge(made, b + 1)
                act.activation(dst, k.bank(b), ACT.Copy).then_inc(act_done, 1)
            act.wait_ge(made, 6)
            act.activation(NT[0], k.bank(5), ACT.Copy).then_inc(act_done, 1)
            act.wait_ge(made, 9)
            act.activation(NT[1], k.bank(0), ACT.Copy).then_inc(act_done, 1)
            act.wait_ge(av_done, 1)
            act.activation(av, k.bank(2), ACT.Copy).then_inc(av_copied, 1)

        @block.vector
        def _(dve):
            for h, (m, ak, bank_m, bank_ak) in enumerate(((5, 7, 4, 6), (8, 10, 7, 1))):
                dve.wait_ge(made, m)
                dve.tensor_tensor(blocks(X[h]), blocks(k.bank(bank_m)), spread(k.c("low0")), ALU.mult).then_inc(x_half, 1)
                dve.wait_ge(made, ak)
                dve.tensor_tensor(blocks(AK[h]), blocks(k.bank(bank_ak)), spread(k.c("up")), ALU.mult).then_inc(ak_ready, 1)
                dve.wait_ge(x_half, h + 1)
                dve.tensor_tensor(blocks(X[h]), blocks(X[h]), spread(k.c("ident")), ALU.add).then_inc(x_ready, 1)

        @block.gpsimd
        def _(pool):
            for h in range(2):
                pool.wait_ge(act_done, 5 + h)
                pool.tensor_tensor(blocks(XT[h]), blocks(NT[h]), spread(k.c("up0")), ALU.mult).then_inc(xt_half, 1)
                pool.wait_ge(xt_half, h + 1)
                pool.tensor_tensor(blocks(XT[h]), blocks(XT[h]), spread(k.c("ident")), ALU.add).then_inc(xt_ready, 1)

    level, PR = [W[9], W[14]], AK
    k.begin()
    level_ready, p_done, p_copied, xp_done, x_ready = (k.sem() for _ in range(5))
    with nc.Block() as block:
        @block.sync
        def _(sp):
            k.sync_work(sp)

        @block.gpsimd
        def _(pool):
            for l in range(1, LEVELS):
                for h in range(2):
                    if l >= 2:
                        pool.wait_ge(p_done, 2 * (l - 2) + h + 1)
                    pool.tensor_tensor(blocks(level[h]), blocks(NT[h]), spread(k.c(f"up{l}")), ALU.mult).then_inc(level_ready, 1)

        @block.tensor
        def _(pe):
            for l in range(1, LEVELS):
                n = 2 * (l - 1)
                for h in range(2):
                    pe.wait_ge(level_ready, n + h + 1)
                    if l >= 2:
                        pe.wait_ge(x_ready, n - 2 + h + 1)
                    for i in range(TB):
                        b = slice(i * P, (i + 1) * P)
                        last = pe.matmul(k.bank(h)[:, b], level[h][:, b], X[h][:, b], start=True, stop=True)
                    last.then_inc(p_done, 1)
                for h in range(2):
                    pe.wait_ge(p_copied, n + h + 1)
                    if l < LEVELS - 1:
                        for i in range(TB):
                            b = slice(i * P, (i + 1) * P)
                            pe.matmul(k.bank(2 + h)[:, b], XT[h][:, b], PR[h][:, b], start=True, stop=True)
                    for i in range(TB):
                        b = slice(i * P, (i + 1) * P)
                        last = pe.matmul(k.bank(4 + h)[:, b], PR[h][:, b], XT[h][:, b], start=True, stop=True)
                    last.then_inc(xp_done, 1)

        @block.scalar
        def _(act):
            for l in range(1, LEVELS):
                for h in range(2):
                    act.wait_ge(p_done, 2 * (l - 1) + h + 1)
                    if l >= 2:
                        act.wait_ge(xp_done, 2 * (l - 2) + h + 1)
                    act.activation(PR[h], k.bank(h), ACT.Copy).then_inc(p_copied, 1)

        @block.vector
        def _(dve):
            for l in range(1, LEVELS):
                for h in range(2):
                    dve.wait_ge(xp_done, 2 * (l - 1) + h + 1)
                    if l < LEVELS - 1:
                        dve.tensor_tensor(X[h], X[h], k.bank(2 + h), ALU.add)
                    dve.tensor_tensor(XT[h], XT[h], k.bank(4 + h), ALU.add).then_inc(x_ready, 1)

    RB, RK, TA = [W[0], W[1]], [W[5], W[6]], W[15]
    k.begin()
    made, masked, ta_done, tv_done, copied = (k.sem() for _ in range(5))
    with nc.Block() as block:
        @block.sync
        def _(sp):
            k.sync_work(sp)

        @block.tensor
        def _(pe):
            for h in range(2):
                for i in range(TB):
                    b, cols = slice(i * P, (i + 1) * P), slice(i * P + 64 * h, i * P + 64 * h + 64)
                    last = pe.matmul(k.psum[half[h], 4, b], tokA[:, cols], XT[h][:, b], start=True, stop=True)
            last.then_inc(ta_done, 1)
            for h in range(2):
                for i in range(TB):
                    b, cols = slice(i * P, (i + 1) * P), slice(i * P + 64 * h, i * P + 64 * h + 64)
                    last = pe.matmul(k.bank(5)[:, cols], XT[h][:, b], av[:, cols], start=True, stop=True)
            last.then_inc(tv_done, 1)
            for h in range(2):
                for n, left in enumerate((bt, kt)):
                    for i in range(TB):
                        b = slice(i * P, (i + 1) * P)
                        last = pe.matmul(k.bank(2 * h + n)[:, b], left[half[h], b], rt[half[h], b], start=True, stop=True)
                    last.then_inc(made, 1)

        @block.scalar
        def _(act):
            act.wait_ge(ta_done, 1)
            act.activation(TA, k.bank(4), ACT.Copy).then_inc(copied, 1)
            act.wait_ge(tv_done, 1)
            act.activation(av, k.bank(5), ACT.Copy).then_inc(copied, 1)

        @block.vector
        def _(dve):
            for n, dst in enumerate((RB[0], RK[0], RB[1], RK[1])):
                dve.wait_ge(made, n + 1)
                dve.tensor_tensor(blocks(dst), blocks(k.bank(n)), spread(k.c("upincl")), ALU.mult).then_inc(masked, 1)

    SA, SAz, Vz = W[17], [W[7], W[8]], [W[2], W[4]]
    S = k.tile(13, 2).rearrange("p (n c) -> p n c", n=NCHUNK)
    tv = av
    k.begin()
    cleared, v_copied, sa_done, sa_ready, state_done, state_ready, sa_copied = (k.sem() for _ in range(7))
    with nc.Block() as block:
        @block.sync
        def _(sp):
            k.sync_work(sp)

        @block.gpsimd
        def _(pool):
            pool.memset(S[:, 0, :], 0.0).then_inc(cleared, 1)
            for p in range(2):
                pool.wait_ge(cleared, 2 * p + 1)
                pool.memset(SAz[p][half[1 - p]], 0.0).then_inc(cleared, 1)
                pool.memset(Vz[p][half[1 - p]], 0.0).then_inc(cleared, 1)

        @block.scalar
        def _(act):
            for p in range(2):
                act.activation(Vz[p][half[p]], tokV[half[p]], ACT.Copy).then_inc(v_copied, 1)
            for n in range(NCHUNK):
                i, p = n // 2, n % 2
                act.wait_ge(sa_ready, n + 1)
                act.activation(SA[half[p], i * P:(i + 1) * P], SAz[p][half[p], i * P:(i + 1) * P], ACT.Copy).then_inc(sa_copied, 1)

        @block.tensor
        def _(pe):
            pe.wait_ge(cleared, 5)
            pe.wait_ge(v_copied, 2)
            for n in range(NCHUNK):
                i, p = n // 2, n % 2
                b = slice(i * P, (i + 1) * P)
                if n >= 1:
                    pe.wait_ge(state_ready, n)
                if n >= 2:
                    pe.wait_ge(sa_ready, n - 1)
                pe.matmul(k.bank(n % 2)[:, 0:P], TA[:, b], S[:, n, :], start=True, stop=True).then_inc(sa_done, 1)
                if n == NCHUNK - 1:
                    break
                out = k.bank(2 + n % 2)[:, 0:P]
                pe.matmul(out, k.c("ident"), S[:, n, :], start=True, stop=False)
                pe.matmul(out, tokK[:, b], Vz[p][:, b], start=False, stop=False)
                pe.wait_ge(sa_ready, n + 1)
                pe.matmul(out, tokB[:, b], SAz[p][:, b], start=False, stop=True).then_inc(state_done, 1)

        @block.vector
        def _(dve):
            dve.wait_ge(cleared, 5)
            for n in range(NCHUNK):
                i, p = n // 2, n % 2
                b = slice(i * P, (i + 1) * P)
                dve.wait_ge(sa_done, n + 1)
                dve.tensor_tensor(SAz[p][half[p], b], tv[half[p], b], k.bank(n % 2)[half[p], 0:P], ALU.add).then_inc(sa_ready, 1)
                if n == NCHUNK - 1:
                    break
                dve.wait_ge(state_done, n + 1)
                dve.scalar_tensor_tensor(out=S[:, n + 1, :], in0=k.bank(2 + n % 2)[:, 0:P], scalar=fexp[:, n:n + 1],
                                         in1=k.c("pair"), op0=ALU.mult, op1=ALU.mult).then_inc(state_ready, 1)

    y, sq, rstd = key, W[7], W[8]
    k.begin()
    y_done, y_copied, mean_done, centred, squared, var_done, root, chain, scaled, affine = (k.sem() for _ in range(10))
    with nc.Block() as block:
        @block.sync
        def _(sp):
            k.sync_work(sp)

        @block.tensor
        def _(pe):
            for i in range(TB):
                b = slice(i * P, (i + 1) * P)
                for h in range(2):
                    cols = slice(i * P + 64 * h, i * P + 64 * h + 64)
                    pe.matmul(k.psum[half[h], 0, b], SA[:, cols], RB[h][:, b], start=True, stop=False)
                    pe.matmul(k.psum[half[h], 0, b], tokV[:, cols], RK[h][:, b], start=False, stop=True)
                for p in range(2):
                    n = 2 * i + p
                    chunk = slice(n * CHUNK, (n + 1) * CHUNK)
                    last = pe.matmul(k.bank(0)[:, chunk], S[:, n, :], rt[:, chunk], start=False, stop=True,
                                     skip_group_check=True)
            last.then_inc(y_done, 1)
            pe.wait_ge(y_copied, 1)
            pe.matmul(k.bank(1), k.c("mean64"), y, start=True, stop=True).then_inc(mean_done, 1)
            pe.wait_ge(squared, 1)
            pe.matmul(k.bank(2), k.c("mean64"), sq, start=True, stop=True).then_inc(var_done, 1)

        @block.scalar
        def _(act):
            act.wait_ge(y_done, 1)
            act.activation(y, k.bank(0), ACT.Copy).then_inc(y_copied, 1)
            act.wait_ge(centred, 1)
            act.activation(sq, y, ACT.Square).then_inc(squared, 1)
            act.wait_ge(var_done, 1)
            act.activation(rstd, k.bank(2), ACT.Sqrt, bias=k.eps(64e-5)).then_inc(root, 1)
            act.wait_ge(scaled, 1)
            act.activation(y, y, ACT.Identity, scale=k.v("lnx_g", j), bias=k.v("lnx_b", j)).then_inc(affine, 1)

        @block.vector
        def _(dve):
            ch = Chain(dve, chain)
            dve.wait_ge(mean_done, 1)
            dve.tensor_tensor(y, y, k.bank(1), ALU.subtract).then_inc(centred, 1)
            dve.wait_ge(root, 1)
            ch.then(dve.reciprocal(rstd, rstd))
            dve.tensor_tensor(y, y, rstd, ALU.mult).then_inc(scaled, 1)
            dve.wait_ge(affine, 1)
            ch.then(dve.tensor_tensor(y, y, bonus, ALU.add))
            ch.then(dve.tensor_tensor(y, y, gate, ALU.mult))



def squared_relu(k, first, src, rhs, out):
    nc = k.nc
    k.begin()
    src_hi, src_lo, relu_done, squared, out_hi, out_lo = (k.sem() for _ in range(6))
    buf = [k.tile(0), k.tile(1)]
    with nc.Block() as block:
        @block.sync
        def _(sp):
            k.sync_work(sp, first + MLP_HALF)

        @block.tensor
        def _(pe):
            for t in range(MLP_HALF):
                if t >= 8:
                    pe.wait_ge(relu_done, t - 7)
                k.product(pe, k.bank(t % 8), first + t, rhs, rhs_ready=src_lo if src and t == 0 else None)

        @block.scalar
        def _(act):
            if src:
                split_tiles_hi(act, src, rhs, src_hi)
            for t in range(MLP_HALF):
                act.wait_ge(k.unit_used, first + t + 1)
                if t >= 2:
                    act.wait_ge(out_lo, t - 1)
                act.activation(buf[t % 2], k.bank(t % 8), ACT.Relu).then_inc(relu_done, 1)
                k.split_hi(act, first + t + AHEAD)
                act.wait_ge(squared, t + 1)
                act.activation(out.hi(t), buf[t % 2], ACT.Copy).then_inc(out_hi, 1)

        @block.vector
        def _(dve):
            if src:
                split_tiles_lo(dve, src, rhs, src_hi, src_lo)
            for t in range(MLP_HALF):
                dve.wait_ge(relu_done, t + 1)
                dve.tensor_tensor(buf[t % 2], buf[t % 2], buf[t % 2], ALU.mult).then_inc(squared, 1)
                k.split_lo(dve, first + t + AHEAD)
                dve.wait_ge(out_hi, t + 1)
                dve.tensor_tensor(out.lo(t), buf[t % 2], out.hi(t).bitcast(F32), ALU.subtract).then_inc(out_lo, 1)


def gated_ffn(k, l, half, first, h, out):
    nc = k.nc
    k.begin()
    base, conv1, conv2, tanh_done, left, finished, out_hi, out_lo = (k.sem() for _ in range(8))
    acc, th = [k.tile(0), k.tile(1)], [k.tile(2), k.tile(3)]
    with nc.Block() as block:
        @block.sync
        def _(sp):
            k.sync_work(sp, first + FFN_TILES)

        @block.tensor
        def _(pe):
            for f in range(FFN_HALF):
                if f >= 4:
                    pe.wait_ge(finished, f - 3)
                for part in range(2):
                    k.product(pe, k.bank(2 * (f % 4) + part), first + 2 * f + part, h)

        @block.scalar
        def _(act):
            for f in range(FFN_HALF):
                j = half * FFN_HALF + f
                act.wait_ge(k.unit_used, first + 2 * f + 1)
                if f >= 2:
                    act.wait_ge(out_lo, f - 1)
                act.activation(acc[f % 2], k.bank(2 * (f % 4)), ACT.Identity, scale=k.v("ffn_w", (3 * l + 2) * FFN_TILES + j),
                               bias=k.v("ffn_b", l * FFN_TILES + j)).then_inc(base, 1)
                k.split_hi(act, first + 2 * f + AHEAD)
                act.wait_ge(conv2, f + 1)
                act.activation(th[f % 2], acc[f % 2], ACT.Tanh, scale=0.5).then_inc(tanh_done, 1)
                k.split_hi(act, first + 2 * f + 1 + AHEAD)
                act.wait_ge(finished, f + 1)
                act.activation(out.hi(f), acc[f % 2], ACT.Copy).then_inc(out_hi, 1)

        @block.vector
        def _(dve):
            for f in range(FFN_HALF):
                j = half * FFN_HALF + f
                g, u, a = k.bank(2 * (f % 4)), k.bank(2 * (f % 4) + 1), acc[f % 2]
                dve.wait_ge(base, f + 1)
                dve.scalar_tensor_tensor(out=a[:, 1:T], in0=g[:, 0:T - 1], scalar=k.v("ffn_w", (3 * l + 1) * FFN_TILES + j),
                                         in1=a[:, 1:T], op0=ALU.mult, op1=ALU.add).then_inc(conv1, 1)
                dve.wait_ge(conv1, f + 1)
                dve.scalar_tensor_tensor(out=a[:, 2:T], in0=g[:, 0:T - 2], scalar=k.v("ffn_w", 3 * l * FFN_TILES + j),
                                         in1=a[:, 2:T], op0=ALU.mult, op1=ALU.add).then_inc(conv2, 1)
                k.split_lo(dve, first + 2 * f + AHEAD)
                dve.wait_ge(tanh_done, f + 1)
                dve.scalar_tensor_tensor(out=a, in0=th[f % 2], scalar=1.0, in1=a, op0=ALU.add, op1=ALU.mult).then_inc(left, 1)
                k.split_lo(dve, first + 2 * f + 1 + AHEAD)
                dve.wait_ge(left, f + 1)
                dve.wait_ge(k.unit_used, first + 2 * f + 2)
                dve.scalar_tensor_tensor(out=a, in0=a, scalar=0.5, in1=u, op0=ALU.mult, op1=ALU.mult).then_inc(finished, 1)
                dve.wait_ge(out_hi, f + 1)
                dve.tensor_tensor(out.lo(f), a, out.hi(f).bitcast(F32), ALU.subtract).then_inc(out_lo, 1)



def head_norms(k, l, bias_in, lam_in):
    nc = k.nc
    k.begin()
    loaded, squared, mean_done, root, inverse, cleared, normed, lam_sum, lam_exp, chain = (k.sem() for _ in range(10))
    src = [k.tile(n) for n in range(8)]
    sq = [k.tile(34), k.tile(35)]
    rs = [k.tile(36), k.tile(37)]
    lam_v = k.tile(38)[:, 0:256]
    lam_p = k.tile(39)[:, 0:128]
    lam = k.small[:, 40:44]
    with nc.Block() as block:
        @block.sync
        def _(sp):
            sp.dma_start(lam_v, lam_in).then_inc(loaded, 16)
            with nc.allow_non_contiguous_dma(reason="one Toeplitz tile per row shift"):
                for h in range(4):
                    sp.dma_start(blocks(k.tile(30 + h)), bias_in(h)).then_inc(loaded, 16)
            sp.wait_ge(loaded, 80)
            k.sync_work(sp)

        @block.gpsimd
        def _(pool):
            for h in range(4):
                pool.memset(k.tile(26 + h)[0:64], 0.0).then_inc(cleared, 1)

        @block.scalar
        def _(act):
            def take_root(n):
                act.wait_ge(mean_done, n + 1)
                if n >= 2:
                    act.wait_ge(normed, n - 1)
                act.activation(rs[n % 2], k.bank(n % 2), ACT.Sqrt, bias=k.eps(64e-6 if n < 4 else 1e-6)).then_inc(root, 1)

            for n in range(8):
                if n >= 2:
                    act.wait_ge(mean_done, n - 1)
                act.activation(sq[n % 2], src[n], ACT.Square).then_inc(squared, 1)
                if n >= 1:
                    take_root(n - 1)
            take_root(7)
            act.wait_ge(lam_sum, 2)
            act.activation(lam[:, 0:2], lam[:, 0:2], ACT.Exp).then_inc(lam_exp, 1)

        @block.tensor
        def _(pe):
            for n in range(8):
                pe.wait_ge(squared, n + 1)
                if n >= 2:
                    pe.wait_ge(root, n - 1)
                pe.matmul(k.bank(n % 2), k.c("sum64" if n < 4 else "mean64"), sq[n % 2], start=True, stop=True).then_inc(mean_done, 1)

        @block.vector
        def _(dve):
            ch = Chain(dve, chain)
            dve.wait_ge(loaded, 80)
            lp = lam_v.rearrange("p (a b c) -> p a b c", a=2, b=2)
            ch.then(dve.tensor_tensor(lam_p.rearrange("p (a c) -> p a c", a=2), lp[:, :, 0, :], lp[:, :, 1, :], ALU.mult))
            dve.reduce_sum(lam[:, 0:1], lam_p[:, 0:64], AX_X).then_inc(lam_sum, 1)
            dve.reduce_sum(lam[:, 1:2], lam_p[:, 64:128], AX_X).then_inc(lam_sum, 1)
            for n in range(8):
                dve.wait_ge(root, n + 1)
                dve.reciprocal(rs[n % 2], rs[n % 2]).then_inc(inverse, 1)
                dve.wait_ge(inverse, n + 1)
                if n < 4:
                    dve.scalar_tensor_tensor(out=src[n], in0=src[n], scalar=k.v("da_q_g", l), in1=rs[n % 2],
                                             op0=ALU.mult, op1=ALU.mult).then_inc(normed, 1)
                else:
                    up = slice(64, 128)
                    ch(dve.scalar_tensor_tensor(out=k.tile(26 + n - 4)[up], in0=src[n][up], scalar=k.v("da_k_g", l)[up],
                                                in1=rs[n % 2][up], op0=ALU.mult, op1=ALU.mult))
                    ch.then(dve.scalar_tensor_tensor(out=src[n][0:64], in0=src[n][0:64], scalar=k.v("da_k_g", l)[0:64],
                                                     in1=rs[n % 2][0:64], op0=ALU.mult, op1=ALU.mult))
                    dve.memset(src[n][up], 0.0).then_inc(normed, 1)
            dve.wait_ge(lam_exp, 1)
            ch.then(dve.tensor_tensor(lam[:, 2:3], lam[:, 1:2], lam[:, 0:1], ALU.subtract))
            ch.then(dve.tensor_scalar(lam[:, 3:4], lam[:, 2:3], -LAM_INIT[l], None, ALU.add))
    return lam[:, 3:4]


def tile_norms(k, jobs, work):
    nc = k.nc
    k.begin()
    squared, mean_done, root, tanh_done, chain = (k.sem() for _ in range(5))
    n_jobs = len(jobs)
    sq = [k.tile(work + n) for n in range(n_jobs)]
    th = [k.tile(work + n_jobs + n) for n in range(n_jobs)]
    with nc.Block() as block:
        @block.sync
        def _(sp):
            k.sync_work(sp)

        @block.scalar
        def _(act):
            for n, (o, mean, gain, factor, gate) in enumerate(jobs):
                act.activation(sq[n], o, ACT.Square).then_inc(squared, 1)
            for n in range(n_jobs):
                act.wait_ge(mean_done, n + 1)
                act.activation(sq[n], k.bank(n), ACT.Sqrt, bias=k.eps(1e-6)).then_inc(root, 1)
            for n, (o, mean, gain, factor, gate) in enumerate(jobs):
                if gate is not None:
                    act.activation(th[n], gate, ACT.Tanh, scale=0.5).then_inc(tanh_done, 1)

        @block.tensor
        def _(pe):
            for n, (o, mean, gain, factor, gate) in enumerate(jobs):
                pe.wait_ge(squared, n + 1)
                pe.matmul(k.bank(n), k.c(mean), sq[n], start=True, stop=True).then_inc(mean_done, 1)

        @block.vector
        def _(dve):
            ch = Chain(dve, chain)
            for n, (o, mean, gain, factor, gate) in enumerate(jobs):
                dve.wait_ge(root, n + 1)
                ch.then(dve.reciprocal(sq[n], sq[n]))
                ch.then(dve.scalar_tensor_tensor(out=o, in0=o, scalar=gain, in1=sq[n], op0=ALU.mult, op1=ALU.mult))
                ch.then(dve.tensor_scalar(o, o, factor, None, ALU.mult))
            gated = [n for n in range(n_jobs) if jobs[n][4] is not None]
            for at, n in enumerate(gated):
                o, gate = jobs[n][0], jobs[n][4]
                dve.wait_ge(tanh_done, at + 1)
                ch.then(dve.scalar_tensor_tensor(out=gate, in0=th[n], scalar=1.0, in1=gate, op0=ALU.add, op1=ALU.mult))
                ch.then(dve.scalar_tensor_tensor(out=o, in0=gate, scalar=0.5, in1=o, op0=ALU.mult, op1=ALU.mult))


def retention(k, q, key, val, work):
    nc = k.nc
    k.begin()
    scores_done, decayed, out_done, copied = (k.sem() for _ in range(4))
    buf = [k.tile(work + n) for n in range(8)]
    half = [slice(0, 64), slice(64, 128)]
    units = [(h, s) for h in range(4) for s in range(TB)]
    decay = k.c("decay")
    with nc.Block() as block:
        @block.sync
        def _(sp):
            k.sync_work(sp)

        @block.tensor
        def _(pe):
            def scores(u):
                h, s = units[u]
                if u >= 6:
                    pe.wait_ge(decayed, u - 5)
                pe.matmul(k.bank(u % 6)[:, 0:T - s * P], key[h // 2][half[h % 2], s * P:(s + 1) * P],
                          q[h // 2][half[h % 2], s * P:T], start=True, stop=True).then_inc(scores_done, 1)

            def out(u):
                h, s = units[u]
                pe.wait_ge(decayed, u + 1)
                last = pe.matmul(k.psum[half[h % 2], 6 + h // 2, s * P:T],
                                 val[h // 2][:, s * P + 64 * (h % 2):s * P + 64 * (h % 2) + 64],
                                 buf[u % 8][:, 0:T - s * P], start=(s == 0), stop=(s == TB - 1))
                last.then_inc(out_done, 1)

            for u in range(len(units)):
                scores(u)
                if u >= 2:
                    out(u - 2)
            out(len(units) - 2)
            out(len(units) - 1)

        @block.vector
        def _(dve):
            for u, (h, s) in enumerate(units):
                dve.wait_ge(scores_done, u + 1)
                if u >= 8:
                    dve.wait_ge(out_done, u - 7)
                dve.tensor_tensor(buf[u % 8][:, 0:T - s * P], decay[:, h * T:h * T + T - s * P],
                                  k.bank(u % 6)[:, 0:T - s * P], ALU.mult).then_inc(decayed, 1)

        @block.scalar
        def _(act):
            for j in range(2):
                act.wait_ge(out_done, 8 * (j + 1))
                act.activation(q[j], k.bank(6 + j), ACT.Copy).then_inc(copied, 1)


def short_conv(k, l, b, c, x):
    nc = k.nc
    k.begin()
    chain = k.sem()
    with nc.Block() as block:
        @block.sync
        def _(sp):
            k.sync_work(sp)

        @block.vector
        def _(dve):
            ch = Chain(dve, chain)
            for j in range(2):
                ch.then(dve.tensor_tensor(c[j], c[j], x[j], ALU.mult))
                ch.then(dve.tensor_scalar(x[j], c[j], k.v("conv_w", 6 * l + 4 + j), k.v("conv_b", 2 * l + j), ALU.mult, ALU.add))
                for s in (1, 2):
                    ch.then(dve.scalar_tensor_tensor(out=x[j][:, s:T], in0=c[j][:, 0:T - s],
                                                     scalar=k.v("conv_w", 6 * l + 2 * (2 - s) + j), in1=x[j][:, s:T],
                                                     op0=ALU.mult, op1=ALU.add))
                ch.then(dve.tensor_tensor(b[j], b[j], x[j], ALU.mult))


def gated_branches(k, l, first, h, src, branch, out, work):
    nc = k.nc
    k.begin()
    src_hi, src_lo, branch_done, tanh_done, chain, read = (k.sem() for _ in range(6))
    gt = k.tile(work, 3)
    part = [k.tile(work + 3 + n) for n in range(3)]
    ks = [range(0, 4), range(4, 6), range(6, 8)]
    with nc.Block() as block:
        @block.sync
        def _(sp):
            k.sync_work(sp, first + 4 * DT)

        @block.tensor
        def _(pe):
            for d in range(DT):
                n = first + 4 * d
                for b in range(3):
                    if d >= 1:
                        pe.wait_ge(tanh_done, 3 * (d - 1) + b + 1)
                    k.product(pe, k.bank(b), n + b, h)
                if d >= 1:
                    pe.wait_ge(read, 3 * d)
                pe.wait_ge(k.lo_ready, n + 4)
                if d == 0:
                    pe.wait_ge(src_lo, DT)
                u = (n + 3) % AHEAD
                for b in range(3):
                    for i in ks[b]:
                        w, end = slice(i * P, (i + 1) * P), i == ks[b][-1]
                        pe.matmul(k.bank(3 + b), k.w_hi[:, u, w], branch.hi(i), start=(i == ks[b][0]), stop=False)
                        pe.matmul(k.bank(3 + b), k.w_hi[:, u, w], branch.lo(i), start=False, stop=False)
                        last = pe.matmul(k.bank(3 + b), k.w_lo[:, u, w], branch.hi(i), start=False, stop=end)
                last.then_inc(k.unit_used, 1)

        @block.scalar
        def _(act):
            split_tiles_hi(act, src, branch, src_hi)
            for d in range(DT):
                n = first + 4 * d
                if d >= 1:
                    act.wait_ge(read, 3 * d)
                for b in range(3):
                    act.wait_ge(k.unit_used, n + b + 1)
                    act.activation(gt[:, b * T:(b + 1) * T], k.bank(b), ACT.Tanh, scale=0.5,
                                   bias=k.v("b_gate", 24 * l + 8 * b + d)).then_inc(tanh_done, 1)
                    k.split_hi(act, n + b + AHEAD)
                k.split_hi(act, n + 3 + AHEAD)

        @block.vector
        def _(dve):
            ch = Chain(dve, chain)
            split_tiles_lo(dve, src, branch, src_hi, src_lo)
            for d in range(DT):
                n = first + 4 * d
                for b in range(3):
                    k.split_lo(dve, n + b + AHEAD)
                dve.wait_ge(tanh_done, 3 * (d + 1))
                ch.then(dve.tensor_scalar(gt, gt, 0.5, 0.5, ALU.mult, ALU.add))
                dve.wait_ge(k.unit_used, n + 4)
                for b in range(3):
                    dve.tensor_tensor(part[b], gt[:, b * T:(b + 1) * T], k.bank(3 + b), ALU.mult).then_inc(read, 1)
                k.split_lo(dve, n + 3 + AHEAD)
                dve.wait_ge(read, 3 * (d + 1))
                ch.then(dve.tensor_tensor(part[0], part[0], part[1], ALU.add))
                ch.then(dve.tensor_tensor(out[d], part[0], part[2], ALU.add))


def epilogue(k, out):
    nc = k.nc
    k.begin()
    with nc.Block() as block:
        @block.sync
        def _(sp):
            sp.dma_start(out, k.xT[:, :, :]).then_inc(k.out_stored, 16)
            sp.wait_ge(k.out_stored, 16)


def program(nc, wts, x_in, const_in, mask_in, vec_in, onehot_in, relb_in, lora_in, lam_in, out, bias_dram):
    with ExitStack() as ctx:
        k = Core(nc, ctx, wts)
        with ExitStack() as phase:
            prologue(k, phase, x_in, const_in, mask_in, vec_in, onehot_in, relb_in, bias_dram)
        x = [k.x(d) for d in range(DT)]
        n = 0
        tiles = lambda a, b: [k.tile(t) for t in range(a, b)]
        MID, EXT = LOW_TILES, LOW_TILES + MID_TILES

        def feed_forward(l, n):
            with ExitStack() as phase:
                k.open_part(phase, 0, 3)
                xs, hidden = k.halves(phase, DT), k.halves(phase, MLP_HALF)
                for half in range(2):
                    squared_relu(k, n, x if half == 0 else None, xs, hidden)
                    n += MLP_HALF
                    project_residual(k, n, None, hidden, ALPHA if half == 0 else 1.0, units=2)
                    n += 2 * DT
                layer_norm(k, "ln2_g", "ln2_b", l, 0)
            return n

        with ExitStack() as phase:
            k.open_part(phase, 0, LOW_TILES)
            k.open_part(phase, MID, MID_TILES)
            with ExitStack() as inner:
                project(k, n, x, k.halves(inner, DT), tiles(0, 27), turned=range(15, 23))
                n += 27
            with ExitStack() as inner:
                k.open_part(inner, EXT, EXT_TILES)
                turn_values(k, tiles(23, 27))
                causal = lambda i, j: [(k.m("ident"), k.m("causal"))] if i == j else []
                attention(k, [([(k.tile(15 + h), k.tile(19 + h), lambda i: 0, causal)], k.tile(23 + h), k.tile(15 + h))
                              for h in range(4)], P ** -0.5, 28)
                rwkv_shift(k)
                rwkv_loras(k, lora_in)
                for j in range(4):
                    rwkv_pair(k, j)
            with ExitStack() as inner:
                project_residual(k, n, tiles(4, 8) + tiles(15, 19), k.halves(inner, DT), ALPHA)
                n += DT
            layer_norm(k, "ln1_g", "ln1_b", 0, 0)
        n = feed_forward(0, n)

        def near(i, j):
            return [(k.m("ident"), k.m("causal" if i == j else "band"))]

        def every(name):
            return lambda i, j: [(k.m("ident"), k.m(name + "causal" if i == j else name))]

        zero, band = lambda i: 0, lambda i: max(i - 1, 0) * P
        with ExitStack() as phase:
            k.open_part(phase, 0, LOW_TILES)
            k.open_part(phase, MID, MID_TILES)
            with ExitStack() as inner:
                project(k, n, x, k.halves(inner, DT), tiles(0, 40), turned=range(32))
                n += 40
            with ExitStack() as inner:
                k.open_part(inner, EXT, EXT_TILES)
                turn_values(k, tiles(32, 40))
                attention(k, [([(k.tile(8 + h), k.tile(24 + h), zero, every("four")),
                                (k.tile(16 + h), k.tile(24 + h), zero, every("sixteen")),
                                (k.tile(h), k.tile(24 + h), band, near)], k.tile(32 + h), k.tile(h)) for h in range(8)],
                          P ** -0.5, EXT)
            with ExitStack() as inner:
                project_residual(k, n, tiles(0, 8), k.halves(inner, DT), ALPHA)
                n += DT
            layer_norm(k, "ln1_g", "ln1_b", 1, 0)
        n = feed_forward(1, n)

        for l in range(DEPTH):
            with ExitStack() as phase:
                k.open_part(phase, 0, LOW_TILES)
                with ExitStack() as mixing:
                    h = k.halves(mixing, DT)
                    with ExitStack() as inner:
                        k.open_part(inner, MID, MID_TILES)
                        rms_norm(k, "norm_mix_g", l, h, 0)
                        project(k, n, None, h, tiles(0, 26), turned=range(12, 16), cos="cos2", sin="sin2", turn="turn2")
                        n += 26

                        def bias_in(head):
                            return bass.AP(bias_dram.tensor, head * (T + P), [[1, P], [P, TB], [1, P]])

                        nlam = head_norms(k, l, bias_in, lam_in[l])
                        turn_values(k, tiles(8, 12) + tiles(16, 18))

                        def relative(head):
                            return lambda i, j: ([(k.tile(30 + head)[:, (i - j) * P:(i - j + 1) * P], k.c("flip"))]
                                                 + ([(k.m("ident"), k.m("causal"))] if i == j else []))

                        attention(k, [([(k.tile(a), k.tile(4 + a), zero, relative(a)),
                                        (k.tile(a), k.tile(26 + a), zero, relative(a))], k.tile(8 + a), k.tile(a))
                                      for a in range(4)], 1.0, 34, difference=nlam)
                        retention(k, tiles(12, 14), tiles(14, 16), tiles(16, 18), 26)
                        tile_norms(k, [(k.tile(a), "mean128", k.v("subln_g", l), 1.0 - LAM_INIT[l], None) for a in range(4)]
                                   + [(k.tile(12 + a), "mean64", k.v("ret_g", l), 1.0, k.tile(18 + a)) for a in range(2)], 26)
                        short_conv(k, l, tiles(20, 22), tiles(22, 24), tiles(24, 26))
                    gated_branches(k, l, n, h, tiles(0, 4) + tiles(12, 14) + tiles(20, 22), k.halves(mixing, DT),
                                   tiles(4, 12), 14)
                    n += 4 * DT
                with ExitStack() as inner:
                    project_residual(k, n, tiles(4, 12), k.halves(inner, DT), 1.0)
                    n += DT
            with ExitStack() as phase:
                k.open_part(phase, 0, 4)
                h, act = k.halves(phase, DT), k.halves(phase, FFN_HALF)
                rms_norm(k, "norm_ffn_g", l, h, 0)
                for half in range(2):
                    gated_ffn(k, l, half, n, h, act)
                    n += FFN_TILES
                    project_residual(k, n, None, act, 1.0, units=2)
                    n += 2 * DT
        assert n == len(UNITS)
        epilogue(k, out)



def pack_weights(i):
    def unit(w):
        if w.shape[1] < P:
            w = np.concatenate([w, np.zeros((w.shape[0], P - w.shape[1]), w.dtype)], 1)
        return w.reshape(-1, P, P).transpose(1, 0, 2).reshape(P, -1)

    def split(w):
        return [unit(w[:, c:c + P]) for c in range(0, w.shape[1], P)]

    def mlp(w1, w2):
        half = MLP_HALF * P
        return [u for h in range(2) for u in split(w1[:, h * half:(h + 1) * half]) + split(w2[h * half:(h + 1) * half])]

    ends = AB_TILES[1:15] + [1824] + AB_TILES[16:] + [i["ab_w_in"].shape[2]]
    g = [unit(i["ab_w_in"][0][:, a:b]) for a, b in zip(AB_TILES, ends)]
    g += split(i["ab_w_out"][0]) + mlp(i["mlp_w1"][0], i["mlp_w2"][0])
    g += split(i["c_w_in"][0]) + split(i["c_w_out"][0]) + mlp(i["mlp_w1"][1], i["mlp_w2"][1])
    for l in range(DEPTH):
        w = i["w_in_2"][l]
        branch = np.concatenate([i["w_branch_da_2"][l], i["w_branch_ret_2"][l], i["w_branch_sc_2"][l]], 0)
        g += split(w[:, 0:3328])
        for d in range(DT):
            g += [unit(w[:, 3328 + b * D + d * P:3328 + b * D + (d + 1) * P]) for b in range(3)]
            g.append(unit(branch[:, d * P:(d + 1) * P]))
        g += split(i["w_out_2"][l])
        f, o = i["w_ffn_in_2"][l], i["w_ffn_out_2"][l]
        inner = FFN_TILES * P
        for h in range(2):
            rows = slice(h * FFN_HALF * P, (h + 1) * FFN_HALF * P)
            g += [unit(f[:, s + c * P:s + (c + 1) * P]) for c in range(h * FFN_HALF, (h + 1) * FFN_HALF) for s in (0, inner)]
            g += split(o[rows])
    return np.concatenate(g, 1)


def pack_vectors(i):
    def cols(v):
        v = np.asarray(v).reshape(-1)
        pad = -len(v) % P
        return np.concatenate([v, np.zeros(pad, v.dtype)]).reshape(-1, P).T

    def twice(v):
        return np.concatenate([v, v], -1)

    def dw(w):
        return w

    parts = {
        "w0": i["ab_w0"], "a0": i["ab_a0"], "b_gate": i["b_gate_2"], "mix": i["ab_shift_mix"], "k_k": i["ab_k_k"],
        "k_a": i["ab_k_a"], "r_k": i["ab_r_k"], "lnx_g": i["ab_lnx_g"], "lnx_b": i["ab_lnx_b"],
        "ln1_g": i["ln1_g"], "ln1_b": i["ln1_b"], "ln2_g": i["ln2_g"], "ln2_b": i["ln2_b"],
        "norm_mix_g": i["norm_mix_g_2"], "norm_ffn_g": i["norm_ffn_g_2"],
        "da_q_g": twice(i["da_q_norm_g_2"]), "da_k_g": twice(i["da_k_norm_g_2"]), "subln_g": i["da_subln_g_2"],
        "ret_g": twice(i["ret_norm_g_2"]), "conv_w": dw(i["sc_conv_w_2"]), "conv_b": i["sc_conv_b_2"],
        "ffn_w": dw(i["ffn_conv_w_2"]), "ffn_b": i["ffn_conv_b_2"],
    }
    out = [cols(parts[name]) for name, _ in vector_entries()]
    return np.concatenate(out, 1)


def build(nc, shapes):
    ap = {n: nc.dram_tensor("in_" + n, s, mybir.dt.from_np(np.dtype(d)), kind="ExternalInput").ap() for n, (s, d) in shapes.items()}
    out = nc.dram_tensor("out", (P, DT, T), F32, kind="ExternalOutput").ap()
    bias_dram = nc.dram_tensor("bias_by_distance", (4, T + P), F32, kind="Internal").ap()
    program(nc, ap["weights"], ap["x"], ap["const"], ap["mask"], ap["vectors"], ap["onehot"], ap["rel_bias"],
            ap["lora"], [ap["lam0"], ap["lam1"]], out, bias_dram)




def kernel(**inputs):
    import concourse.bacc as bacc
    from concourse.bass_utils import run_bass_kernel_spmd as run

    i = {n: np.asarray(a) for n, a in inputs.items()}
    const, mask, onehot = constants()
    z = np.zeros((64, 512), np.float32)
    gup = i["ab_g_up"][0]
    lora = np.concatenate([np.concatenate([i["ab_w_up"][0], z], 0), np.concatenate([z, i["ab_a_up"][0]], 0),
                           gup[0:P], np.concatenate([gup[P:], np.zeros((2 * P - gup.shape[0], 512), np.float32)], 0)], 1)
    arrays = {
        "weights": pack_weights(i),
        "x": np.ascontiguousarray(i["x"][0].T.reshape(DT, P, T).transpose(1, 0, 2)),
        "const": const, "mask": mask, "vectors": np.ascontiguousarray(pack_vectors(i)), "onehot": onehot,
        "rel_bias": np.ascontiguousarray(i["rel_bias_2"]), "lora": lora,
        "lam0": np.ascontiguousarray(np.broadcast_to(i["da_lambda_2"][0].reshape(1, 256), (P, 256))),
        "lam1": np.ascontiguousarray(np.broadcast_to(i["da_lambda_2"][1].reshape(1, 256), (P, 256))),
    }
    nc = bacc.Bacc("TRN2", target_bir_lowering=False, num_devices=1)
    build(nc, {n: (a.shape, a.dtype) for n, a in arrays.items()})
    got = run(nc, [{"in_" + n: a for n, a in arrays.items()}], core_ids=[0]).results[0]["out"]
    return np.ascontiguousarray(got.transpose(1, 0, 2).reshape(D, T).T).reshape(1, T, D)
```

```python
from contextlib import ExitStack

import numpy as np

import concourse.bass as bass
from concourse import mybir

F32 = mybir.dt.float32
F32R = mybir.dt.float32r
BF16 = mybir.dt.bfloat16
ACT = mybir.ActivationFunctionType
ALU = mybir.AluOpType
AX_X = mybir.AxisListType.X

P = 128
T = 512
TB = T // P
D = 1024
DT = D // P
DEPTH = 2
ALPHA = (2 * DEPTH) ** 0.25
ROPE_THETA, ROPE_THETA_2 = 500000.0, 10000.0
MLP_TILES = 4 * D // P
FFN_TILES = 2816 // P
CHUNK = 64
NCHUNK = T // CHUNK
LEVELS = 6
UNIT = DT * P
SLOT = 2 * UNIT
RING = 3
AHEAD = 3
LOW, MID, EXTRA, EXT = 0, 24, 40, 47
PART_TILES = {LOW: 24, MID: 16, EXTRA: 7, EXT: 16}
NEG = -1.0e30
LAM_INIT = [0.8 - 0.6 * float(np.exp(-0.3 * l)) for l in range(DEPTH)]



def layout(entries):
    at, out = 0, {}
    for name, width in entries:
        out[name] = (at, width)
        at += width
    return out, at


COMMON = [("ident", P), ("mean", P), ("mean64", P), ("sum64", P), ("eps", 4)]
FIRST = [("cos", T), ("sin", T), ("turn", P), ("reset", T), ("pair", P), ("low0", P)] + \
    [(f"up{l}", P) for l in range(LEVELS)] + [("up", P), ("upincl", P)]
SECOND = [("cos2", T), ("sin2", T), ("turn2", P), ("decay", 4 * T), ("mean128", P), ("flip", P)]
CONST_PARTS = [layout(part) for part in (COMMON, FIRST, SECOND)]
CONSTS, CONST_W = layout(COMMON + FIRST + SECOND)
MASKS = ["ident", "causal", "band", "four", "fourcausal", "sixteen", "sixteencausal"]
EPS = [1e-5, 1e-6, 64e-6, 64e-5]


def constants():
    c = np.zeros((P, CONST_W), np.float32)

    def put(name, value):
        at, width = CONSTS[name]
        c[:, at:at + width] = value

    pos = np.arange(T, dtype=np.float32)

    def rope(cos, sin, turn, theta, half, period):
        inv = np.float32(theta) ** (-np.arange(half, dtype=np.float32) / np.float32(half))
        ang = pos[None, :] * inv[:, None].astype(np.float32)
        co, si, tu = np.ones((P, T)), np.zeros((P, T)), np.zeros((P, P))
        for b in range(0, P, period):
            co[b:b + half] = co[b + half:b + 2 * half] = np.cos(ang)
            si[b:b + half] = si[b + half:b + 2 * half] = np.sin(ang)
            for i in range(half):
                tu[b + half + i, b + i] = -1.0
                tu[b + i, b + half + i] = 1.0
        put(cos, co)
        put(sin, si)
        put(turn, tu)

    rope("cos", "sin", "turn", ROPE_THETA, 16, P)
    rope("cos2", "sin2", "turn2", ROPE_THETA_2, 32, 64)
    lg = np.log(1.0 - 2.0 ** (-5.0 - np.arange(4)))
    n = np.arange(T)[None, :] - np.arange(P)[:, None]
    put("decay", np.concatenate([np.where(n >= 0, np.exp(g * np.maximum(n, 0)), 0.0) / 8.0 for g in lg], 1))
    put("reset", np.broadcast_to((np.arange(T) % CHUNK != 0).astype(np.float32), (P, T)))
    a, b = np.arange(P)[:, None], np.arange(P)[None, :]
    block = a // 64 == b // 64
    put("ident", a == b)
    put("mean", 1.0 / D)
    put("mean128", 1.0 / P)
    put("mean64", block / 64.0)
    put("sum64", block)
    put("flip", a + b == P - 1)
    put("pair", block)
    for l in range(LEVELS):
        w = 1 << l
        low = (a // (2 * w) == b // (2 * w)) & (a % (2 * w) >= w) & (b % (2 * w) < w)
        if l == 0:
            put("low0", low)
        put(f"up{l}", low.T)
    put("up", block & (a < b))
    put("upincl", block & (a <= b))
    put("eps", np.broadcast_to(np.array(EPS, np.float32), (P, len(EPS))))
    d = a - b
    masks = {"ident": (d == 0) * 1.0, "causal": np.where(d >= 0, 0, NEG), "band": np.where(d <= 0, 0, NEG),
             "four": np.where(d % 4 == 0, 0, NEG), "fourcausal": np.where((d % 4 == 0) & (d >= 0), 0, NEG),
             "sixteen": np.where(d % 16 == 0, 0, NEG), "sixteencausal": np.where((d % 16 == 0) & (d >= 0), 0, NEG)}
    m = np.concatenate([masks[k] for k in MASKS], 1).astype(np.float32)
    dist = np.maximum(np.arange(T + P) - (P - 1), 0)
    nf = np.maximum(dist, 1).astype(np.float32)
    large = 16 + (np.log(nf / np.float32(16)) / np.float32(np.log(8.0)) * np.float32(16)).astype(np.int32)
    bucket = np.where(dist < 16, dist, np.minimum(large, 31))
    onehot = (bucket[None, :] == np.arange(32)[:, None]).astype(np.float32)
    return c, m, onehot



def vector_entries():
    e = [("w0", 4), ("a0", 4), ("b_gate", 24 * DEPTH)]
    e += [("mix", 15), ("k_k", 4), ("k_a", 4), ("r_k", 4), ("lnx_g", 4), ("lnx_b", 4)]
    e += [(n, DT * DEPTH) for n in ("ln1_g", "ln1_b", "ln2_g", "ln2_b", "norm_mix_g", "norm_ffn_g")]
    e += [(n, DEPTH) for n in ("da_q_g", "da_k_g", "subln_g", "ret_g")]
    e += [("conv_w", 6 * DEPTH), ("conv_b", 2 * DEPTH), ("ffn_w", 3 * FFN_TILES * DEPTH), ("ffn_b", FFN_TILES * DEPTH)]
    return e


VECTORS, VECTOR_W = layout(vector_entries())
HALVED = 8 + 24 * DEPTH

AB_TILES = [c * P for c in range(14)] + [1792] + [1824 + c * P for c in range(12)]
MLP_HALF, FFN_HALF = MLP_TILES // 2, FFN_TILES // 2
FFN_PARTS = [6, 5]


def unit_parts():
    mlp = ([8] * MLP_HALF + [8, 8] * DT) * 2
    u = [8] * (27 + DT) + mlp + [8] * (40 + DT) + mlp
    for _ in range(DEPTH):
        u += [8] * (26 + 4 * DT + DT) + ([8] * FFN_TILES + FFN_PARTS * DT) * 2
    return u


UNITS = unit_parts()


def group_units():
    groups, n = [], 0
    while n < len(UNITS):
        end = n + 1
        while end < len(UNITS) and sum(UNITS[n:end + 1]) * P <= SLOT and end - n < 2:
            end += 1
        groups.append((n, end))
        n = end
    return groups


GROUPS = group_units()
GROUP_OF = [g for g, (a, b) in enumerate(GROUPS) for _ in range(a, b)]
UNIT_AT = [P * sum(UNITS[:n]) for n in range(len(UNITS) + 1)]


class Halves:

    def __init__(self, hi, lo):
        self.hi_t, self.lo_t = hi, lo

    def hi(self, n):
        return self.hi_t[:, n, :]

    def lo(self, n):
        return self.lo_t[:, n, :]


class Core:

    def __init__(self, nc, ctx, wts):
        self.nc = nc
        self.names = 0
        self.ring = ctx.enter_context(nc.sbuf_tensor("ring", [P, RING, SLOT], F32))
        self.w_hi = ctx.enter_context(nc.sbuf_tensor("w_hi", [P, AHEAD, UNIT], F32R))
        self.w_lo = ctx.enter_context(nc.sbuf_tensor("w_lo", [P, AHEAD, UNIT], F32R))
        self.xT = ctx.enter_context(nc.sbuf_tensor("xT", [P, DT, T], F32))
        self.consts = {}
        self.common = self.open_constants(ctx, 0)
        self.mask = ctx.enter_context(nc.sbuf_tensor("mask", [P, len(MASKS) * P], BF16))
        self.vec = ctx.enter_context(nc.sbuf_tensor("vec", [P, VECTOR_W], F32))
        self.small = ctx.enter_context(nc.sbuf_tensor("small", [P, 64], F32))
        self.psum = ctx.enter_context(nc.psum_tensor("psum", [P, 8, T], F32))
        sem = lambda name: ctx.enter_context(nc.semaphore(name))
        self.slot_filled = [sem(f"slot_filled{i}") for i in range(RING)]
        self.hi_ready, self.lo_ready, self.unit_used = sem("hi_ready"), sem("lo_ready"), sem("unit_used")
        self.out_stored = sem("out_stored")
        self.pools = [[sem(f"stage{p}_{i}") for i in range(24)] for p in range(2)]
        self.parts = {}
        self.stage = 0
        self.next_sem = 0
        self.next_group = 0
        self.wts = wts

    def space(self, stack, tiles, dtype=F32):
        self.names += 1
        return stack.enter_context(self.nc.sbuf_tensor(f"space{self.names}", [P, tiles, T], dtype))

    def halves(self, stack, tiles):
        return Halves(self.space(stack, tiles, F32R), self.space(stack, tiles, F32R))

    def open_constants(self, stack, part):
        entries, width = CONST_PARTS[part]
        held = stack.enter_context(self.nc.sbuf_tensor(f"constants{part}", [P, width], F32))
        self.consts.update({name: held[:, at:at + w] for name, (at, w) in entries.items()})
        return held

    def open_part(self, stack, first, tiles=None):
        tiles = tiles or PART_TILES[first]
        for other in [f for f in self.parts if first <= f < first + tiles or f <= first < f + self.parts[f][1]]:
            del self.parts[other]
        self.parts[first] = (self.space(stack, tiles), tiles)

    def x(self, d):
        return self.xT[:, d, :]

    def tile(self, n, count=1):
        first = max(f for f in self.parts if f <= n)
        part, tiles = self.parts[first]
        assert n + count <= first + tiles, (n, count)
        return part[:, n - first:n - first + count, :].rearrange("p a t -> p (a t)")

    def bank(self, b):
        return self.psum[:, b, :]

    def c(self, name):
        return self.consts[name]

    def m(self, name):
        n = MASKS.index(name)
        return self.mask[:, n * P:(n + 1) * P]

    def v(self, name, j):
        at, width = VECTORS[name]
        assert j < width
        return self.vec[:, at + j:at + j + 1]

    def eps(self, value):
        at = EPS.index(value)
        return self.c("eps")[:, at:at + 1]

    def begin(self):
        self.stage += 1
        self.next_sem = 0

    def sem(self):
        self.next_sem += 1
        return self.pools[self.stage % 2][self.next_sem - 1]

    def fill(self, sp, stop):
        while self.next_group < len(GROUPS):
            g = self.next_group
            if g >= RING:
                split = GROUPS[g - RING][1]
                if split > stop:
                    break
                sp.wait_ge(self.lo_ready, split)
            a, b = UNIT_AT[GROUPS[g][0]], UNIT_AT[GROUPS[g][1]]
            sp.dma_start(self.ring[:, g % RING, 0:b - a], self.wts[:, a:b]).then_inc(self.slot_filled[g % RING], 16)
            self.next_group += 1

    def sync_work(self, sp, end=None):
        for s in self.pools[(self.stage + 1) % 2]:
            sp.sem_clear(s)
        if end is not None:
            self.fill(sp, end + AHEAD)

    def raw(self, n):
        g = GROUP_OF[n]
        at = UNIT_AT[n] - UNIT_AT[GROUPS[g][0]]
        return self.ring[:, g % RING, at:at + UNITS[n] * P]

    def split_hi(self, act, n):
        if n >= len(UNITS):
            return
        g = GROUP_OF[n]
        act.wait_ge(self.slot_filled[g % RING], 16 * (g // RING + 1))
        if n >= AHEAD:
            act.wait_ge(self.unit_used, n - AHEAD + 1)
        act.activation(self.w_hi[:, n % AHEAD, 0:UNITS[n] * P], self.raw(n), ACT.Copy).then_inc(self.hi_ready, 1)

    def split_lo(self, dve, n):
        if n >= len(UNITS):
            return
        w = slice(0, UNITS[n] * P)
        dve.wait_ge(self.hi_ready, n + 1)
        dve.tensor_tensor(self.w_lo[:, n % AHEAD, w], self.raw(n), self.w_hi[:, n % AHEAD, w].bitcast(F32),
                          ALU.subtract).then_inc(self.lo_ready, 1)

    def product(self, pe, out, n, rhs, first=0, units=1, rhs_ready=None):
        at, total = 0, sum(UNITS[n:n + units])
        for u in range(n, n + units):
            pe.wait_ge(self.lo_ready, u + 1)
            for i in range(UNITS[u]):
                w = slice(i * P, (i + 1) * P)
                hi, lo = self.w_hi[:, u % AHEAD, w], self.w_lo[:, u % AHEAD, w]
                if rhs_ready is not None:
                    pe.wait_ge(rhs_ready, at + 1)
                pe.matmul(out, hi, rhs.hi(first + at), start=(at == 0), stop=False)
                pe.matmul(out, hi, rhs.lo(first + at), start=False, stop=False)
                last = pe.matmul(out, lo, rhs.hi(first + at), start=False, stop=(at == total - 1))
                at += 1
            last.then_inc(self.unit_used, 1)


class Chain:

    def __init__(self, eng, sem):
        self.eng, self.sem, self.n = eng, sem, 0

    def __call__(self, ins):
        ins.then_inc(self.sem, 1)
        self.n += 1
        return self.n

    def sync(self):
        self.eng.wait_ge(self.sem, self.n)

    def then(self, ins):
        self(ins)
        self.sync()


class Work:

    def __init__(self, ticks, tensor=None, scalar=None, vector=None, gpsimd=None, end=None):
        self.ticks, self.tensor, self.scalar, self.vector, self.gpsimd, self.end = ticks, tensor, scalar, vector, gpsimd, end


def in_turn(works):
    return [(w, t) for t in range(max(w.ticks for w in works)) for w in works if t < w.ticks]


def behind(lead, work, after):
    out, u = [], 0
    for t in range(lead.ticks):
        out.append((lead, t))
        while u < work.ticks and after(u) <= t:
            out.append((work, u))
            u += 1
    return out + [(work, v) for v in range(u, work.ticks)]


def run(k, schedule):
    ends = [w.end for w, _ in schedule if w.end is not None]
    with k.nc.Block() as block:
        @block.sync
        def _(sp):
            k.sync_work(sp, max(ends) if ends else None)

        @block.tensor
        def _(pe):
            for w, t in schedule:
                if w.tensor:
                    w.tensor(pe, t)

        @block.scalar
        def _(act):
            for w, t in schedule:
                if w.scalar:
                    w.scalar(act, t)

        @block.vector
        def _(dve):
            for w, t in schedule:
                if w.vector:
                    w.vector(dve, t)

        @block.gpsimd
        def _(pool):
            for w, t in schedule:
                if w.gpsimd:
                    w.gpsimd(pool, t)



def prologue(k, stack, first_const, x_in, const_in, mask_in, vec_in, onehot_in, relb_in, bias_dram):
    nc = k.nc
    loaded, halved, bias_done, bias_copied, stored, oh_loaded = (k.sem() for _ in range(6))
    k.open_part(stack, 0, 6)
    onehot = k.tile(0, 2)[0:32, 0:T + P]
    relb = k.tile(0, 2)[0:32, T + P:T + P + 4]
    row = k.tile(2, 2)[0:4, 0:T + P]
    masks = k.tile(4, 2)[:, 0:len(MASKS) * P]
    with nc.Block() as block:
        @block.sync
        def _(sp):
            sp.dma_start(k.xT[:, :, :], x_in).then_inc(loaded, 16)
            sp.dma_start(k.vec[:, :], vec_in).then_inc(loaded, 16)
            sp.dma_start(masks, mask_in).then_inc(loaded, 16)
            sp.dma_start(onehot, onehot_in).then_inc(oh_loaded, 16)
            sp.dma_start(relb, relb_in).then_inc(oh_loaded, 16)
            k.fill(sp, 0)
            a = CONST_PARTS[0][1]
            sp.dma_start(k.common[:, :], const_in[:, 0:a]).then_inc(loaded, 16)
            sp.dma_start(first_const[:, :], const_in[:, a:a + CONST_PARTS[1][1]]).then_inc(loaded, 16)
            sp.wait_ge(bias_copied, 2)
            sp.dma_start(bias_dram, row).then_inc(stored, 16)
            sp.wait_ge(stored, 16)
            sp.wait_ge(loaded, 80)

        @block.vector
        def _(dve):
            dve.wait_ge(loaded, 80)
            dve.tensor_scalar(k.vec[:, 0:HALVED], k.vec[:, 0:HALVED], 0.5, None, ALU.mult).then_inc(halved, 1)
            dve.tensor_copy(k.mask[:, :], masks).then_inc(halved, 1)
            for n in range(AHEAD):
                k.split_lo(dve, n)

        @block.tensor
        def _(pe):
            pe.wait_ge(oh_loaded, 32)
            for b, (lo, hi) in enumerate(((0, T), (T, T + P))):
                pe.matmul(k.psum[0:4, b, 0:hi - lo], relb, onehot[:, lo:hi], start=True, stop=True).then_inc(bias_done, 1)

        @block.scalar
        def _(act):
            for b, (lo, hi) in enumerate(((0, T), (T, T + P))):
                act.wait_ge(bias_done, b + 1)
                act.activation(row[:, lo:hi], k.psum[0:4, b, 0:hi - lo], ACT.Copy).then_inc(bias_copied, 1)
            for n in range(AHEAD):
                k.split_hi(act, n)


def split_tiles_hi(act, tiles, halves, ready):
    for n, v in enumerate(tiles):
        act.activation(halves.hi(n), v, ACT.Copy).then_inc(ready, 1)


def split_tiles_lo(dve, tiles, halves, hi_ready, ready):
    for n, v in enumerate(tiles):
        dve.wait_ge(hi_ready, n + 1)
        dve.tensor_tensor(halves.lo(n), v, halves.hi(n).bitcast(F32), ALU.subtract).then_inc(ready, 1)


def project(k, first, src, rhs, out, turned=(), cos="cos", sin="sin", turn="turn", banks=(0, 1, 2, 3, 4, 5),
            turn_banks=(6, 7), free=None):
    src_hi, src_lo, copied, turned_done, chain, roped = (k.sem() for _ in range(6))
    order = [t for t in range(len(out)) if t in turned]
    n_out = len(out)

    def due(t):
        return [r for r, o in enumerate(order) if o == t - 2]

    def tensor(pe, t):
        for r in due(t):
            nb = len(turn_banks)
            pe.wait_ge(copied, order[r] + 1)
            if r >= nb:
                pe.wait_ge(roped, r - nb + 1)
            pe.matmul(k.bank(turn_banks[r % nb]), k.c(turn), out[order[r]], start=True, stop=True).then_inc(turned_done, 1)
        if t < n_out:
            if t >= len(banks):
                pe.wait_ge(copied, t - len(banks) + 1)
            k.product(pe, k.bank(banks[t % len(banks)]), first + t, rhs, rhs_ready=src_lo if src and t == 0 else None)

    def scalar(act, t):
        if t == 0 and src:
            split_tiles_hi(act, src, rhs, src_hi)
        if 1 <= t <= n_out:
            o = t - 1
            if free is not None:
                free(act, o)
            act.wait_ge(k.unit_used, first + t)
            act.activation(out[o], k.bank(banks[o % len(banks)]), ACT.Copy).then_inc(copied, 1)
            k.split_hi(act, first + o + AHEAD)

    chains = []

    def vector(dve, t):
        if t == 0:
            chains.append(Chain(dve, chain))
            if src:
                split_tiles_lo(dve, src, rhs, src_hi, src_lo)
        ch = chains[0]
        if 1 <= t <= n_out:
            k.split_lo(dve, first + t - 1 + AHEAD)
        for r in due(t):
            bank, o = k.bank(turn_banks[r % len(turn_banks)]), out[order[r]]
            dve.wait_ge(turned_done, r + 1)
            ch(dve.tensor_tensor(bank, bank, k.c(sin), ALU.mult))
            ch.then(dve.tensor_tensor(o, o, k.c(cos), ALU.mult))
            dve.tensor_tensor(o, o, bank, ALU.add).then_inc(roped, 1)

    w = Work(n_out + 2, tensor, scalar, vector, end=first + n_out)
    w.copied, w.roped = copied, roped
    return w


def project_residual(k, first, src, rhs, scale, units=1):
    nc = k.nc
    k.begin()
    src_hi, src_lo, added = (k.sem() for _ in range(3))
    end = first + DT * units
    with nc.Block() as block:
        @block.sync
        def _(sp):
            k.sync_work(sp, end)

        @block.scalar
        def _(act):
            if src:
                split_tiles_hi(act, src, rhs, src_hi)
            for n in range(first, end):
                k.split_hi(act, n + AHEAD)

        @block.tensor
        def _(pe):
            for t in range(DT):
                k.product(pe, k.bank(t), first + t * units, rhs, units=units, rhs_ready=src_lo if src and t == 0 else None)

        @block.vector
        def _(dve):
            if src:
                split_tiles_lo(dve, src, rhs, src_hi, src_lo)
            for t in range(DT):
                for n in range(first + t * units, first + (t + 1) * units):
                    k.split_lo(dve, n + AHEAD)
                dve.wait_ge(k.unit_used, first + (t + 1) * units)
                dve.scalar_tensor_tensor(out=k.x(t), in0=k.x(t), scalar=scale, in1=k.bank(t),
                                         op0=ALU.mult, op1=ALU.add).then_inc(added, 1)


def layer_norm(k, g, b, j, scratch):
    nc = k.nc
    k.begin()
    mean_done, centred, squared, var_done, root, inverse, scaled, shifted = (k.sem() for _ in range(8))
    sq = [k.tile(scratch), k.tile(scratch + 1)]
    rstd = k.tile(scratch + 2)
    with nc.Block() as block:
        @block.sync
        def _(sp):
            k.sync_work(sp)

        @block.tensor
        def _(pe):
            for d in range(DT):
                last = pe.matmul(k.bank(0), k.c("mean"), k.x(d), start=(d == 0), stop=(d == DT - 1))
            last.then_inc(mean_done, 1)
            for d in range(DT):
                pe.wait_ge(squared, d + 1)
                pe.matmul(k.bank(1), k.c("mean"), sq[d % 2], start=(d == 0), stop=(d == DT - 1)).then_inc(var_done, 1)

        @block.vector
        def _(dve):
            dve.wait_ge(mean_done, 1)
            for d in range(DT):
                dve.tensor_tensor(k.x(d), k.x(d), k.bank(0), ALU.subtract).then_inc(centred, 1)
            dve.wait_ge(root, 1)
            dve.reciprocal(rstd, rstd).then_inc(inverse, 1)
            dve.wait_ge(inverse, 1)
            for d in range(DT):
                dve.tensor_tensor(k.x(d), k.x(d), rstd, ALU.mult).then_inc(scaled, 1)

        @block.scalar
        def _(act):
            for d in range(DT):
                act.wait_ge(centred, d + 1)
                if d >= 2:
                    act.wait_ge(var_done, d - 1)
                act.activation(sq[d % 2], k.x(d), ACT.Square).then_inc(squared, 1)
            act.wait_ge(var_done, DT)
            act.activation(rstd, k.bank(1), ACT.Sqrt, bias=k.eps(1e-5)).then_inc(root, 1)
            for d in range(DT):
                act.wait_ge(scaled, d + 1)
                act.activation(k.x(d), k.x(d), ACT.Identity, scale=k.v(g, j * DT + d),
                               bias=k.v(b, j * DT + d)).then_inc(shifted, 1)


def rms_norm(k, g, j, out, work):
    nc = k.nc
    k.begin()
    squared, mean_done, root, inverse, scaled, out_hi, out_lo = (k.sem() for _ in range(7))
    sq = [k.tile(work), k.tile(work + 1)]
    rstd = k.tile(work + 2)
    with nc.Block() as block:
        @block.sync
        def _(sp):
            k.sync_work(sp)

        @block.tensor
        def _(pe):
            for d in range(DT):
                pe.wait_ge(squared, d + 1)
                pe.matmul(k.bank(0), k.c("mean"), sq[d % 2], start=(d == 0), stop=(d == DT - 1)).then_inc(mean_done, 1)

        @block.scalar
        def _(act):
            for d in range(DT):
                if d >= 2:
                    act.wait_ge(mean_done, d - 1)
                act.activation(sq[d % 2], k.x(d), ACT.Square).then_inc(squared, 1)
            act.wait_ge(mean_done, DT)
            act.activation(rstd, k.bank(0), ACT.Sqrt, bias=k.eps(1e-6)).then_inc(root, 1)
            for d in range(DT):
                act.wait_ge(scaled, d + 1)
                act.activation(out.hi(d), sq[d % 2], ACT.Copy).then_inc(out_hi, 1)

        @block.vector
        def _(dve):
            dve.wait_ge(root, 1)
            dve.reciprocal(rstd, rstd).then_inc(inverse, 1)
            dve.wait_ge(inverse, 1)
            def lo(d):
                dve.wait_ge(out_hi, d + 1)
                dve.tensor_tensor(out.lo(d), sq[d % 2], out.hi(d).bitcast(F32), ALU.subtract).then_inc(out_lo, 1)

            for d in range(DT):
                if d >= 2:
                    dve.wait_ge(out_lo, d - 1)
                dve.scalar_tensor_tensor(out=sq[d % 2], in0=k.x(d), scalar=k.v(g, j * DT + d), in1=rstd,
                                         op0=ALU.mult, op1=ALU.mult).then_inc(scaled, 1)
                if d >= 1:
                    lo(d - 1)
            lo(DT - 1)


def attention(k, heads, scale, prob, probT, banks, ready=None, difference=None):
    scores_done, maxima, exps_done, probs_ready, turned, turned_copied, out_done, out_copied, chain = \
        (k.sem() for _ in range(9))
    units = [(h, i) for h in range(len(heads)) for i in range(TB)]
    U = len(units)
    G = len(heads[0][0])
    s_bank, t_bank, o_bank = [k.bank(b) for b in banks[:G]], k.bank(banks[G]), k.bank(banks[G + 1])
    s = k.small[:, 0:16]

    def fills(u):
        return max(min(u - 1, U), 0) + (min(u, U) + TB - 1) // TB

    def tensor(pe, u):
        at = fills(u)
        if u < U and units[u][1] == 0:
            h = units[u][0]
            if ready is not None:
                ready(pe, h)
            if at >= 1:
                pe.wait_ge(turned_copied, at)
            for j in range(TB):
                b = slice(j * P, (j + 1) * P)
                last = pe.transpose(t_bank[:, b], heads[h][1][:, b], k.c("ident"))
            last.then_inc(turned, 1)
            at += 1
        if 1 <= u <= U:
            h, i = units[u - 1]
            pe.wait_ge(probs_ready, u)
            if at >= 1:
                pe.wait_ge(turned_copied, at)
            for j in range(i + 1):
                b = slice(j * P, (j + 1) * P)
                last = pe.transpose(t_bank[:, b], prob[0][:, b], k.c("ident"))
            last.then_inc(turned, 1)
            at += 1
        if u < U:
            h, i = units[u]
            if u >= 1:
                pe.wait_ge(exps_done, G * u)
            for g, (q, key, first, terms) in enumerate(heads[h][0]):
                lo, hi = first(i), (i + 1) * P
                adds = [(j, a) for j in range(lo // P, i + 1) for a in terms(i, j)]
                last = pe.matmul(s_bank[g][:, lo:hi], q[:, i * P:(i + 1) * P], key[:, lo:hi], start=True, stop=not adds)
                for n, (j, (lhsT, rhs)) in enumerate(adds):
                    last = pe.matmul(s_bank[g][:, j * P:(j + 1) * P], lhsT, rhs, start=False, stop=(n == len(adds) - 1))
            last.then_inc(scores_done, 1)
        if 1 <= u <= U:
            h, i = units[u - 1]
            pe.wait_ge(turned_copied, at)
            if u >= 2:
                pe.wait_ge(out_copied, u - 1)
            for j in range(i + 1):
                b = slice(j * P, (j + 1) * P)
                last = pe.matmul(o_bank[:, 0:P], heads[h][1][:, b], probT[:, b], start=(j == 0), stop=(j == i))
            last.then_inc(out_done, 1)

    def scalar(act, u):
        at = fills(u)
        if u < U and units[u][1] == 0:
            act.wait_ge(turned, at + 1)
            act.activation(heads[units[u][0]][1], t_bank, ACT.Copy).then_inc(turned_copied, 1)
            at += 1
        if 1 <= u <= U:
            h, i = units[u - 1]
            act.wait_ge(turned, at + 1)
            if u >= 2:
                act.wait_ge(out_done, u - 1)
            act.activation(probT[:, 0:(i + 1) * P], t_bank[:, 0:(i + 1) * P], ACT.Copy).then_inc(turned_copied, 1)
        if u < U:
            h, i = units[u]
            act.wait_ge(maxima, u + 1)
            for g, (q, key, first, terms) in enumerate(heads[h][0]):
                lo, hi = first(i), (i + 1) * P
                nm = s[:, 6 + g:7 + g] if difference is not None else s[:, 6:7]
                act.activation(prob[g][:, lo:hi], s_bank[g][:, lo:hi], ACT.Exp, bias=nm, scale=scale,
                               accum_out=s[:, 3 + g:4 + g]).then_inc(exps_done, 1)

    chains = []

    def vector(dve, u):
        if u == 0:
            chains.append(Chain(dve, chain))
        ch = chains[0]
        if 2 <= u <= U + 1:
            h, i = units[u - 2]
            dve.wait_ge(out_done, u - 1)
            dve.tensor_copy(heads[h][2][:, i * P:(i + 1) * P], o_bank[:, 0:P]).then_inc(out_copied, 1)
        if u < U:
            h, i = units[u]
            dve.wait_ge(scores_done, u + 1)
            if u >= 1:
                dve.wait_ge(turned, fills(u) + (units[u][1] == 0) + 1)
            for g, (q, key, first, terms) in enumerate(heads[h][0]):
                ch(dve.reduce_max(s[:, g:g + 1], s_bank[g][:, first(i):(i + 1) * P], AX_X))
            ch.sync()
            if difference is not None:
                dve.tensor_scalar(s[:, 6:8], s[:, 0:2], -scale, None, ALU.mult).then_inc(maxima, 1)
            else:
                for g in range(1, G):
                    ch.then(dve.tensor_tensor(s[:, 0:1], s[:, 0:1], s[:, g:g + 1], ALU.max))
                dve.tensor_scalar(s[:, 6:7], s[:, 0:1], -scale, None, ALU.mult).then_inc(maxima, 1)
            hi = (i + 1) * P
            dve.wait_ge(exps_done, G * (u + 1))
            if difference is not None:
                ch.then(dve.reciprocal(s[:, 8:10], s[:, 3:5]))
                ch(dve.tensor_scalar(s[:, 9:10], s[:, 9:10], difference, None, ALU.mult))
                ch(dve.tensor_scalar(prob[0][:, 0:hi], prob[0][:, 0:hi], s[:, 8:9], None, ALU.mult))
                ch.sync()
                dve.scalar_tensor_tensor(out=prob[0][:, 0:hi], in0=prob[1][:, 0:hi], scalar=s[:, 9:10],
                                         in1=prob[0][:, 0:hi], op0=ALU.mult, op1=ALU.add).then_inc(probs_ready, 1)
            else:
                for g in range(1, G):
                    lo = heads[h][0][g][2](i)
                    ch(dve.tensor_tensor(s[:, 3:4], s[:, 3:4], s[:, 3 + g:4 + g], ALU.add))
                    ch.then(dve.tensor_tensor(prob[0][:, lo:hi], prob[0][:, lo:hi], prob[g][:, lo:hi], ALU.add))
                ch.then(dve.reciprocal(s[:, 8:9], s[:, 3:4]))
                dve.tensor_scalar(prob[0][:, 0:hi], prob[0][:, 0:hi], s[:, 8:9], None, ALU.mult).then_inc(probs_ready, 1)

    w = Work(U + 2, tensor, scalar, vector)
    w.out_done = out_done
    return w



def rwkv_shift(k):
    stepped, edge, mixed = (k.sem() for _ in range(3))
    zs = [k.tile(n) for n in list(range(12)) + [24, 25, 26]]
    delta = [k.tile(31), k.tile(32), k.tile(33)]

    def gpsimd(pool, t):
        z, d = zs[t], delta[t % 3]
        if t >= 3:
            pool.wait_ge(mixed, t - 2)
        pool.tensor_tensor(d[:, 1:T], z[:, 0:T - 1], z[:, 1:T], ALU.subtract).then_inc(stepped, 1)

    def scalar(act, t):
        if t >= 3:
            act.wait_ge(mixed, t - 2)
        act.activation(delta[t % 3][:, 0:1], zs[t][:, 0:1], ACT.Copy, scale=-1.0).then_inc(edge, 1)

    def vector(dve, t):
        dve.wait_ge(stepped, t + 1)
        dve.wait_ge(edge, t + 1)
        dve.scalar_tensor_tensor(out=zs[t], in0=delta[t % 3], scalar=k.v("mix", t), in1=zs[t], op0=ALU.mult,
                                 op1=ALU.add).then_inc(mixed, 1)

    return Work(len(zs), scalar=scalar, vector=vector, gpsimd=gpsimd)


def rwkv_loras(k, lora_in):
    nc = k.nc
    k.begin()
    loaded, tanh_done, gates_ready, s_done, a_done, g_done, s_tanh, a_tanh, g_copied, gate_tanh, finished = \
        (k.sem() for _ in range(11))
    wup, aup, gup1, gup2 = (k.tile(31 + n) for n in range(4))
    tw = k.tile(35)
    z_wa, z_g = k.tile(24), k.tile(25, 2)
    with nc.Block() as block:
        @block.sync
        def _(sp):
            sp.dma_start(k.tile(31, 4), lora_in).then_inc(loaded, 16)
            sp.wait_ge(loaded, 16)
            k.sync_work(sp)

        @block.scalar
        def _(act):
            act.activation(tw, z_wa, ACT.Tanh).then_inc(tanh_done, 1)
            act.activation(z_g, z_g, ACT.Tanh, scale=0.5).then_inc(gate_tanh, 1)
            for j in range(4):
                act.wait_ge(s_done, j + 1)
                act.activation(k.tile(16 + j), k.bank(j % 2), ACT.Tanh, scale=0.5, bias=k.v("w0", j)).then_inc(s_tanh, 1)
                act.wait_ge(a_done, j + 1)
                act.activation(k.tile(20 + j), k.bank(2 + j % 2), ACT.Tanh, scale=0.5, bias=k.v("a0", j)).then_inc(a_tanh, 1)
                act.wait_ge(g_done, j + 1)
                act.activation(k.tile(27 + j), k.bank(4 + j % 2), ACT.Copy).then_inc(g_copied, 1)

        @block.vector
        def _(dve):
            dve.wait_ge(gate_tanh, 1)
            dve.tensor_scalar(z_g, z_g, 0.5, 0.5, ALU.mult, ALU.add).then_inc(gates_ready, 1)
            half = 0.5 * float(np.exp(-0.5))
            for j in range(4):
                dve.wait_ge(s_tanh, j + 1)
                dve.tensor_scalar(k.tile(16 + j), k.tile(16 + j), -half, -half, ALU.mult, ALU.add).then_inc(finished, 1)
                dve.wait_ge(a_tanh, j + 1)
                dve.tensor_scalar(k.tile(20 + j), k.tile(20 + j), 0.5, 0.5, ALU.mult, ALU.add).then_inc(finished, 1)

        @block.tensor
        def _(pe):
            pe.wait_ge(loaded, 16)
            pe.wait_ge(tanh_done, 1)
            for j in range(4):
                cols = slice(j * P, (j + 1) * P)
                if j >= 2:
                    pe.wait_ge(s_tanh, j - 1)
                    pe.wait_ge(a_tanh, j - 1)
                    pe.wait_ge(g_copied, j - 1)
                pe.matmul(k.bank(j % 2), wup[:, cols], tw, start=True, stop=True).then_inc(s_done, 1)
                pe.matmul(k.bank(2 + j % 2), aup[:, cols], z_wa, start=True, stop=True).then_inc(a_done, 1)
                if j == 0:
                    pe.wait_ge(gates_ready, 1)
                pe.matmul(k.bank(4 + j % 2), gup1[:, cols], z_g[:, 0:T], start=True, stop=False)
                pe.matmul(k.bank(4 + j % 2), gup2[:, cols], z_g[:, T:2 * T], start=False, stop=True).then_inc(g_done, 1)


def blocks(tile):
    return tile.rearrange("p (i t) -> p i t", i=TB)


def spread(mask):
    return mask.unsqueeze(1).to_broadcast([P, TB, P])


HALF = [slice(0, 64), slice(64, 128)]


class Pair:

    def __init__(self, k, j, work, bank, small):
        self.k, self.j = k, j
        W = [k.tile(work + n) for n in range(16)]
        self.r, self.key, self.val, self.lw, self.rate, self.gate = (k.tile(b + j) for b in (0, 4, 8, 16, 20, 27))
        self.at, self.bt, self.kt, self.rt = self.lw, self.rate, self.key, self.r
        self.temps = W[0:10]
        self.bonus = W[15]
        self.tokA, self.tokB, self.tokK, self.tokV = W[0:4]
        self.X, self.XT, self.NT, self.AK, self.level = W[4:6], W[6:8], W[8:10], W[10:12], W[12:14]
        self.av = W[14]
        self.RB, self.RK, self.TA = self.X, self.NT, self.level[0]
        self.SA, self.SAz, self.Vz = self.tokA, self.AK, self.XT
        self.states = [self.level[1], self.val]
        self.banks = [k.bank(bank + b) for b in range(4)]
        self.bank0 = bank
        self.fsum, self.fexp, self.om = (k.small[:, small + a:small + b] for a, b in ((0, 7), (8, 15), (16, 17)))

    def S(self, n):
        return self.states[n // 4][:, (n % 4) * P:(n % 4 + 1) * P]

    def scale(self):
        k, j = self.k, self.j
        square_ready, square_sum, root, rk_ready, bonus_sum, sums_ready, exps_done, chain, read = (k.sem() for _ in range(9))
        kk, sq, t2, rk, cum, cen, prv, nrm, e_in, e_out = self.temps
        r, key, val, lw, rate, om = self.r, self.key, self.val, self.lw, self.rate, self.om

        def tensor(pe, t):
            if t == 0:
                pe.wait_ge(square_ready, 1)
                pe.matmul(self.banks[0], k.c("sum64"), sq, start=True, stop=True).then_inc(square_sum, 1)
                pe.wait_ge(rk_ready, 1)
                pe.matmul(self.banks[1], k.c("sum64"), rk, start=True, stop=True).then_inc(bonus_sum, 1)

        def scalar(act, t):
            if t == 0:
                act.wait_ge(square_sum, 1)
                act.activation(nrm, self.banks[0], ACT.Sqrt).then_inc(root, 1)
            if t == 1:
                act.wait_ge(sums_ready, 1)
                act.activation(e_in, cen, ACT.Exp).then_inc(exps_done, 1)
                act.activation(e_out, cen, ACT.Exp, scale=-1.0).then_inc(exps_done, 1)
                act.activation(prv, prv, ACT.Exp).then_inc(exps_done, 1)
                act.activation(self.fexp, self.fsum, ACT.Exp, scale=0.5).then_inc(exps_done, 1)

        chains = []

        def vector(dve, t):
            if t == 0:
                chains.append(Chain(dve, chain))
                ch = chains[0]
                ch(dve.tensor_scalar(om, k.v("k_a", j), -1.0, 1.0, ALU.mult, ALU.add))
                ch.then(dve.tensor_scalar(kk, key, k.v("k_k", j), None, ALU.mult))
                dve.tensor_tensor(sq, kk, kk, ALU.mult).then_inc(square_ready, 1)
                ch.then(dve.tensor_scalar(t2, rate, k.v("k_a", j), om, ALU.mult, ALU.add))
                ch.then(dve.tensor_tensor(key, key, t2, ALU.mult))
                dve.scalar_tensor_tensor(out=rk, in0=r, scalar=k.v("r_k", j), in1=key, op0=ALU.mult,
                                         op1=ALU.mult).then_inc(rk_ready, 1)
                ch.then(dve.tensor_tensor_scan(cum, k.c("reset"), lw, 0.0, ALU.mult, ALU.add))
                cum3 = cum.rearrange("p (n c) -> p n c", n=NCHUNK)
                total = cum3[:, :, CHUNK - 1:CHUNK]
                ch(dve.tensor_tensor(self.fsum.unsqueeze(2), total[:, 0:NCHUNK - 1, :], total[:, 1:NCHUNK, :], ALU.add))
                ch.then(dve.scalar_tensor_tensor(out=cen.rearrange("p (n c) -> p n c", n=NCHUNK),
                                                 in0=total.to_broadcast([P, NCHUNK, CHUNK]), scalar=-0.5, in1=cum3,
                                                 op0=ALU.mult, op1=ALU.add))
                dve.tensor_tensor(prv, cen, lw, ALU.subtract).then_inc(sums_ready, 1)
            ch = chains[0]
            if t == 1:
                dve.wait_ge(root, 1)
                ch.then(dve.tensor_scalar(nrm, nrm, 1e-12, None, ALU.max))
                ch.then(dve.reciprocal(nrm, nrm))
                ch.then(dve.tensor_tensor(kk, kk, nrm, ALU.mult))
                ch(dve.tensor_tensor(rate, rate, kk, ALU.mult))
                dve.wait_ge(bonus_sum, 1)
                ch(dve.tensor_tensor(self.bonus, val, self.banks[1], ALU.mult))
            if t == 2:
                dve.wait_ge(exps_done, 4)
                ch(dve.scalar_tensor_tensor(out=lw, in0=kk, scalar=-1.0, in1=prv, op0=ALU.mult, op1=ALU.mult))
                ch.sync()
                ch(dve.tensor_tensor(rate, rate, e_out, ALU.mult))
                ch(dve.tensor_tensor(key, key, e_out, ALU.mult))
                ch(dve.tensor_tensor(r, r, e_in, ALU.mult))

        return Work(3, tensor, scalar, vector)

    def matrices(self):
        k = self.k
        made, act_done, dve_done, x_ready, xt_half, xt_ready = (k.sem() for _ in range(6))
        at, bt, kt = self.at, self.bt, self.kt
        X, XT, NT, AK, b4 = self.X, self.XT, self.NT, self.AK, self.banks

        def outer(pe, bank, left, right, h):
            for i in range(TB):
                b = slice(i * P, (i + 1) * P)
                last = pe.matmul(bank[:, b], left[HALF[h], b], right[HALF[h], b], start=True, stop=True)
            last.then_inc(made, 1)

        def tensor(pe, t):
            if t == 0:
                for src, bank in zip((at, bt, kt, self.val), b4):
                    for i in range(TB):
                        b = slice(i * P, (i + 1) * P)
                        last = pe.transpose(bank[:, b], src[:, b], k.c("ident"))
                    last.then_inc(made, 1)
            if t == 1:
                pe.wait_ge(act_done, 1)
                outer(pe, b4[0], at, bt, 0)
                pe.wait_ge(act_done, 2)
                outer(pe, b4[1], bt, at, 0)
                pe.wait_ge(act_done, 3)
                outer(pe, b4[2], kt, at, 0)
            if t == 2:
                pe.wait_ge(act_done, 4)
                outer(pe, b4[3], at, bt, 1)
                pe.wait_ge(dve_done, 1)
                outer(pe, b4[0], bt, at, 1)
                pe.wait_ge(act_done, 5)
                outer(pe, b4[1], kt, at, 1)
            if t == 3:
                pe.wait_ge(dve_done, 4)
                for h in range(2):
                    for i in range(TB):
                        b, cols = slice(i * P, (i + 1) * P), slice(i * P + 64 * h, i * P + 64 * h + 64)
                        last = pe.matmul(b4[2][:, cols], AK[h][:, b], self.tokV[:, cols], start=True, stop=True)
                last.then_inc(made, 1)

        def scalar(act, t):
            if t == 0:
                for n, dst in enumerate((self.tokA, self.tokB, self.tokK, self.tokV)):
                    act.wait_ge(made, n + 1)
                    act.activation(dst, b4[n], ACT.Copy).then_inc(act_done, 1)
            if t in (1, 2):
                act.wait_ge(made, 6 if t == 1 else 9)
                act.activation(NT[t - 1], b4[1 if t == 1 else 0], ACT.Copy).then_inc(act_done, 1)
            if t == 3:
                act.wait_ge(made, 11)
                act.activation(self.av, b4[2], ACT.Copy).then_inc(act_done, 1)

        def vector(dve, t):
            if t in (1, 2):
                h = t - 1
                dve.wait_ge(made, 5 + 3 * h)
                dve.tensor_tensor(blocks(X[h]), blocks(b4[3 * h]), spread(k.c("low0")), ALU.mult).then_inc(dve_done, 1)
                dve.wait_ge(made, 7 + 3 * h)
                dve.tensor_tensor(blocks(AK[h]), blocks(b4[2 - h]), spread(k.c("up")), ALU.mult).then_inc(dve_done, 1)
                dve.wait_ge(dve_done, 2 * h + 1)
                dve.tensor_tensor(blocks(X[h]), blocks(X[h]), spread(k.c("ident")), ALU.add).then_inc(x_ready, 1)

        def gpsimd(pool, t):
            if t in (1, 2):
                h = t - 1
                pool.wait_ge(act_done, 5 + h)
                pool.tensor_tensor(blocks(XT[h]), blocks(NT[h]), spread(k.c("up0")), ALU.mult).then_inc(xt_half, 1)
                pool.wait_ge(xt_half, h + 1)
                pool.tensor_tensor(blocks(XT[h]), blocks(XT[h]), spread(k.c("ident")), ALU.add).then_inc(xt_ready, 1)

        return Work(4, tensor, scalar, vector, gpsimd)

    def invert(self):
        k = self.k
        level_ready, p_done, p_copied, xp_done, x_ready = (k.sem() for _ in range(5))
        X, XT, NT, PR, level = self.X, self.XT, self.NT, self.AK, self.level

        def bank(l, h, what):
            p, q = (0, 2) if l % 2 else (2, 0)
            return self.banks[p + h] if what == "p" else self.banks[(q if h == 0 else p) + what]

        def gpsimd(pool, t):
            l = t + 1
            for h in range(2):
                if l >= 2:
                    pool.wait_ge(p_done, 2 * (l - 2) + h + 1)
                pool.tensor_tensor(blocks(level[h]), blocks(NT[h]), spread(k.c(f"up{l}")), ALU.mult).then_inc(level_ready, 1)

        def tensor(pe, t):
            l, n = t + 1, 2 * t
            for h in range(2):
                pe.wait_ge(level_ready, n + h + 1)
                if l >= 2:
                    pe.wait_ge(x_ready, n - 2 + h + 1)
                for i in range(TB):
                    b = slice(i * P, (i + 1) * P)
                    last = pe.matmul(bank(l, h, "p")[:, b], level[h][:, b], X[h][:, b], start=True, stop=True)
                last.then_inc(p_done, 1)
            for h in range(2):
                pe.wait_ge(p_copied, n + 2 if h == 0 else n + 2)
                if l < LEVELS - 1:
                    for i in range(TB):
                        b = slice(i * P, (i + 1) * P)
                        pe.matmul(bank(l, h, 0)[:, b], XT[h][:, b], PR[h][:, b], start=True, stop=True)
                for i in range(TB):
                    b = slice(i * P, (i + 1) * P)
                    last = pe.matmul(bank(l, h, 1)[:, b], PR[h][:, b], XT[h][:, b], start=True, stop=True)
                last.then_inc(xp_done, 1)

        def scalar(act, t):
            l = t + 1
            for h in range(2):
                act.wait_ge(p_done, 2 * t + h + 1)
                if l >= 2:
                    act.wait_ge(xp_done, 2 * (t - 1) + h + 1)
                act.activation(PR[h], bank(l, h, "p"), ACT.Copy).then_inc(p_copied, 1)

        def vector(dve, t):
            l = t + 1
            for h in range(2):
                dve.wait_ge(xp_done, 2 * t + h + 1)
                if l < LEVELS - 1:
                    dve.tensor_tensor(X[h], X[h], bank(l, h, 0), ALU.add)
                dve.tensor_tensor(XT[h], XT[h], bank(l, h, 1), ALU.add).then_inc(x_ready, 1)

        return Work(LEVELS - 1, tensor, scalar, vector, gpsimd)

    def apply_inverse(self):
        k, b4 = self.k, self.banks
        made, masked, ta_done, tv_done, copied = (k.sem() for _ in range(5))

        def tensor(pe, t):
            if t == 0:
                for h in range(2):
                    for i in range(TB):
                        b, cols = slice(i * P, (i + 1) * P), slice(i * P + 64 * h, i * P + 64 * h + 64)
                        last = pe.matmul(b4[0][HALF[h], b], self.tokA[:, cols], self.XT[h][:, b], start=True, stop=True)
                last.then_inc(ta_done, 1)
                for h in range(2):
                    for i in range(TB):
                        b, cols = slice(i * P, (i + 1) * P), slice(i * P + 64 * h, i * P + 64 * h + 64)
                        last = pe.matmul(b4[1][:, cols], self.XT[h][:, b], self.av[:, cols], start=True, stop=True)
                last.then_inc(tv_done, 1)
            else:
                h = t - 1
                if h == 1:
                    pe.wait_ge(copied, 2)
                for n, left in enumerate((self.bt, self.kt)):
                    for i in range(TB):
                        b = slice(i * P, (i + 1) * P)
                        last = pe.matmul(b4[2 - 2 * h + n][:, b], left[HALF[h], b], self.rt[HALF[h], b], start=True, stop=True)
                    last.then_inc(made, 1)

        def scalar(act, t):
            if t == 0:
                act.wait_ge(ta_done, 1)
                act.activation(self.TA, b4[0], ACT.Copy).then_inc(copied, 1)
                act.wait_ge(tv_done, 1)
                act.activation(self.av, b4[1], ACT.Copy).then_inc(copied, 1)

        def vector(dve, t):
            if t >= 1:
                h = t - 1
                for n, dst in enumerate((self.RB[h], self.RK[h])):
                    dve.wait_ge(made, 2 * h + n + 1)
                    dve.tensor_tensor(blocks(dst), blocks(b4[2 - 2 * h + n]), spread(k.c("upincl")), ALU.mult).then_inc(masked, 1)

        return Work(3, tensor, scalar, vector)

    def chunks(self):
        k, b4 = self.k, self.banks
        cleared, v_copied, sa_done, sa_ready, state_done, state_ready, sa_copied = (k.sem() for _ in range(7))
        SA, SAz, Vz, S, tokV = self.SA, self.SAz, self.Vz, self.S, self.tokV

        def gpsimd(pool, n):
            if n == 0:
                pool.memset(S(0), 0.0).then_inc(cleared, 1)
                for p in range(2):
                    pool.wait_ge(cleared, 2 * p + 1)
                    pool.memset(SAz[p][HALF[1 - p]], 0.0).then_inc(cleared, 1)
                    pool.memset(Vz[p][HALF[1 - p]], 0.0).then_inc(cleared, 1)

        def scalar(act, n):
            if n == 0:
                for p in range(2):
                    act.activation(Vz[p][HALF[p]], tokV[HALF[p]], ACT.Copy).then_inc(v_copied, 1)
            i, p = n // 2, n % 2
            act.wait_ge(sa_ready, n + 1)
            act.activation(SA[HALF[p], i * P:(i + 1) * P], SAz[p][HALF[p], i * P:(i + 1) * P], ACT.Copy).then_inc(sa_copied, 1)

        def tensor(pe, n):
            i, p = n // 2, n % 2
            b = slice(i * P, (i + 1) * P)
            if n == 0:
                pe.wait_ge(cleared, 5)
                pe.wait_ge(v_copied, 2)
            if n >= 1:
                pe.wait_ge(state_ready, n)
            if n >= 2:
                pe.wait_ge(sa_ready, n - 1)
            pe.matmul(b4[n % 2][:, 0:P], self.TA[:, b], S(n), start=True, stop=True).then_inc(sa_done, 1)
            if n == NCHUNK - 1:
                return
            out = b4[2 + n % 2][:, 0:P]
            pe.matmul(out, k.c("ident"), S(n), start=True, stop=False)
            pe.matmul(out, self.tokK[:, b], Vz[p][:, b], start=False, stop=False)
            pe.wait_ge(sa_ready, n + 1)
            pe.matmul(out, self.tokB[:, b], SAz[p][:, b], start=False, stop=True).then_inc(state_done, 1)

        def vector(dve, n):
            i, p = n // 2, n % 2
            b = slice(i * P, (i + 1) * P)
            if n == 0:
                dve.wait_ge(cleared, 5)
            dve.wait_ge(sa_done, n + 1)
            dve.tensor_tensor(SAz[p][HALF[p], b], self.av[HALF[p], b], b4[n % 2][HALF[p], 0:P], ALU.add).then_inc(sa_ready, 1)
            if n == NCHUNK - 1:
                return
            dve.wait_ge(state_done, n + 1)
            dve.scalar_tensor_tensor(out=S(n + 1), in0=b4[2 + n % 2][:, 0:P], scalar=self.fexp[:, n:n + 1],
                                     in1=k.c("pair"), op0=ALU.mult, op1=ALU.mult).then_inc(state_ready, 1)

        return Work(NCHUNK, tensor, scalar, vector, gpsimd)

    def outputs(self):
        k, j, b4 = self.k, self.j, self.banks
        y_done, y_copied, mean_done, centred, squared, var_done, root, chain, scaled, affine = (k.sem() for _ in range(10))
        y, sq, rstd = self.key, self.SAz[0], self.SAz[1]

        def tensor(pe, t):
            if t == 0:
                for i in range(TB):
                    b = slice(i * P, (i + 1) * P)
                    for h in range(2):
                        cols = slice(i * P + 64 * h, i * P + 64 * h + 64)
                        pe.matmul(b4[0][HALF[h], b], self.SA[:, cols], self.RB[h][:, b], start=True, stop=False)
                        pe.matmul(b4[0][HALF[h], b], self.tokV[:, cols], self.RK[h][:, b], start=False, stop=True)
                    for n in (2 * i, 2 * i + 1):
                        chunk = slice(n * CHUNK, (n + 1) * CHUNK)
                        last = pe.matmul(b4[0][:, chunk], self.S(n), self.rt[:, chunk], start=False, stop=True,
                                         skip_group_check=True)
                last.then_inc(y_done, 1)
            if t == 1:
                pe.wait_ge(y_copied, 1)
                pe.matmul(b4[1], k.c("mean64"), y, start=True, stop=True).then_inc(mean_done, 1)
            if t == 2:
                pe.wait_ge(squared, 1)
                pe.matmul(b4[2], k.c("mean64"), sq, start=True, stop=True).then_inc(var_done, 1)

        def scalar(act, t):
            if t == 0:
                act.wait_ge(y_done, 1)
                act.activation(y, b4[0], ACT.Copy).then_inc(y_copied, 1)
            if t == 1:
                act.wait_ge(centred, 1)
                act.activation(sq, y, ACT.Square).then_inc(squared, 1)
            if t == 2:
                act.wait_ge(var_done, 1)
                act.activation(rstd, b4[2], ACT.Sqrt, bias=k.eps(64e-5)).then_inc(root, 1)
            if t == 3:
                act.wait_ge(scaled, 1)
                act.activation(y, y, ACT.Identity, scale=k.v("lnx_g", j), bias=k.v("lnx_b", j)).then_inc(affine, 1)

        chains = []

        def vector(dve, t):
            if t == 0:
                chains.append(Chain(dve, chain))
            ch = chains[0]
            if t == 1:
                dve.wait_ge(mean_done, 1)
                dve.tensor_tensor(y, y, b4[1], ALU.subtract).then_inc(centred, 1)
            if t == 3:
                dve.wait_ge(root, 1)
                ch.then(dve.reciprocal(rstd, rstd))
                dve.tensor_tensor(y, y, rstd, ALU.mult).then_inc(scaled, 1)
            if t == 4:
                dve.wait_ge(affine, 1)
                ch.then(dve.tensor_tensor(y, y, self.bonus, ALU.add))
                ch.then(dve.tensor_tensor(y, y, self.gate, ALU.mult))

        return Work(5, tensor, scalar, vector)



def squared_relu(k, first, src, rhs, out):
    nc = k.nc
    k.begin()
    src_hi, src_lo, relu_done, squared, out_hi, out_lo = (k.sem() for _ in range(6))
    buf = [k.tile(0), k.tile(1)]
    with nc.Block() as block:
        @block.sync
        def _(sp):
            k.sync_work(sp, first + MLP_HALF)

        @block.tensor
        def _(pe):
            for t in range(MLP_HALF):
                if t >= 8:
                    pe.wait_ge(relu_done, t - 7)
                k.product(pe, k.bank(t % 8), first + t, rhs, rhs_ready=src_lo if src and t == 0 else None)

        @block.scalar
        def _(act):
            if src:
                split_tiles_hi(act, src, rhs, src_hi)
            for t in range(MLP_HALF):
                act.wait_ge(k.unit_used, first + t + 1)
                if t >= 2:
                    act.wait_ge(out_lo, t - 1)
                act.activation(buf[t % 2], k.bank(t % 8), ACT.Relu).then_inc(relu_done, 1)
                k.split_hi(act, first + t + AHEAD)
                act.wait_ge(squared, t + 1)
                act.activation(out.hi(t), buf[t % 2], ACT.Copy).then_inc(out_hi, 1)

        @block.vector
        def _(dve):
            if src:
                split_tiles_lo(dve, src, rhs, src_hi, src_lo)
            for t in range(MLP_HALF):
                dve.wait_ge(relu_done, t + 1)
                dve.tensor_tensor(buf[t % 2], buf[t % 2], buf[t % 2], ALU.mult).then_inc(squared, 1)
                k.split_lo(dve, first + t + AHEAD)
                dve.wait_ge(out_hi, t + 1)
                dve.tensor_tensor(out.lo(t), buf[t % 2], out.hi(t).bitcast(F32), ALU.subtract).then_inc(out_lo, 1)


def gated_ffn(k, l, half, first, h, out):
    nc = k.nc
    k.begin()
    base, conv1, conv2, tanh_done, left, finished, out_hi, out_lo = (k.sem() for _ in range(8))
    acc, th = [k.tile(0), k.tile(1)], [k.tile(2), k.tile(3)]
    with nc.Block() as block:
        @block.sync
        def _(sp):
            k.sync_work(sp, first + FFN_TILES)

        @block.tensor
        def _(pe):
            for f in range(FFN_HALF):
                if f >= 4:
                    pe.wait_ge(finished, f - 3)
                for part in range(2):
                    k.product(pe, k.bank(2 * (f % 4) + part), first + 2 * f + part, h)

        @block.scalar
        def _(act):
            for f in range(FFN_HALF):
                j = half * FFN_HALF + f
                act.wait_ge(k.unit_used, first + 2 * f + 1)
                if f >= 2:
                    act.wait_ge(out_lo, f - 1)
                act.activation(acc[f % 2], k.bank(2 * (f % 4)), ACT.Identity, scale=k.v("ffn_w", (3 * l + 2) * FFN_TILES + j),
                               bias=k.v("ffn_b", l * FFN_TILES + j)).then_inc(base, 1)
                k.split_hi(act, first + 2 * f + AHEAD)
                act.wait_ge(conv2, f + 1)
                act.activation(th[f % 2], acc[f % 2], ACT.Tanh, scale=0.5).then_inc(tanh_done, 1)
                k.split_hi(act, first + 2 * f + 1 + AHEAD)
                act.wait_ge(finished, f + 1)
                act.activation(out.hi(f), acc[f % 2], ACT.Copy).then_inc(out_hi, 1)

        @block.vector
        def _(dve):
            for f in range(FFN_HALF):
                j = half * FFN_HALF + f
                g, u, a = k.bank(2 * (f % 4)), k.bank(2 * (f % 4) + 1), acc[f % 2]
                dve.wait_ge(base, f + 1)
                dve.scalar_tensor_tensor(out=a[:, 1:T], in0=g[:, 0:T - 1], scalar=k.v("ffn_w", (3 * l + 1) * FFN_TILES + j),
                                         in1=a[:, 1:T], op0=ALU.mult, op1=ALU.add).then_inc(conv1, 1)
                dve.wait_ge(conv1, f + 1)
                dve.scalar_tensor_tensor(out=a[:, 2:T], in0=g[:, 0:T - 2], scalar=k.v("ffn_w", 3 * l * FFN_TILES + j),
                                         in1=a[:, 2:T], op0=ALU.mult, op1=ALU.add).then_inc(conv2, 1)
                k.split_lo(dve, first + 2 * f + AHEAD)
                dve.wait_ge(tanh_done, f + 1)
                dve.scalar_tensor_tensor(out=a, in0=th[f % 2], scalar=1.0, in1=a, op0=ALU.add, op1=ALU.mult).then_inc(left, 1)
                k.split_lo(dve, first + 2 * f + 1 + AHEAD)
                dve.wait_ge(left, f + 1)
                dve.wait_ge(k.unit_used, first + 2 * f + 2)
                dve.scalar_tensor_tensor(out=a, in0=a, scalar=0.5, in1=u, op0=ALU.mult, op1=ALU.mult).then_inc(finished, 1)
                dve.wait_ge(out_hi, f + 1)
                dve.tensor_tensor(out.lo(f), a, out.hi(f).bitcast(F32), ALU.subtract).then_inc(out_lo, 1)



def head_norms(k, l, bias_in, lam_in):
    nc = k.nc
    k.begin()
    loaded, squared, mean_done, root, inverse, cleared, normed, lam_sum, lam_exp, chain = (k.sem() for _ in range(10))
    src = [k.tile(n) for n in range(8)]
    sq = [k.tile(34), k.tile(35)]
    rs = [k.tile(36), k.tile(37)]
    lam_v = k.tile(38)[:, 0:256]
    lam_p = k.tile(39)[:, 0:128]
    lam = k.small[:, 40:44]
    with nc.Block() as block:
        @block.sync
        def _(sp):
            sp.dma_start(lam_v, lam_in).then_inc(loaded, 16)
            with nc.allow_non_contiguous_dma(reason="one Toeplitz tile per row shift"):
                for h in range(4):
                    sp.dma_start(blocks(k.tile(30 + h)), bias_in(h)).then_inc(loaded, 16)
            sp.wait_ge(loaded, 80)
            k.sync_work(sp)

        @block.gpsimd
        def _(pool):
            for h in range(4):
                pool.memset(k.tile(26 + h)[0:64], 0.0).then_inc(cleared, 1)

        @block.scalar
        def _(act):
            def take_root(n):
                act.wait_ge(mean_done, n + 1)
                if n >= 2:
                    act.wait_ge(normed, n - 1)
                act.activation(rs[n % 2], k.bank(n % 2), ACT.Sqrt, bias=k.eps(64e-6 if n < 4 else 1e-6)).then_inc(root, 1)

            for n in range(8):
                if n >= 2:
                    act.wait_ge(mean_done, n - 1)
                act.activation(sq[n % 2], src[n], ACT.Square).then_inc(squared, 1)
                if n >= 1:
                    take_root(n - 1)
            take_root(7)
            act.wait_ge(lam_sum, 2)
            act.activation(lam[:, 0:2], lam[:, 0:2], ACT.Exp).then_inc(lam_exp, 1)

        @block.tensor
        def _(pe):
            for n in range(8):
                pe.wait_ge(squared, n + 1)
                if n >= 2:
                    pe.wait_ge(root, n - 1)
                pe.matmul(k.bank(n % 2), k.c("sum64" if n < 4 else "mean64"), sq[n % 2], start=True, stop=True).then_inc(mean_done, 1)

        @block.vector
        def _(dve):
            ch = Chain(dve, chain)
            dve.wait_ge(loaded, 80)
            lp = lam_v.rearrange("p (a b c) -> p a b c", a=2, b=2)
            ch.then(dve.tensor_tensor(lam_p.rearrange("p (a c) -> p a c", a=2), lp[:, :, 0, :], lp[:, :, 1, :], ALU.mult))
            dve.reduce_sum(lam[:, 0:1], lam_p[:, 0:64], AX_X).then_inc(lam_sum, 1)
            dve.reduce_sum(lam[:, 1:2], lam_p[:, 64:128], AX_X).then_inc(lam_sum, 1)
            for n in range(8):
                dve.wait_ge(root, n + 1)
                dve.reciprocal(rs[n % 2], rs[n % 2]).then_inc(inverse, 1)
                dve.wait_ge(inverse, n + 1)
                if n < 4:
                    dve.scalar_tensor_tensor(out=src[n], in0=src[n], scalar=k.v("da_q_g", l), in1=rs[n % 2],
                                             op0=ALU.mult, op1=ALU.mult).then_inc(normed, 1)
                else:
                    up = slice(64, 128)
                    ch(dve.scalar_tensor_tensor(out=k.tile(26 + n - 4)[up], in0=src[n][up], scalar=k.v("da_k_g", l)[up],
                                                in1=rs[n % 2][up], op0=ALU.mult, op1=ALU.mult))
                    ch.then(dve.scalar_tensor_tensor(out=src[n][0:64], in0=src[n][0:64], scalar=k.v("da_k_g", l)[0:64],
                                                     in1=rs[n % 2][0:64], op0=ALU.mult, op1=ALU.mult))
                    dve.memset(src[n][up], 0.0).then_inc(normed, 1)
            dve.wait_ge(lam_exp, 1)
            ch.then(dve.tensor_tensor(lam[:, 2:3], lam[:, 1:2], lam[:, 0:1], ALU.subtract))
            ch.then(dve.tensor_scalar(lam[:, 3:4], lam[:, 2:3], -LAM_INIT[l], None, ALU.add))
    return lam[:, 3:4]


def tile_norms(k, jobs, work):
    nc = k.nc
    k.begin()
    squared, mean_done, root, tanh_done, chain = (k.sem() for _ in range(5))
    n_jobs = len(jobs)
    sq = [k.tile(work + n) for n in range(n_jobs)]
    th = [k.tile(work + n_jobs + n) for n in range(n_jobs)]
    with nc.Block() as block:
        @block.sync
        def _(sp):
            k.sync_work(sp)

        @block.scalar
        def _(act):
            for n, (o, mean, gain, factor, gate) in enumerate(jobs):
                act.activation(sq[n], o, ACT.Square).then_inc(squared, 1)
            for n in range(n_jobs):
                act.wait_ge(mean_done, n + 1)
                act.activation(sq[n], k.bank(n), ACT.Sqrt, bias=k.eps(1e-6)).then_inc(root, 1)
            for n, (o, mean, gain, factor, gate) in enumerate(jobs):
                if gate is not None:
                    act.activation(th[n], gate, ACT.Tanh, scale=0.5).then_inc(tanh_done, 1)

        @block.tensor
        def _(pe):
            for n, (o, mean, gain, factor, gate) in enumerate(jobs):
                pe.wait_ge(squared, n + 1)
                pe.matmul(k.bank(n), k.c(mean), sq[n], start=True, stop=True).then_inc(mean_done, 1)

        @block.vector
        def _(dve):
            ch = Chain(dve, chain)
            for n, (o, mean, gain, factor, gate) in enumerate(jobs):
                dve.wait_ge(root, n + 1)
                ch.then(dve.reciprocal(sq[n], sq[n]))
                ch.then(dve.scalar_tensor_tensor(out=o, in0=o, scalar=gain, in1=sq[n], op0=ALU.mult, op1=ALU.mult))
                ch.then(dve.tensor_scalar(o, o, factor, None, ALU.mult))
            gated = [n for n in range(n_jobs) if jobs[n][4] is not None]
            for at, n in enumerate(gated):
                o, gate = jobs[n][0], jobs[n][4]
                dve.wait_ge(tanh_done, at + 1)
                ch.then(dve.scalar_tensor_tensor(out=gate, in0=th[n], scalar=1.0, in1=gate, op0=ALU.add, op1=ALU.mult))
                ch.then(dve.scalar_tensor_tensor(out=o, in0=gate, scalar=0.5, in1=o, op0=ALU.mult, op1=ALU.mult))


def turn_tiles(k, tiles, banks):
    turned, copied = k.sem(), k.sem()

    def tensor(pe, t):
        for i in range(TB):
            b = slice(i * P, (i + 1) * P)
            last = pe.transpose(k.bank(banks[t])[:, b], tiles[t][:, b], k.c("ident"))
        last.then_inc(turned, 1)

    def scalar(act, t):
        act.wait_ge(turned, t + 1)
        act.activation(tiles[t], k.bank(banks[t]), ACT.Copy).then_inc(copied, 1)

    w = Work(len(tiles), tensor, scalar)
    w.copied = copied
    return w


def retention(k, q, key, val, work, values_turned):
    scores_done, decayed, out_done, copied = (k.sem() for _ in range(4))
    buf = [k.tile(work + n) for n in range(8)]
    units = [(h, s) for h in range(4) for s in range(TB)]
    U = len(units)
    decay = k.c("decay")

    def tensor(pe, u):
        if u < U:
            h, s = units[u]
            if u >= 4:
                pe.wait_ge(decayed, u - 3)
            pe.matmul(k.bank(2 + u % 4)[:, 0:T - s * P], key[h // 2][HALF[h % 2], s * P:(s + 1) * P],
                      q[h // 2][HALF[h % 2], s * P:T], start=True, stop=True).then_inc(scores_done, 1)
        if u >= 2:
            v = u - 2
            h, s = units[v]
            if v == 0:
                pe.wait_ge(values_turned, 2)
            pe.wait_ge(decayed, v + 1)
            pe.matmul(k.bank(6 + h // 2)[HALF[h % 2], s * P:T], val[h // 2][:, s * P + 64 * (h % 2):s * P + 64 * (h % 2) + 64],
                      buf[v % 8][:, 0:T - s * P], start=(s == 0), stop=(s == TB - 1)).then_inc(out_done, 1)

    def vector(dve, u):
        if u < U:
            h, s = units[u]
            dve.wait_ge(scores_done, u + 1)
            if u >= 8:
                dve.wait_ge(out_done, u - 7)
            dve.tensor_tensor(buf[u % 8][:, 0:T - s * P], decay[:, h * T:h * T + T - s * P],
                              k.bank(2 + u % 4)[:, 0:T - s * P], ALU.mult).then_inc(decayed, 1)

    def scalar(act, u):
        if u in (9, U + 1):
            j = 0 if u == 9 else 1
            act.wait_ge(out_done, 8 * (j + 1))
            act.activation(q[j], k.bank(6 + j), ACT.Copy).then_inc(copied, 1)

    return Work(U + 2, tensor, scalar, vector)


def short_conv(k, l, b, c, x):
    chain, ready, tapped, done = (k.sem() for _ in range(4))

    def gpsimd(pool, t):
        if t < 2:
            pool.tensor_tensor(c[t], c[t], x[t], ALU.mult).then_inc(ready, 1)
        elif t < 4:
            j = t - 2
            pool.wait_ge(tapped, j + 1)
            pool.tensor_tensor(b[j], b[j], x[j], ALU.mult).then_inc(done, 1)

    chains = []

    def vector(dve, t):
        if t == 0:
            chains.append(Chain(dve, chain))
        if t in (1, 2):
            ch, j = chains[0], t - 1
            dve.wait_ge(ready, j + 1)
            ch.then(dve.tensor_scalar(x[j], c[j], k.v("conv_w", 6 * l + 4 + j), k.v("conv_b", 2 * l + j), ALU.mult, ALU.add))
            ch.then(dve.scalar_tensor_tensor(out=x[j][:, 1:T], in0=c[j][:, 0:T - 1], scalar=k.v("conv_w", 6 * l + 2 + j),
                                             in1=x[j][:, 1:T], op0=ALU.mult, op1=ALU.add))
            dve.scalar_tensor_tensor(out=x[j][:, 2:T], in0=c[j][:, 0:T - 2], scalar=k.v("conv_w", 6 * l + j),
                                     in1=x[j][:, 2:T], op0=ALU.mult, op1=ALU.add).then_inc(tapped, 1)

    return Work(4, vector=vector, gpsimd=gpsimd)


def load_constants(k, held, const_in):
    nc = k.nc
    k.begin()
    loaded = k.sem()
    with nc.Block() as block:
        @block.sync
        def _(sp):
            sp.dma_start(held[:, :], const_in[:, CONST_W - CONST_PARTS[2][1]:CONST_W]).then_inc(loaded, 16)
            sp.wait_ge(loaded, 16)
            k.sync_work(sp)


def gated_branches(k, l, first, h, src, branch, out, work):
    nc = k.nc
    k.begin()
    src_hi, src_lo, branch_done, tanh_done, chain, read = (k.sem() for _ in range(6))
    gt = k.tile(work, 3)
    part = [k.tile(work + 3 + n) for n in range(3)]
    ks = [range(0, 4), range(4, 6), range(6, 8)]
    with nc.Block() as block:
        @block.sync
        def _(sp):
            k.sync_work(sp, first + 4 * DT)

        @block.tensor
        def _(pe):
            for d in range(DT):
                n = first + 4 * d
                for b in range(3):
                    if d >= 1:
                        pe.wait_ge(tanh_done, 3 * (d - 1) + b + 1)
                    k.product(pe, k.bank(b), n + b, h)
                if d >= 1:
                    pe.wait_ge(read, 3 * d)
                pe.wait_ge(k.lo_ready, n + 4)
                if d == 0:
                    pe.wait_ge(src_lo, DT)
                u = (n + 3) % AHEAD
                for b in range(3):
                    for i in ks[b]:
                        w, end = slice(i * P, (i + 1) * P), i == ks[b][-1]
                        pe.matmul(k.bank(3 + b), k.w_hi[:, u, w], branch.hi(i), start=(i == ks[b][0]), stop=False)
                        pe.matmul(k.bank(3 + b), k.w_hi[:, u, w], branch.lo(i), start=False, stop=False)
                        last = pe.matmul(k.bank(3 + b), k.w_lo[:, u, w], branch.hi(i), start=False, stop=end)
                last.then_inc(k.unit_used, 1)

        @block.scalar
        def _(act):
            split_tiles_hi(act, src, branch, src_hi)
            for d in range(DT):
                n = first + 4 * d
                if d >= 1:
                    act.wait_ge(read, 3 * d)
                for b in range(3):
                    act.wait_ge(k.unit_used, n + b + 1)
                    act.activation(gt[:, b * T:(b + 1) * T], k.bank(b), ACT.Tanh, scale=0.5,
                                   bias=k.v("b_gate", 24 * l + 8 * b + d)).then_inc(tanh_done, 1)
                    k.split_hi(act, n + b + AHEAD)
                k.split_hi(act, n + 3 + AHEAD)

        @block.vector
        def _(dve):
            ch = Chain(dve, chain)
            split_tiles_lo(dve, src, branch, src_hi, src_lo)
            for d in range(DT):
                n = first + 4 * d
                for b in range(3):
                    k.split_lo(dve, n + b + AHEAD)
                dve.wait_ge(tanh_done, 3 * (d + 1))
                ch.then(dve.tensor_scalar(gt, gt, 0.5, 0.5, ALU.mult, ALU.add))
                dve.wait_ge(k.unit_used, n + 4)
                for b in range(3):
                    dve.tensor_tensor(part[b], gt[:, b * T:(b + 1) * T], k.bank(3 + b), ALU.mult).then_inc(read, 1)
                k.split_lo(dve, n + 3 + AHEAD)
                dve.wait_ge(read, 3 * (d + 1))
                ch.then(dve.tensor_tensor(part[0], part[0], part[1], ALU.add))
                ch.then(dve.tensor_tensor(out[d], part[0], part[2], ALU.add))


def epilogue(k, out):
    nc = k.nc
    k.begin()
    with nc.Block() as block:
        @block.sync
        def _(sp):
            sp.dma_start(out, k.xT[:, :, :]).then_inc(k.out_stored, 16)
            sp.wait_ge(k.out_stored, 16)


def program(nc, wts, x_in, const_in, mask_in, vec_in, onehot_in, relb_in, lora_in, lam_in, out, bias_dram):
    with ExitStack() as ctx:
        k = Core(nc, ctx, wts)
        first_block = ExitStack()
        first_const = k.open_constants(first_block, 1)
        with ExitStack() as phase:
            prologue(k, phase, first_const, x_in, const_in, mask_in, vec_in, onehot_in, relb_in, bias_dram)
        x = [k.x(d) for d in range(DT)]
        n = 0
        tiles = lambda a, b: [k.tile(t) for t in range(a, b)]

        def feed_forward(l, n):
            with ExitStack() as phase:
                k.open_part(phase, LOW, 3)
                xs, hidden = k.halves(phase, DT), k.halves(phase, MLP_HALF)
                for half in range(2):
                    squared_relu(k, n, x if half == 0 else None, xs, hidden)
                    n += MLP_HALF
                    project_residual(k, n, None, hidden, ALPHA if half == 0 else 1.0, units=2)
                    n += 2 * DT
                layer_norm(k, "ln2_g", "ln2_b", l, 0)
            return n

        with ExitStack() as phase:
            k.open_part(phase, LOW)
            k.open_part(phase, MID)
            k.open_part(phase, EXTRA)
            with ExitStack() as inner:
                k.begin()
                place = [k.tile(b + h) for h in range(4) for b in (12, 16, 20)]
                place += [k.tile(t) for t in list(range(12)) + [24, 25, 26]]
                proj = project(k, n, x, k.halves(inner, DT), place, turned=[t for t in range(12) if t % 3 < 2],
                               banks=(0, 1, 2), turn_banks=(3, 4))
                causal = lambda i, j: [(k.m("ident"), k.m("causal"))] if i == j else []

                def head_ready(pe, h):
                    pe.wait_ge(proj.roped, 2 * h + 2)
                    pe.wait_ge(proj.copied, 3 * h + 3)

                moba = attention(k, [([(k.tile(12 + h), k.tile(16 + h), lambda i: 0, causal)], k.tile(20 + h), k.tile(12 + h))
                                     for h in range(4)], P ** -0.5, [k.tile(40)], k.tile(41), (5, 6, 7), ready=head_ready)
                schedule = behind(proj, moba, lambda u: 3 * (u // TB) + 5 + min(u % TB, 2))
                run(k, schedule)
                n += 27
            with ExitStack() as inner:
                k.open_part(inner, EXT)
                k.begin()
                run(k, in_turn([rwkv_shift(k)]))
                rwkv_loras(k, lora_in)
                for c in range(2):
                    pairs = [Pair(k, 2 * c, 31, 0, 0), Pair(k, 2 * c + 1, 47, 4, 20)]
                    for step in (Pair.scale, Pair.matrices, Pair.invert, Pair.apply_inverse, Pair.chunks, Pair.outputs):
                        k.begin()
                        run(k, in_turn([step(p) for p in pairs]))
            with ExitStack() as inner:
                project_residual(k, n, tiles(4, 8) + tiles(12, 16), k.halves(inner, DT), ALPHA)
                n += DT
            layer_norm(k, "ln1_g", "ln1_b", 0, 0)
        n = feed_forward(0, n)

        def near(i, j):
            return [(k.m("ident"), k.m("causal" if i == j else "band"))]

        def every(name):
            return lambda i, j: [(k.m("ident"), k.m(name + "causal" if i == j else name))]

        zero, band = lambda i: 0, lambda i: max(i - 1, 0) * P
        with ExitStack() as phase:
            k.open_part(phase, LOW)
            k.open_part(phase, MID)
            with ExitStack() as inner:
                k.begin()
                sets = [[k.tile(8 + 5 * c + b) for b in range(5)] for c in range(3)]
                seen = []

                def set_free(act, t):
                    h = t // 5
                    if h >= 3 and t % 5 == 0:
                        act.wait_ge(seen[0].out_done, TB * (h - 2))

                proj = project(k, n, x, k.halves(inner, DT), [sets[h % 3][b] for h in range(8) for b in range(5)],
                               turned=[t for t in range(40) if t % 5 < 4], banks=(0, 1), turn_banks=(2,), free=set_free)

                def head_ready(pe, h):
                    pe.wait_ge(proj.roped, 4 * h + 4)
                    pe.wait_ge(proj.copied, 5 * h + 5)

                heads = []
                for h in range(8):
                    q0, q1, q2, key, val = sets[h % 3]
                    heads.append(([(q1, key, zero, every("four")), (q2, key, zero, every("sixteen")), (q0, key, band, near)],
                                  val, k.tile(h)))
                dilated = attention(k, heads, P ** -0.5, [k.tile(MID + g) for g in range(3)], k.tile(MID + 3), (3, 4, 5, 6, 7),
                                    ready=head_ready)
                seen.append(dilated)
                run(k, behind(proj, dilated, lambda u: 5 * (u // TB) + 7 + u % TB))
                n += 40
            with ExitStack() as inner:
                project_residual(k, n, tiles(0, 8), k.halves(inner, DT), ALPHA)
                n += DT
            layer_norm(k, "ln1_g", "ln1_b", 1, 0)
        n = feed_forward(1, n)
        first_block.close()

        second_const = k.open_constants(ctx, 2)
        load_constants(k, second_const, const_in)
        for l in range(DEPTH):
            with ExitStack() as phase:
                k.open_part(phase, LOW)
                with ExitStack() as mixing:
                    h = k.halves(mixing, DT)
                    with ExitStack() as inner:
                        k.open_part(inner, MID)
                        rms_norm(k, "norm_mix_g", l, h, 0)
                        k.begin()
                        run(k, in_turn([project(k, n, None, h, tiles(0, 12))]))

                        def bias_in(head):
                            return bass.AP(bias_dram.tensor, head * (T + P), [[1, P], [P, TB], [1, P]])

                        nlam = head_norms(k, l, bias_in, lam_in[l])

                        def relative(head):
                            return lambda i, j: ([(k.tile(30 + head)[:, (i - j) * P:(i - j + 1) * P], k.c("flip"))]
                                                 + ([(k.m("ident"), k.m("causal"))] if i == j else []))

                        k.begin()
                        rest = project(k, n + 12, None, h, tiles(12, 26), turned=range(4), cos="cos2", sin="sin2", turn="turn2",
                                       banks=(0, 1, 2), turn_banks=(3,))
                        diff = attention(k, [([(k.tile(a), k.tile(4 + a), zero, relative(a)),
                                               (k.tile(a), k.tile(26 + a), zero, relative(a))], k.tile(8 + a), k.tile(a))
                                             for a in range(4)], 1.0, [k.tile(34), k.tile(35)], k.tile(36), (4, 5, 6, 7),
                                         difference=nlam)
                        run(k, behind(rest, diff, lambda u: u - 1))
                        n += 26
                        k.begin()
                        turn = turn_tiles(k, tiles(16, 18), (0, 1))
                        run(k, in_turn([turn, short_conv(k, l, tiles(20, 22), tiles(22, 24), tiles(24, 26)),
                                        retention(k, tiles(12, 14), tiles(14, 16), tiles(16, 18), 26, turn.copied)]))
                        tile_norms(k, [(k.tile(a), "mean128", k.v("subln_g", l), 1.0 - LAM_INIT[l], None) for a in range(4)]
                                   + [(k.tile(12 + a), "mean64", k.v("ret_g", l), 1.0, k.tile(18 + a)) for a in range(2)], 26)
                    gated_branches(k, l, n, h, tiles(0, 4) + tiles(12, 14) + tiles(20, 22), k.halves(mixing, DT),
                                   tiles(4, 12), 14)
                    n += 4 * DT
                with ExitStack() as inner:
                    project_residual(k, n, tiles(4, 12), k.halves(inner, DT), 1.0)
                    n += DT
            with ExitStack() as phase:
                k.open_part(phase, LOW, 4)
                h, act = k.halves(phase, DT), k.halves(phase, FFN_HALF)
                rms_norm(k, "norm_ffn_g", l, h, 0)
                for half in range(2):
                    gated_ffn(k, l, half, n, h, act)
                    n += FFN_TILES
                    project_residual(k, n, None, act, 1.0, units=2)
                    n += 2 * DT
        assert n == len(UNITS)
        epilogue(k, out)



def pack_weights(i):
    def unit(w):
        if w.shape[1] < P:
            w = np.concatenate([w, np.zeros((w.shape[0], P - w.shape[1]), w.dtype)], 1)
        return w.reshape(-1, P, P).transpose(1, 0, 2).reshape(P, -1)

    def split(w):
        return [unit(w[:, c:c + P]) for c in range(0, w.shape[1], P)]

    def mlp(w1, w2):
        half = MLP_HALF * P
        return [u for h in range(2) for u in split(w1[:, h * half:(h + 1) * half]) + split(w2[h * half:(h + 1) * half])]

    ends = AB_TILES[1:15] + [1824] + AB_TILES[16:] + [i["ab_w_in"].shape[2]]
    ab = [unit(i["ab_w_in"][0][:, a:b]) for a, b in zip(AB_TILES, ends)]
    g = [ab[15 + 4 * part + h] for h in range(4) for part in range(3)] + ab[0:15]
    g += split(i["ab_w_out"][0]) + mlp(i["mlp_w1"][0], i["mlp_w2"][0])
    c = split(i["c_w_in"][0])
    g += [c[8 * part + h] for h in range(8) for part in range(5)] + split(i["c_w_out"][0]) + mlp(i["mlp_w1"][1], i["mlp_w2"][1])
    for l in range(DEPTH):
        w = i["w_in_2"][l]
        branch = np.concatenate([i["w_branch_da_2"][l], i["w_branch_ret_2"][l], i["w_branch_sc_2"][l]], 0)
        g += split(w[:, 0:3328])
        for d in range(DT):
            g += [unit(w[:, 3328 + b * D + d * P:3328 + b * D + (d + 1) * P]) for b in range(3)]
            g.append(unit(branch[:, d * P:(d + 1) * P]))
        g += split(i["w_out_2"][l])
        f, o = i["w_ffn_in_2"][l], i["w_ffn_out_2"][l]
        inner = FFN_TILES * P
        for h in range(2):
            rows = slice(h * FFN_HALF * P, (h + 1) * FFN_HALF * P)
            g += [unit(f[:, s + c * P:s + (c + 1) * P]) for c in range(h * FFN_HALF, (h + 1) * FFN_HALF) for s in (0, inner)]
            g += split(o[rows])
    return np.concatenate(g, 1)


def pack_vectors(i):
    def cols(v):
        v = np.asarray(v).reshape(-1)
        pad = -len(v) % P
        return np.concatenate([v, np.zeros(pad, v.dtype)]).reshape(-1, P).T

    def twice(v):
        return np.concatenate([v, v], -1)

    def dw(w):
        return w

    parts = {
        "w0": i["ab_w0"], "a0": i["ab_a0"], "b_gate": i["b_gate_2"], "mix": i["ab_shift_mix"], "k_k": i["ab_k_k"],
        "k_a": i["ab_k_a"], "r_k": i["ab_r_k"], "lnx_g": i["ab_lnx_g"], "lnx_b": i["ab_lnx_b"],
        "ln1_g": i["ln1_g"], "ln1_b": i["ln1_b"], "ln2_g": i["ln2_g"], "ln2_b": i["ln2_b"],
        "norm_mix_g": i["norm_mix_g_2"], "norm_ffn_g": i["norm_ffn_g_2"],
        "da_q_g": twice(i["da_q_norm_g_2"]), "da_k_g": twice(i["da_k_norm_g_2"]), "subln_g": i["da_subln_g_2"],
        "ret_g": twice(i["ret_norm_g_2"]), "conv_w": dw(i["sc_conv_w_2"]), "conv_b": i["sc_conv_b_2"],
        "ffn_w": dw(i["ffn_conv_w_2"]), "ffn_b": i["ffn_conv_b_2"],
    }
    out = [cols(parts[name]) for name, _ in vector_entries()]
    return np.concatenate(out, 1)


def build(nc, shapes):
    ap = {n: nc.dram_tensor("in_" + n, s, mybir.dt.from_np(np.dtype(d)), kind="ExternalInput").ap() for n, (s, d) in shapes.items()}
    out = nc.dram_tensor("out", (P, DT, T), F32, kind="ExternalOutput").ap()
    bias_dram = nc.dram_tensor("bias_by_distance", (4, T + P), F32, kind="Internal").ap()
    program(nc, ap["weights"], ap["x"], ap["const"], ap["mask"], ap["vectors"], ap["onehot"], ap["rel_bias"],
            ap["lora"], [ap["lam0"], ap["lam1"]], out, bias_dram)




def kernel(**inputs):
    import concourse.bacc as bacc
    from concourse.bass_utils import run_bass_kernel_spmd as run

    i = {n: np.asarray(a) for n, a in inputs.items()}
    const, mask, onehot = constants()
    z = np.zeros((64, 512), np.float32)
    gup = i["ab_g_up"][0]
    lora = np.concatenate([np.concatenate([i["ab_w_up"][0], z], 0), np.concatenate([z, i["ab_a_up"][0]], 0),
                           gup[0:P], np.concatenate([gup[P:], np.zeros((2 * P - gup.shape[0], 512), np.float32)], 0)], 1)
    arrays = {
        "weights": pack_weights(i),
        "x": np.ascontiguousarray(i["x"][0].T.reshape(DT, P, T).transpose(1, 0, 2)),
        "const": const, "mask": mask, "vectors": np.ascontiguousarray(pack_vectors(i)), "onehot": onehot,
        "rel_bias": np.ascontiguousarray(i["rel_bias_2"]), "lora": lora,
        "lam0": np.ascontiguousarray(np.broadcast_to(i["da_lambda_2"][0].reshape(1, 256), (P, 256))),
        "lam1": np.ascontiguousarray(np.broadcast_to(i["da_lambda_2"][1].reshape(1, 256), (P, 256))),
    }
    nc = bacc.Bacc("TRN2", target_bir_lowering=False, num_devices=1)
    build(nc, {n: (a.shape, a.dtype) for n, a in arrays.items()})
    got = run(nc, [{"in_" + n: a for n, a in arrays.items()}], core_ids=[0]).results[0]["out"]
    return np.ascontiguousarray(got.transpose(1, 0, 2).reshape(D, T).T).reshape(1, T, D)
```

```python
from contextlib import ExitStack

import numpy as np

import concourse.bass as bass
from concourse import mybir

F32 = mybir.dt.float32
F32R = mybir.dt.float32r
BF16 = mybir.dt.bfloat16
ACT = mybir.ActivationFunctionType
ALU = mybir.AluOpType
AX_X = mybir.AxisListType.X

P = 128
T = 512
TB = T // P
D = 1024
DT = D // P
DEPTH = 2
ALPHA = (2 * DEPTH) ** 0.25
ROPE_THETA, ROPE_THETA_2 = 500000.0, 10000.0
MLP_TILES = 4 * D // P
FFN_TILES = 2816 // P
CHUNK = 64
NCHUNK = T // CHUNK
LEVELS = 6
UNIT = DT * P
SLOT = 2 * UNIT
RING = 3
AHEAD = 3
LOW, MID, EXTRA, EXT = 0, 24, 40, 47
SEMS = 74
PART_TILES = {LOW: 24, MID: 16, EXTRA: 7, EXT: 16}
NEG = -1.0e30
LAM_INIT = [0.8 - 0.6 * float(np.exp(-0.3 * l)) for l in range(DEPTH)]



def layout(entries):
    at, out = 0, {}
    for name, width in entries:
        out[name] = (at, width)
        at += width
    return out, at


COMMON = [("ident", P), ("mean", P), ("mean64", P), ("sum64", P), ("eps", 4)]
FIRST = [("cos", T), ("sin", T), ("reset", T), ("pair", P), ("low0", P)] + \
    [(f"up{l}", P) for l in range(LEVELS)] + [("up", P), ("upincl", P)]
SECOND = [("cos2", T), ("sin2", T), ("decay", 4 * T), ("mean128", P), ("flip", P)]
CONST_PARTS = [layout(part) for part in (COMMON, FIRST, SECOND)]
CONSTS, CONST_W = layout(COMMON + FIRST + SECOND)
MASKS = ["ident", "causal", "band", "four", "fourcausal", "sixteen", "sixteencausal"]
EPS = [1e-5, 1e-6, 64e-6, 64e-5]


def constants():
    c = np.zeros((P, CONST_W), np.float32)

    def put(name, value):
        at, width = CONSTS[name]
        c[:, at:at + width] = value

    pos = np.arange(T, dtype=np.float32)

    def rope(cos, sin, theta, half, period):
        inv = np.float32(theta) ** (-np.arange(half, dtype=np.float32) / np.float32(half))
        ang = pos[None, :] * inv[:, None].astype(np.float32)
        co, si = np.ones((P, T)), np.zeros((P, T))
        for b in range(0, P, period):
            co[b:b + half] = co[b + 32:b + 32 + half] = np.cos(ang)
            si[b:b + half], si[b + 32:b + 32 + half] = np.sin(ang), -np.sin(ang)
        put(cos, co)
        put(sin, si)

    rope("cos", "sin", ROPE_THETA, 16, P)
    rope("cos2", "sin2", ROPE_THETA_2, 32, 64)
    lg = np.log(1.0 - 2.0 ** (-5.0 - np.arange(4)))
    n = np.arange(T)[None, :] - np.arange(P)[:, None]
    put("decay", np.concatenate([np.where(n >= 0, np.exp(g * np.maximum(n, 0)), 0.0) / 8.0 for g in lg], 1))
    put("reset", np.broadcast_to((np.arange(T) % CHUNK != 0).astype(np.float32), (P, T)))
    a, b = np.arange(P)[:, None], np.arange(P)[None, :]
    block = a // 64 == b // 64
    put("ident", a == b)
    put("mean", 1.0 / D)
    put("mean128", 1.0 / P)
    put("mean64", block / 64.0)
    put("sum64", block)
    put("flip", a + b == P - 1)
    put("pair", block)
    for l in range(LEVELS):
        w = 1 << l
        low = (a // (2 * w) == b // (2 * w)) & (a % (2 * w) >= w) & (b % (2 * w) < w)
        if l == 0:
            put("low0", low)
        put(f"up{l}", low.T)
    put("up", block & (a < b))
    put("upincl", block & (a <= b))
    put("eps", np.broadcast_to(np.array(EPS, np.float32), (P, len(EPS))))
    d = a - b
    masks = {"ident": (d == 0) * 1.0, "causal": np.where(d >= 0, 0, NEG), "band": np.where(d <= 0, 0, NEG),
             "four": np.where(d % 4 == 0, 0, NEG), "fourcausal": np.where((d % 4 == 0) & (d >= 0), 0, NEG),
             "sixteen": np.where(d % 16 == 0, 0, NEG), "sixteencausal": np.where((d % 16 == 0) & (d >= 0), 0, NEG)}
    m = np.concatenate([masks[k] for k in MASKS], 1).astype(np.float32)
    dist = np.maximum(np.arange(T + P) - (P - 1), 0)
    nf = np.maximum(dist, 1).astype(np.float32)
    large = 16 + (np.log(nf / np.float32(16)) / np.float32(np.log(8.0)) * np.float32(16)).astype(np.int32)
    bucket = np.where(dist < 16, dist, np.minimum(large, 31))
    onehot = (bucket[None, :] == np.arange(32)[:, None]).astype(np.float32)
    return c, m, onehot



def vector_entries():
    e = [("w0", 4), ("a0", 4), ("b_gate", 24 * DEPTH)]
    e += [("mix", 15), ("k_k", 4), ("k_a", 4), ("r_k", 4), ("lnx_g", 4), ("lnx_b", 4)]
    e += [(n, DT * DEPTH) for n in ("ln1_g", "ln1_b", "ln2_g", "ln2_b", "norm_mix_g", "norm_ffn_g")]
    e += [(n, DEPTH) for n in ("da_q_g", "da_k_g", "subln_g", "ret_g")]
    e += [("conv_w", 6 * DEPTH), ("conv_b", 2 * DEPTH), ("ffn_w", 3 * FFN_TILES * DEPTH), ("ffn_b", FFN_TILES * DEPTH)]
    return e


VECTORS, VECTOR_W = layout(vector_entries())
HALVED = 8 + 24 * DEPTH

AB_TILES = [c * P for c in range(14)] + [1792] + [1824 + c * P for c in range(12)]
MOBA = [[15 + 4 * part + h for part in range(3)] for h in range(4)]
RWKV = [[4 * part + j for part in range(3)] for j in range(4)]
AB_ORDER = [12, 13, 14] + MOBA[0] + RWKV[0] + MOBA[1] + RWKV[1] + MOBA[2] + RWKV[2] + RWKV[3] + MOBA[3]
MIX_ORDER = [18, 19, 20, 12, 21, 14, 22, 13, 23, 15, 24, 16, 25, 17]
MLP_HALF, FFN_HALF = MLP_TILES // 2, FFN_TILES // 2
FFN_PARTS = [6, 5]


def unit_parts():
    mlp = ([8] * MLP_HALF + [8, 8] * DT) * 2
    u = [8] * (27 + DT) + mlp + [8] * (40 + DT) + mlp
    for _ in range(DEPTH):
        u += [8] * (26 + 4 * DT + DT) + ([8] * FFN_TILES + FFN_PARTS * DT) * 2
    return u


UNITS = unit_parts()


def group_units():
    groups, n = [], 0
    while n < len(UNITS):
        end = n + 1
        while end < len(UNITS) and sum(UNITS[n:end + 1]) * P <= SLOT and end - n < 2:
            end += 1
        groups.append((n, end))
        n = end
    return groups


GROUPS = group_units()
GROUP_OF = [g for g, (a, b) in enumerate(GROUPS) for _ in range(a, b)]
UNIT_AT = [P * sum(UNITS[:n]) for n in range(len(UNITS) + 1)]


class Halves:

    def __init__(self, hi, lo):
        self.hi_t, self.lo_t = hi, lo

    def hi(self, n):
        return self.hi_t[:, n, :]

    def lo(self, n):
        return self.lo_t[:, n, :]


class Core:

    def __init__(self, nc, ctx, wts):
        self.nc = nc
        self.names = 0
        self.ring = ctx.enter_context(nc.sbuf_tensor("ring", [P, RING, SLOT], F32))
        self.w_hi = ctx.enter_context(nc.sbuf_tensor("w_hi", [P, AHEAD, UNIT], F32R))
        self.w_lo = ctx.enter_context(nc.sbuf_tensor("w_lo", [P, AHEAD, UNIT], F32R))
        self.xT = ctx.enter_context(nc.sbuf_tensor("xT", [P, DT, T], F32))
        self.consts = {}
        self.common = self.open_constants(ctx, 0)
        self.mask = ctx.enter_context(nc.sbuf_tensor("mask", [P, len(MASKS) * P], BF16))
        self.vec = ctx.enter_context(nc.sbuf_tensor("vec", [P, VECTOR_W], F32))
        self.small = ctx.enter_context(nc.sbuf_tensor("small", [P, 144], F32))
        self.psum = ctx.enter_context(nc.psum_tensor("psum", [P, 8, T], F32))
        sem = lambda name: ctx.enter_context(nc.semaphore(name))
        self.slot_filled = [sem(f"slot_filled{i}") for i in range(RING)]
        self.hi_ready, self.lo_ready, self.unit_used = sem("hi_ready"), sem("lo_ready"), sem("unit_used")
        self.out_stored = sem("out_stored")
        self.pools = [[sem(f"stage{p}_{i}") for i in range(SEMS)] for p in range(2)]
        self.parts = {}
        self.stage = 0
        self.next_sem = 0
        self.next_group = 0
        self.wts = wts

    def space(self, stack, tiles, dtype=F32):
        self.names += 1
        return stack.enter_context(self.nc.sbuf_tensor(f"space{self.names}", [P, tiles, T], dtype))

    def halves(self, stack, tiles):
        return Halves(self.space(stack, tiles, F32R), self.space(stack, tiles, F32R))

    def open_constants(self, stack, part):
        entries, width = CONST_PARTS[part]
        held = stack.enter_context(self.nc.sbuf_tensor(f"constants{part}", [P, width], F32))
        self.consts.update({name: held[:, at:at + w] for name, (at, w) in entries.items()})
        return held

    def open_part(self, stack, first, tiles=None):
        tiles = tiles or PART_TILES[first]
        for other in [f for f in self.parts if first <= f < first + tiles or f <= first < f + self.parts[f][1]]:
            del self.parts[other]
        self.parts[first] = (self.space(stack, tiles), tiles)

    def x(self, d):
        return self.xT[:, d, :]

    def tile(self, n, count=1):
        first = max(f for f in self.parts if f <= n)
        part, tiles = self.parts[first]
        assert n + count <= first + tiles, (n, count)
        return part[:, n - first:n - first + count, :].rearrange("p a t -> p (a t)")

    def bank(self, b):
        return self.psum[:, b, :]

    def c(self, name):
        return self.consts[name]

    def m(self, name):
        n = MASKS.index(name)
        return self.mask[:, n * P:(n + 1) * P]

    def v(self, name, j):
        at, width = VECTORS[name]
        assert j < width
        return self.vec[:, at + j:at + j + 1]

    def eps(self, value):
        at = EPS.index(value)
        return self.c("eps")[:, at:at + 1]

    def begin(self):
        self.stage += 1
        self.next_sem = 0

    def sem(self):
        self.next_sem += 1
        return self.pools[self.stage % 2][self.next_sem - 1]

    def fill(self, sp, stop):
        while self.next_group < len(GROUPS):
            g = self.next_group
            if g >= RING:
                split = GROUPS[g - RING][1]
                if split > stop:
                    break
                sp.wait_ge(self.lo_ready, split)
            a, b = UNIT_AT[GROUPS[g][0]], UNIT_AT[GROUPS[g][1]]
            sp.dma_start(self.ring[:, g % RING, 0:b - a], self.wts[:, a:b]).then_inc(self.slot_filled[g % RING], 16)
            self.next_group += 1

    def sync_work(self, sp, end=None):
        for s in self.pools[(self.stage + 1) % 2]:
            sp.sem_clear(s)
        if end is not None:
            self.fill(sp, end + AHEAD)

    def raw(self, n):
        g = GROUP_OF[n]
        at = UNIT_AT[n] - UNIT_AT[GROUPS[g][0]]
        return self.ring[:, g % RING, at:at + UNITS[n] * P]

    def split_hi(self, act, n):
        if n >= len(UNITS):
            return
        g = GROUP_OF[n]
        act.wait_ge(self.slot_filled[g % RING], 16 * (g // RING + 1))
        if n >= AHEAD:
            act.wait_ge(self.unit_used, n - AHEAD + 1)
        act.activation(self.w_hi[:, n % AHEAD, 0:UNITS[n] * P], self.raw(n), ACT.Copy).then_inc(self.hi_ready, 1)

    def split_lo(self, dve, n):
        if n >= len(UNITS):
            return
        w = slice(0, UNITS[n] * P)
        dve.wait_ge(self.hi_ready, n + 1)
        dve.tensor_tensor(self.w_lo[:, n % AHEAD, w], self.raw(n), self.w_hi[:, n % AHEAD, w].bitcast(F32),
                          ALU.subtract).then_inc(self.lo_ready, 1)

    def product(self, pe, out, n, rhs, first=0, units=1, rhs_ready=None, part=None):
        at, total = 0, sum(UNITS[n:n + units])
        for u in range(n, n + units):
            pe.wait_ge(self.lo_ready, u + 1)
            last = None
            for i in range(UNITS[u]):
                if part is not None and at not in part:
                    at += 1
                    continue
                w = slice(i * P, (i + 1) * P)
                hi, lo = self.w_hi[:, u % AHEAD, w], self.w_lo[:, u % AHEAD, w]
                if rhs_ready is not None:
                    pe.wait_ge(rhs_ready, at + 1)
                pe.matmul(out, hi, rhs.hi(first + at), start=(at == 0), stop=False)
                pe.matmul(out, hi, rhs.lo(first + at), start=False, stop=False)
                last = pe.matmul(out, lo, rhs.hi(first + at), start=False, stop=(at == total - 1))
                at += 1
            if part is None or at - 1 in part:
                last.then_inc(self.unit_used, 1)


class Chain:

    def __init__(self, eng, sem):
        self.eng, self.sem, self.n = eng, sem, 0

    def __call__(self, ins):
        ins.then_inc(self.sem, 1)
        self.n += 1
        return self.n

    def sync(self):
        self.eng.wait_ge(self.sem, self.n)

    def then(self, ins):
        self(ins)
        self.sync()


class Work:

    def __init__(self, ticks, tensor=None, scalar=None, vector=None, gpsimd=None, end=None):
        self.ticks, self.tensor, self.scalar, self.vector, self.gpsimd, self.end = ticks, tensor, scalar, vector, gpsimd, end


def behind(lead, followers):
    out, at = [], [0] * len(followers)
    for t in range(lead.ticks):
        out.append((lead, t))
        for n, (work, after) in enumerate(followers):
            while at[n] < work.ticks and after(at[n]) <= t:
                out.append((work, at[n]))
                at[n] += 1
    for n, (work, after) in enumerate(followers):
        out += [(work, u) for u in range(at[n], work.ticks)]
    return out


def braid(first, second):
    out = []
    for t in range(max(len(first), len(second))):
        out += first[t:t + 1] + second[t:t + 1]
    return out


def ticks(work):
    return [(work, t) for t in range(work.ticks)]


def run(k, schedule, loads=None):
    ends = [w.end for w, _ in schedule if w.end is not None]
    with k.nc.Block() as block:
        @block.sync
        def _(sp):
            if loads is not None:
                loads(sp)
            k.sync_work(sp, max(ends) if ends else None)

        @block.tensor
        def _(pe):
            for w, t in schedule:
                if w.tensor:
                    w.tensor(pe, t)

        @block.scalar
        def _(act):
            for w, t in schedule:
                if w.scalar:
                    w.scalar(act, t)

        @block.vector
        def _(dve):
            for w, t in schedule:
                if w.vector:
                    w.vector(dve, t)

        @block.gpsimd
        def _(pool):
            for w, t in schedule:
                if w.gpsimd:
                    w.gpsimd(pool, t)



def prologue(k, stack, first_const, x_in, const_in, mask_in, vec_in, onehot_in, relb_in, bias_dram):
    nc = k.nc
    loaded, halved, bias_done, bias_copied, stored, oh_loaded = (k.sem() for _ in range(6))
    k.open_part(stack, 0, 6)
    onehot = k.tile(0, 2)[0:32, 0:T + P]
    relb = k.tile(0, 2)[0:32, T + P:T + P + 4]
    row = k.tile(2, 2)[0:4, 0:T + P]
    masks = k.tile(4, 2)[:, 0:len(MASKS) * P]
    with nc.Block() as block:
        @block.sync
        def _(sp):
            sp.dma_start(k.xT[:, :, :], x_in).then_inc(loaded, 16)
            sp.dma_start(k.vec[:, :], vec_in).then_inc(loaded, 16)
            sp.dma_start(masks, mask_in).then_inc(loaded, 16)
            sp.dma_start(onehot, onehot_in).then_inc(oh_loaded, 16)
            sp.dma_start(relb, relb_in).then_inc(oh_loaded, 16)
            k.fill(sp, 0)
            a = CONST_PARTS[0][1]
            sp.dma_start(k.common[:, :], const_in[:, 0:a]).then_inc(loaded, 16)
            sp.dma_start(first_const[:, :], const_in[:, a:a + CONST_PARTS[1][1]]).then_inc(loaded, 16)
            sp.wait_ge(bias_copied, 2)
            sp.dma_start(bias_dram, row).then_inc(stored, 16)
            sp.wait_ge(stored, 16)
            sp.wait_ge(loaded, 80)

        @block.vector
        def _(dve):
            dve.wait_ge(loaded, 80)
            dve.tensor_scalar(k.vec[:, 0:HALVED], k.vec[:, 0:HALVED], 0.5, None, ALU.mult).then_inc(halved, 1)
            dve.tensor_copy(k.mask[:, :], masks).then_inc(halved, 1)
            for n in range(AHEAD):
                k.split_lo(dve, n)

        @block.tensor
        def _(pe):
            pe.wait_ge(oh_loaded, 32)
            for b, (lo, hi) in enumerate(((0, T), (T, T + P))):
                pe.matmul(k.psum[0:4, b, 0:hi - lo], relb, onehot[:, lo:hi], start=True, stop=True).then_inc(bias_done, 1)

        @block.scalar
        def _(act):
            for b, (lo, hi) in enumerate(((0, T), (T, T + P))):
                act.wait_ge(bias_done, b + 1)
                act.activation(row[:, lo:hi], k.psum[0:4, b, 0:hi - lo], ACT.Copy).then_inc(bias_copied, 1)
            for n in range(AHEAD):
                k.split_hi(act, n)


def split_tiles_hi(act, tiles, halves, ready):
    for n, v in enumerate(tiles):
        act.activation(halves.hi(n), v, ACT.Copy).then_inc(ready, 1)


def split_tiles_lo(dve, tiles, halves, hi_ready, ready):
    for n, v in enumerate(tiles):
        dve.wait_ge(hi_ready, n + 1)
        dve.tensor_tensor(halves.lo(n), v, halves.hi(n).bitcast(F32), ALU.subtract).then_inc(ready, 1)


def split_work(k, tiles, halves, ready):
    hi_ready, lo_ready = k.sem(), k.sem()

    def scalar(act, i):
        ready(act, i)
        act.activation(halves.hi(i), tiles[i], ACT.Copy).then_inc(hi_ready, 1)

    def vector(dve, i):
        dve.wait_ge(hi_ready, i + 1)
        dve.tensor_tensor(halves.lo(i), tiles[i], halves.hi(i).bitcast(F32), ALU.subtract).then_inc(lo_ready, 1)

    w = Work(len(tiles), scalar=scalar, vector=vector)
    w.out_lo = lo_ready
    return w


def project(k, first, src, rhs, out, turned=(), cos="cos", sin="sin", rows=64, banks=(0, 1, 2), free=None,
            rhs_ready=None, factor=None):
    src_hi, src_lo, copied, chain, roped = (k.sem() for _ in range(5))
    if src:
        rhs_ready = src_lo
    order = [t for t in range(len(out)) if t in turned]
    n_out, nb = len(out), len(banks)

    def tensor(pe, t):
        if t < n_out:
            if t - nb in order:
                pe.wait_ge(roped, order.index(t - nb) + 1)
            elif t >= nb:
                pe.wait_ge(copied, t - nb + 1)
            k.product(pe, k.bank(banks[t % nb]), first + t, rhs, rhs_ready=rhs_ready if t == 0 else None)

    def scalar(act, t):
        if t == 0 and src:
            split_tiles_hi(act, src, rhs, src_hi)
        if 1 <= t <= n_out:
            o = t - 1
            if free is not None:
                free(act, o)
            if factor is None:
                act.wait_ge(k.unit_used, first + t)
                act.activation(out[o], k.bank(banks[o % nb]), ACT.Copy).then_inc(copied, 1)
            k.split_hi(act, first + o + AHEAD)

    chains = []

    def vector(dve, t):
        if t == 0:
            chains.append(Chain(dve, chain))
            if src:
                split_tiles_lo(dve, src, rhs, src_hi, src_lo)
        ch = chains[0]
        if 1 <= t <= n_out:
            if factor is not None:
                dve.wait_ge(k.unit_used, first + t)
                dve.tensor_tensor(out[t - 1], k.bank(banks[(t - 1) % nb]), factor, ALU.mult).then_inc(copied, 1)
            k.split_lo(dve, first + t - 1 + AHEAD)
        if t - 1 in order:
            bank, o, c, si = k.bank(banks[(t - 1) % nb]), out[t - 1], k.c(cos), k.c(sin)
            dve.wait_ge(copied, t)
            for r in range(0, rows, 64):
                a, b = slice(r, r + 32), slice(r + 32, r + 64)
                ch(dve.tensor_tensor(bank[a], o[b], si[b], ALU.mult))
                ch(dve.tensor_tensor(bank[b], o[a], si[a], ALU.mult))
            ch.sync()
            ch.then(dve.tensor_tensor(o[0:rows], o[0:rows], c[0:rows], ALU.mult))
            dve.tensor_tensor(o[0:rows], o[0:rows], bank[0:rows], ALU.add).then_inc(roped, 1)

    w = Work(n_out + 1, tensor, scalar, vector, end=first + n_out)
    w.copied, w.roped = copied, roped
    return w


def project_residual(k, first, src, rhs, scale, units=1, rhs_ready=None, free=None, sums=None, acc=None, sq=None,
                     early=0):
    src_hi, src_lo, added, squared, summed = (k.sem() for _ in range(5))
    if src:
        rhs_ready = src_lo
    nb = 6 if sums else 8

    def tensor(pe, t):
        if t == DT:
            if free is not None:
                free(pe, 6)
            pe.wait_ge(summed, DT - 2)
            pe.matmul(k.bank(6), k.c("mean"), acc, start=True, stop=False)
            pe.wait_ge(added if sums == "x" else squared, DT)
            pe.matmul(k.bank(6), k.c("mean"), k.x(DT - 1) if sums == "x" else sq[(DT - 1) % 2], start=False, stop=True)
        if t < DT:
            if t >= nb:
                pe.wait_ge(added, t - nb + 1)
            elif free is not None:
                free(pe, t)
            if t < early:
                pe.wait_ge(rhs_ready, DT)
                k.product(pe, k.bank(t), first + t, rhs, part=[DT - 1])
            else:
                k.product(pe, k.bank(t % nb), first + t * units, rhs, units=units, rhs_ready=rhs_ready if t == 0 else None)

    def most(pe, t):
        k.product(pe, k.bank(t), first + t, rhs, rhs_ready=rhs_ready if t == 0 else None, part=range(DT - 1))

    def scalar(act, t):
        if src and t == 0:
            split_tiles_hi(act, src, rhs, src_hi)
        if sums == "squares" and 1 <= t <= DT:
            d = t - 1
            act.wait_ge(added, d + 1)
            if d >= 2:
                act.wait_ge(summed, max(d - 2, 1))
            act.activation(sq[d % 2], k.x(d), ACT.Square).then_inc(squared, 1)
        if sums and t == DT:
            act.activation(k.small[:, 50:51], k.eps(1e-6), ACT.Sqrt)
        if t < DT:
            for n in range(first + t * units, first + (t + 1) * units):
                k.split_hi(act, n + AHEAD)

    def vector(dve, t):
        if src and t == 0:
            split_tiles_lo(dve, src, rhs, src_hi, src_lo)
        if t < DT:
            for n in range(first + t * units, first + (t + 1) * units):
                k.split_lo(dve, n + AHEAD)
            dve.wait_ge(k.unit_used, first + (t + 1) * units)
            dve.scalar_tensor_tensor(out=k.x(t), in0=k.x(t), scalar=scale, in1=k.bank(t % nb),
                                     op0=ALU.mult, op1=ALU.add).then_inc(added, 1)

    def gpsimd(pool, t):
        if sums and 2 <= t < DT:
            d = t - 1
            here = [k.x(d - 1), k.x(d)] if sums == "x" else [sq[(d - 1) % 2], sq[d % 2]]
            pool.wait_ge(added if sums == "x" else squared, d + 1)
            if d >= 2:
                pool.wait_ge(summed, d - 1)
            pool.tensor_tensor(acc, here[0] if d == 1 else acc, here[1], ALU.add).then_inc(summed, 1)

    w = Work(DT + 1 if sums else DT, tensor, scalar, vector, gpsimd, end=first + DT * units)
    w.early = Work(early, most)
    w.added = added
    return w


def layer_norm(k, g, b, j, scratch, out=None):
    centred, squared, var_done, root, inverse, scaled, shifted, out_hi, out_lo = (k.sem() for _ in range(9))
    sq = [k.tile(scratch), k.tile(scratch + 1)]
    rstd = k.tile(scratch + 2)

    def tensor(pe, t):
        for d in range(DT):
            pe.wait_ge(squared, d + 1)
            pe.matmul(k.bank(7), k.c("mean"), sq[d % 2], start=(d == 0), stop=(d == DT - 1)).then_inc(var_done, 1)

    def vector(dve, t):
        for d in range(DT):
            dve.tensor_tensor(k.x(d), k.x(d), k.bank(6), ALU.subtract).then_inc(centred, 1)
        dve.wait_ge(root, 1)
        dve.reciprocal(rstd, rstd).then_inc(inverse, 1)
        dve.wait_ge(inverse, 1)

        def lo(d):
            dve.wait_ge(out_hi, d + 1)
            dve.tensor_tensor(out.lo(d), k.x(d), out.hi(d).bitcast(F32), ALU.subtract).then_inc(out_lo, 1)

        for d in range(DT):
            dve.tensor_tensor(k.x(d), k.x(d), rstd, ALU.mult).then_inc(scaled, 1)
            if out is not None and d >= 1:
                lo(d - 1)
        if out is not None:
            lo(DT - 1)

    def scalar(act, t):
        for d in range(DT):
            act.wait_ge(centred, d + 1)
            if d >= 2:
                act.wait_ge(var_done, d - 1)
            act.activation(sq[d % 2], k.x(d), ACT.Square).then_inc(squared, 1)
        act.wait_ge(var_done, DT)
        act.activation(rstd, k.bank(7), ACT.Sqrt, bias=k.eps(1e-5)).then_inc(root, 1)
        for d in range(DT):
            act.wait_ge(scaled, d + 1)
            act.activation(k.x(d), k.x(d), ACT.Identity, scale=k.v(g, j * DT + d),
                           bias=k.v(b, j * DT + d)).then_inc(shifted, 1)
            if out is not None:
                act.wait_ge(shifted, d + 1)
                act.activation(out.hi(d), k.x(d), ACT.Copy).then_inc(out_hi, 1)

    w = Work(1, tensor, scalar, vector)
    w.shifted, w.out_lo = shifted, out_lo
    return w


def rms_norm(k, g, j, out, sq, rstd, summed):
    squared, mean_done, root, rstd_ready, out_hi, out_lo = (k.sem() for _ in range(6))

    def tensor(pe, d):
        if d < DT:
            pe.wait_ge(squared, d + 1)
            pe.matmul(k.bank(6), k.c("mean"), sq[d % 2], start=(d == 0), stop=(d == DT - 1)).then_inc(mean_done, 1)

    def scalar(act, d):
        if d < DT:
            if d >= 2:
                act.wait_ge(mean_done, d - 1)
            act.activation(sq[d % 2], k.x(d), ACT.Square).then_inc(squared, 1)
        else:
            for n in range(DT):
                act.activation(out.hi(n), k.x(n), ACT.Identity, scale=k.v(g, j * DT + n)).then_inc(out_hi, 1)
            if not summed:
                act.wait_ge(mean_done, DT)
            act.activation(rstd, k.bank(6), ACT.Sqrt, bias=k.eps(1e-6)).then_inc(root, 1)

    def vector(dve, d):
        if d == DT:
            for n in range(DT):
                dve.wait_ge(out_hi, n + 1)
                dve.scalar_tensor_tensor(out=out.lo(n), in0=k.x(n), scalar=k.v(g, j * DT + n), in1=out.hi(n).bitcast(F32),
                                         op0=ALU.mult, op1=ALU.subtract).then_inc(out_lo, 1)
            dve.wait_ge(root, 1)
            dve.reciprocal(rstd, rstd).then_inc(rstd_ready, 1)
            dve.wait_ge(rstd_ready, 1)

    if summed:
        w = Work(1, None, lambda act, t: scalar(act, DT), lambda dve, t: vector(dve, DT))
    else:
        w = Work(DT + 1, tensor, scalar, vector)
    w.out_lo, w.rstd_ready = out_lo, rstd_ready
    return w


def attention(k, heads, scale, prob, probT, banks, ready=None, difference=None):
    scores_done, maxima, exps_done, probs_ready, turned, turned_copied, out_done, out_copied, chain = \
        (k.sem() for _ in range(9))
    units = [(h, i) for h in range(len(heads)) for i in range(TB)]
    U = len(units)
    G = len(heads[0][0])
    s_bank, t_bank, o_bank = [k.bank(b) for b in banks[:G]], k.bank(banks[G]), k.bank(banks[G + 1])
    s = k.small[:, 0:16]

    def fills(u):
        return max(min(u - 1, U), 0) + (min(u, U) + TB - 1) // TB

    def tensor(pe, u):
        at = fills(u)
        if u < U and units[u][1] == 0:
            h = units[u][0]
            if ready is not None:
                ready(pe, h)
            if at >= 1:
                pe.wait_ge(turned_copied, at)
            for j in range(TB):
                b = slice(j * P, (j + 1) * P)
                last = pe.transpose(t_bank[:, b], heads[h][1][:, b], k.c("ident"))
            last.then_inc(turned, 1)
            at += 1
        if 1 <= u <= U:
            h, i = units[u - 1]
            pe.wait_ge(probs_ready, u)
            if at >= 1:
                pe.wait_ge(turned_copied, at)
            for j in range(i + 1):
                b = slice(j * P, (j + 1) * P)
                last = pe.transpose(t_bank[:, b], prob[0][:, b], k.c("ident"))
            last.then_inc(turned, 1)
            at += 1
        if u < U:
            h, i = units[u]
            if u >= 1:
                pe.wait_ge(exps_done, G * u)
            for g, (q, key, first, terms) in enumerate(heads[h][0]):
                lo, hi = first(i), (i + 1) * P
                adds = [(j, a) for j in range(lo // P, i + 1) for a in terms(i, j)]
                last = pe.matmul(s_bank[g][:, lo:hi], q[:, i * P:(i + 1) * P], key[:, lo:hi], start=True, stop=not adds)
                for n, (j, (lhsT, rhs)) in enumerate(adds):
                    last = pe.matmul(s_bank[g][:, j * P:(j + 1) * P], lhsT, rhs, start=False, stop=(n == len(adds) - 1))
            last.then_inc(scores_done, 1)
        if 1 <= u <= U:
            h, i = units[u - 1]
            pe.wait_ge(turned_copied, at)
            if u >= 2:
                pe.wait_ge(out_copied, u - 1)
            for j in range(i + 1):
                b = slice(j * P, (j + 1) * P)
                last = pe.matmul(o_bank[:, 0:P], heads[h][1][:, b], probT[:, b], start=(j == 0), stop=(j == i))
            last.then_inc(out_done, 1)

    def scalar(act, u):
        at = fills(u)
        if u < U and units[u][1] == 0:
            act.wait_ge(turned, at + 1)
            act.activation(heads[units[u][0]][1], t_bank, ACT.Copy).then_inc(turned_copied, 1)
            at += 1
        if 1 <= u <= U:
            h, i = units[u - 1]
            act.wait_ge(turned, at + 1)
            if u >= 2:
                act.wait_ge(out_done, u - 1)
            act.activation(probT[:, 0:(i + 1) * P], t_bank[:, 0:(i + 1) * P], ACT.Copy).then_inc(turned_copied, 1)
        if u < U:
            h, i = units[u]
            act.wait_ge(maxima, u + 1)
            for g, (q, key, first, terms) in enumerate(heads[h][0]):
                lo, hi = first(i), (i + 1) * P
                nm = s[:, 6 + g:7 + g] if difference is not None else s[:, 6:7]
                act.activation(prob[g][:, lo:hi], s_bank[g][:, lo:hi], ACT.Exp, bias=nm, scale=scale,
                               accum_out=s[:, 3 + g:4 + g]).then_inc(exps_done, 1)

    chains = []

    def vector(dve, u):
        if u == 0:
            chains.append(Chain(dve, chain))
        ch = chains[0]
        if 2 <= u <= U + 1:
            h, i = units[u - 2]
            dve.wait_ge(out_done, u - 1)
            dve.tensor_copy(heads[h][2][:, i * P:(i + 1) * P], o_bank[:, 0:P]).then_inc(out_copied, 1)
        if u < U:
            h, i = units[u]
            dve.wait_ge(scores_done, u + 1)
            if u >= 1:
                dve.wait_ge(turned, fills(u) + (units[u][1] == 0) + 1)
            for g, (q, key, first, terms) in enumerate(heads[h][0]):
                ch(dve.reduce_max(s[:, g:g + 1], s_bank[g][:, first(i):(i + 1) * P], AX_X))
            ch.sync()
            if difference is not None:
                dve.tensor_scalar(s[:, 6:8], s[:, 0:2], -scale, None, ALU.mult).then_inc(maxima, 1)
            else:
                for g in range(1, G):
                    ch.then(dve.tensor_tensor(s[:, 0:1], s[:, 0:1], s[:, g:g + 1], ALU.max))
                dve.tensor_scalar(s[:, 6:7], s[:, 0:1], -scale, None, ALU.mult).then_inc(maxima, 1)
            hi = (i + 1) * P
            dve.wait_ge(exps_done, G * (u + 1))
            if difference is not None:
                ch.then(dve.reciprocal(s[:, 8:10], s[:, 3:5]))
                ch(dve.tensor_scalar(s[:, 9:10], s[:, 9:10], difference, None, ALU.mult))
                ch(dve.tensor_scalar(prob[0][:, 0:hi], prob[0][:, 0:hi], s[:, 8:9], None, ALU.mult))
                ch.sync()
                dve.scalar_tensor_tensor(out=prob[0][:, 0:hi], in0=prob[1][:, 0:hi], scalar=s[:, 9:10],
                                         in1=prob[0][:, 0:hi], op0=ALU.mult, op1=ALU.add).then_inc(probs_ready, 1)
            else:
                for g in range(1, G):
                    lo = heads[h][0][g][2](i)
                    ch(dve.tensor_tensor(s[:, 3:4], s[:, 3:4], s[:, 3 + g:4 + g], ALU.add))
                    ch.then(dve.tensor_tensor(prob[0][:, lo:hi], prob[0][:, lo:hi], prob[g][:, lo:hi], ALU.add))
                ch.then(dve.reciprocal(s[:, 8:9], s[:, 3:4]))
                dve.tensor_scalar(prob[0][:, 0:hi], prob[0][:, 0:hi], s[:, 8:9], None, ALU.mult).then_inc(probs_ready, 1)

    w = Work(U + 2, tensor, scalar, vector)
    w.out_done, w.out_copied = out_done, out_copied
    return w



def rwkv_shift(k, zs, mix, copied, at, delta):
    stepped, edge, mixed = (k.sem() for _ in range(3))

    def gpsimd(pool, t):
        pool.wait_ge(copied, at[t] + 1)
        if t >= 3:
            pool.wait_ge(mixed, t - 2)
        pool.tensor_tensor(delta[t % 3][:, 1:T], zs[t][:, 0:T - 1], zs[t][:, 1:T], ALU.subtract).then_inc(stepped, 1)

    def scalar(act, t):
        act.wait_ge(copied, at[t] + 1)
        if t >= 3:
            act.wait_ge(mixed, t - 2)
        act.activation(delta[t % 3][:, 0:1], zs[t][:, 0:1], ACT.Copy, scale=-1.0).then_inc(edge, 1)

    def vector(dve, t):
        dve.wait_ge(stepped, t + 1)
        dve.wait_ge(edge, t + 1)
        dve.scalar_tensor_tensor(out=zs[t], in0=delta[t % 3], scalar=k.v("mix", mix[t]), in1=zs[t],
                                 op0=ALU.mult, op1=ALU.add).then_inc(mixed, 1)

    w = Work(len(zs), scalar=scalar, vector=vector, gpsimd=gpsimd)
    w.mixed = mixed
    return w


def rwkv_loras(k, mixed, loaded, weights, banks):
    tanh_done, gates_ready, gate_tanh, product_done, consumed, finished = (k.sem() for _ in range(6))
    wup, aup, gup1, gup2 = weights
    tw, z_wa, z_g = k.tile(46), k.tile(24), k.tile(25, 2)
    M = 12
    half = 0.5 * float(np.exp(-0.5))

    def scalar(act, m):
        if m == 0:
            act.wait_ge(mixed, 3)
            act.activation(tw, z_wa, ACT.Tanh).then_inc(tanh_done, 1)
            act.activation(z_g, z_g, ACT.Tanh, scale=0.5).then_inc(gate_tanh, 1)
        if 1 <= m <= M:
            j, kind = (m - 1) // 3, (m - 1) % 3
            bank = k.bank(banks[(m - 1) % 2])
            act.wait_ge(product_done, m)
            if kind == 2:
                act.activation(k.tile(27 + j), bank, ACT.Copy).then_inc(consumed, 1)
            else:
                act.activation(k.tile((16, 20)[kind] + j), bank, ACT.Tanh, scale=0.5,
                               bias=k.v(("w0", "a0")[kind], j)).then_inc(consumed, 1)

    def vector(dve, m):
        if m == 0:
            dve.wait_ge(gate_tanh, 1)
            dve.tensor_scalar(z_g, z_g, 0.5, 0.5, ALU.mult, ALU.add).then_inc(gates_ready, 1)
        if m >= 2 and (m - 2) % 3 < 2:
            j, kind = (m - 2) // 3, (m - 2) % 3
            o, a = k.tile((16, 20)[kind] + j), (-half, 0.5)[kind]
            dve.wait_ge(consumed, m - 1)
            dve.tensor_scalar(o, o, a, a, ALU.mult, ALU.add).then_inc(finished, 1)

    def tensor(pe, m):
        if m < M:
            j, kind = m // 3, m % 3
            cols, bank = slice(j * P, (j + 1) * P), k.bank(banks[m % 2])
            if m == 0:
                pe.wait_ge(loaded, 16)
                pe.wait_ge(tanh_done, 1)
            if m == 2:
                pe.wait_ge(gates_ready, 1)
            if m >= 2:
                pe.wait_ge(consumed, m - 1)
            if kind == 0:
                last = pe.matmul(bank, wup[:, cols], tw, start=True, stop=True)
            elif kind == 1:
                last = pe.matmul(bank, aup[:, cols], z_wa, start=True, stop=True)
            else:
                pe.matmul(bank, gup1[:, cols], z_g[:, 0:T], start=True, stop=False)
                last = pe.matmul(bank, gup2[:, cols], z_g[:, T:2 * T], start=False, stop=True)
            last.then_inc(product_done, 1)

    w = Work(M + 2, tensor, scalar, vector)
    w.consumed, w.finished = consumed, finished
    return w


def rwkv_scales(k, pairs, mixed, loras, temps, banks):
    square_ready, square_sum, root, rk_ready, bonus_sum, bonus_made, sums_ready, outward, exps_done, rate_made, \
        scaled, chain = (k.sem() for _ in range(12))
    kk, sq, cum, rk, cen, prv = temps
    nrm, t2, e_out, e_in = sq, cum, cum, cen

    def tensor(pe, t):
        j, step = t // 4, t % 4
        if step == 1:
            pe.wait_ge(square_ready, j + 1)
            if j == 0:
                pe.wait_ge(loras.consumed, 12)
            else:
                pe.wait_ge(root, j)
            pe.matmul(k.bank(banks[0]), k.c("sum64"), sq, start=True, stop=True).then_inc(square_sum, 1)
            pe.wait_ge(rk_ready, j + 1)
            if j >= 1:
                pe.wait_ge(bonus_made, j)
            pe.matmul(k.bank(banks[1]), k.c("sum64"), rk, start=True, stop=True).then_inc(bonus_sum, 1)

    def scalar(act, t):
        j, step = t // 4, t % 4
        pair = pairs[j]
        if step == 2:
            act.wait_ge(square_sum, j + 1)
            act.activation(nrm, k.bank(banks[0]), ACT.Sqrt).then_inc(root, 1)
            act.wait_ge(sums_ready, j + 1)
            act.activation(e_out, cen, ACT.Exp, scale=-1.0).then_inc(outward, 1)
            act.activation(prv, prv, ACT.Exp).then_inc(exps_done, 1)
            act.activation(pair.fexp, pair.fsum, ACT.Exp, scale=0.5).then_inc(exps_done, 1)
            act.wait_ge(outward, j + 1)
            act.activation(e_in, cen, ACT.Exp).then_inc(exps_done, 1)

    chains = []

    def vector(dve, t):
        j, step = t // 4, t % 4
        pair = pairs[j]
        r, key, val, lw, rate, om = pair.r, pair.key, pair.val, pair.lw, pair.rate, pair.om
        if t == 0:
            chains.append(Chain(dve, chain))
            dve.wait_ge(loras.consumed, 12)
            dve.wait_ge(loras.finished, 8)
        ch = chains[0]
        if step == 0:
            dve.wait_ge(mixed, 3 * j + 6)
            ch(dve.tensor_scalar(om, k.v("k_a", j), -1.0, 1.0, ALU.mult, ALU.add))
            ch.then(dve.tensor_scalar(kk, key, k.v("k_k", j), None, ALU.mult))
            dve.tensor_tensor(sq, kk, kk, ALU.mult).then_inc(square_ready, 1)
            if j >= 1:
                dve.wait_ge(scaled, 3 * j)
            ch.then(dve.tensor_scalar(t2, rate, k.v("k_a", j), om, ALU.mult, ALU.add))
            ch.then(dve.tensor_tensor(key, key, t2, ALU.mult))
            dve.scalar_tensor_tensor(out=rk, in0=r, scalar=k.v("r_k", j), in1=key, op0=ALU.mult,
                                     op1=ALU.mult).then_inc(rk_ready, 1)
        if step == 1:
            ch.then(dve.tensor_tensor_scan(cum, k.c("reset"), lw, 0.0, ALU.mult, ALU.add))
            cum3 = cum.rearrange("p (n c) -> p n c", n=NCHUNK)
            total = cum3[:, :, CHUNK - 1:CHUNK]
            ch(dve.tensor_tensor(pair.fsum.unsqueeze(2), total[:, 0:NCHUNK - 1, :], total[:, 1:NCHUNK, :], ALU.add))
            ch.then(dve.scalar_tensor_tensor(out=cen.rearrange("p (n c) -> p n c", n=NCHUNK),
                                             in0=total.to_broadcast([P, NCHUNK, CHUNK]), scalar=-0.5, in1=cum3,
                                             op0=ALU.mult, op1=ALU.add))
            dve.tensor_tensor(prv, cen, lw, ALU.subtract).then_inc(sums_ready, 1)
        if step == 3:
            dve.wait_ge(root, j + 1)
            ch.then(dve.tensor_scalar(nrm, nrm, 1e-12, None, ALU.max))
            ch.then(dve.reciprocal(nrm, nrm))
            ch.then(dve.tensor_tensor(kk, kk, nrm, ALU.mult))
            dve.tensor_tensor(rate, rate, kk, ALU.mult).then_inc(rate_made, 1)
            dve.wait_ge(bonus_sum, j + 1)
            dve.tensor_tensor(pair.bonus, val, k.bank(banks[1]), ALU.mult).then_inc(bonus_made, 1)
            dve.wait_ge(exps_done, 3 * (j + 1))
            ch.then(dve.scalar_tensor_tensor(out=lw, in0=kk, scalar=-1.0, in1=prv, op0=ALU.mult, op1=ALU.mult))

    def gpsimd(pool, t):
        j, step = t // 4, t % 4
        pair = pairs[j]
        if step == 3:
            pool.wait_ge(exps_done, 3 * (j + 1))
            pool.tensor_tensor(pair.key, pair.key, e_out, ALU.mult).then_inc(scaled, 1)
            pool.tensor_tensor(pair.r, pair.r, e_in, ALU.mult).then_inc(scaled, 1)
            pool.wait_ge(rate_made, j + 1)
            pool.tensor_tensor(pair.rate, pair.rate, e_out, ALU.mult).then_inc(scaled, 1)

    return Work(4 * len(pairs), tensor, scalar, vector, gpsimd)


def blocks(tile):
    return tile.rearrange("p (i t) -> p i t", i=TB)


def spread(mask):
    return mask.unsqueeze(1).to_broadcast([P, TB, P])


HALF = [slice(0, 64), slice(64, 128)]


class Pair:

    def __init__(self, k, j):
        self.k, self.j = k, j
        self.r, self.key, self.val, self.lw, self.rate, self.gate = (k.tile(b + j) for b in (0, 4, 8, 16, 20, 27))
        self.at, self.bt, self.kt, self.rt = self.lw, self.rate, self.key, self.r
        self.bonus = k.tile((24, 25, 26, 46)[j])
        small = 64 + 20 * j
        self.last_outputs = None
        self.fsum, self.fexp, self.om = (k.small[:, small + a:small + b] for a, b in ((0, 7), (8, 15), (16, 17)))

    def open(self, work, bank):
        k = self.k
        W = [k.tile(work + n) for n in range(15)]
        self.tokA, self.tokB, self.tokK, self.tokV = W[0:4]
        self.X, self.XT, self.NT, self.AK, self.level = W[4:6], W[6:8], W[8:10], W[10:12], W[12:14]
        self.av = W[14]
        self.RB, self.RK, self.TA = self.X, self.NT, self.level[0]
        self.SA, self.SAz, self.Vz = self.tokA, self.AK, self.XT
        self.states = [self.level[1], self.val]
        self.banks = [k.bank(bank + b) for b in range(4)]

    def S(self, n):
        return self.states[n // 4][:, (n % 4) * P:(n % 4 + 1) * P]

    def matrices(self, before=None):
        k = self.k
        made, act_done, dve_done, x_ready, xt_ready = (k.sem() for _ in range(5))
        at, bt, kt = self.at, self.bt, self.kt
        X, XT, NT, AK, b4 = self.X, self.XT, self.NT, self.AK, self.banks
        self.m = dict(act_done=act_done, x_ready=x_ready, xt_ready=xt_ready)

        def outer(pe, bank, left, right, h):
            for i in range(TB):
                b = slice(i * P, (i + 1) * P)
                last = pe.matmul(bank[:, b], left[HALF[h], b], right[HALF[h], b], start=True, stop=True)
            last.then_inc(made, 1)

        def tensor(pe, t):
            if t == 0:
                if before is not None:
                    pe.wait_ge(before.o["y_copied"], 1)
                    pe.wait_ge(before.o["centred"], 1)
                    pe.wait_ge(before.o["root"], 1)
                for src, bank in zip((at, bt, kt, self.val), b4):
                    for i in range(TB):
                        b = slice(i * P, (i + 1) * P)
                        last = pe.transpose(bank[:, b], src[:, b], k.c("ident"))
                    last.then_inc(made, 1)
            if t == 1:
                pe.wait_ge(act_done, 1)
                outer(pe, b4[0], at, bt, 0)
                pe.wait_ge(act_done, 2)
                outer(pe, b4[1], bt, at, 0)
                pe.wait_ge(act_done, 3)
                outer(pe, b4[2], kt, at, 0)
            if t == 2:
                pe.wait_ge(act_done, 4)
                outer(pe, b4[3], at, bt, 1)
                pe.wait_ge(dve_done, 1)
                outer(pe, b4[0], bt, at, 1)
                pe.wait_ge(act_done, 5)
                outer(pe, b4[1], kt, at, 1)
            if t == 3:
                pe.wait_ge(dve_done, 4)
                for h in range(2):
                    for i in range(TB):
                        b, cols = slice(i * P, (i + 1) * P), slice(i * P + 64 * h, i * P + 64 * h + 64)
                        last = pe.matmul(b4[2][:, cols], AK[h][:, b], self.tokV[:, cols], start=True, stop=True)
                last.then_inc(made, 1)

        def scalar(act, t):
            if t == 0:
                for n, dst in enumerate((self.tokA, self.tokB, self.tokK, self.tokV)):
                    act.wait_ge(made, n + 1)
                    act.activation(dst, b4[n], ACT.Copy).then_inc(act_done, 1)
            if t in (1, 2):
                act.wait_ge(made, 6 if t == 1 else 9)
                act.activation(NT[t - 1], b4[1 if t == 1 else 0], ACT.Copy).then_inc(act_done, 1)
            if t == 3:
                act.wait_ge(made, 11)
                act.activation(self.av, b4[2], ACT.Copy).then_inc(act_done, 1)

        def vector(dve, t):
            if t in (1, 2):
                h = t - 1
                dve.wait_ge(made, 5 + 3 * h)
                dve.tensor_tensor(blocks(X[h]), blocks(b4[3 * h]), spread(k.c("low0")), ALU.mult).then_inc(dve_done, 1)
                dve.wait_ge(made, 7 + 3 * h)
                dve.tensor_tensor(blocks(AK[h]), blocks(b4[2 - h]), spread(k.c("up")), ALU.mult).then_inc(dve_done, 1)
                dve.wait_ge(dve_done, 2 * h + 1)
                dve.tensor_tensor(blocks(X[h]), blocks(X[h]), spread(k.c("ident")), ALU.add).then_inc(x_ready, 1)

        def gpsimd(pool, t):
            if t in (1, 2):
                h = t - 1
                pool.wait_ge(act_done, 5 + h)
                pool.tensor_tensor(blocks(XT[h]), blocks(NT[h]), spread(k.c("up0")), ALU.mult).then_inc(xt_ready, 1)
                pool.wait_ge(xt_ready, 2 * h + 1)
                pool.tensor_tensor(blocks(XT[h]), blocks(XT[h]), spread(k.c("ident")), ALU.add).then_inc(xt_ready, 1)

        return Work(4, tensor, scalar, vector, gpsimd)

    def invert(self, same_stage):
        k = self.k
        level_ready, p_done, p_copied, xp_done, x_ready = (k.sem() for _ in range(5))
        X, XT, NT, PR, level = self.X, self.XT, self.NT, self.AK, self.level
        self.i = dict(p_done=p_done, p_copied=p_copied, xp_done=xp_done, x_ready=x_ready)

        def bank(l, h, what):
            p, q = (0, 2) if l % 2 else (2, 0)
            return self.banks[p + h] if what == "p" else self.banks[(q if h == 0 else p) + what]

        def gpsimd(pool, t):
            l = t + 1
            for h in range(2):
                if l >= 2:
                    pool.wait_ge(p_done, 2 * (l - 2) + h + 1)
                pool.tensor_tensor(blocks(level[h]), blocks(NT[h]), spread(k.c(f"up{l}")), ALU.mult).then_inc(level_ready, 1)

        def tensor(pe, t):
            l, n = t + 1, 2 * t
            if t == 0 and same_stage:
                pe.wait_ge(self.m["x_ready"], 2)
                pe.wait_ge(self.m["xt_ready"], 4)
                pe.wait_ge(self.m["act_done"], 7)
            for h in range(2):
                pe.wait_ge(level_ready, n + h + 1)
                if l >= 2:
                    pe.wait_ge(x_ready, n - 2 + h + 1)
                for i in range(TB):
                    b = slice(i * P, (i + 1) * P)
                    last = pe.matmul(bank(l, h, "p")[:, b], level[h][:, b], X[h][:, b], start=True, stop=True)
                last.then_inc(p_done, 1)
            for h in range(2):
                pe.wait_ge(p_copied, n + 2 if h == 0 else n + 2)
                if l < LEVELS - 1:
                    for i in range(TB):
                        b = slice(i * P, (i + 1) * P)
                        pe.matmul(bank(l, h, 0)[:, b], XT[h][:, b], PR[h][:, b], start=True, stop=True)
                for i in range(TB):
                    b = slice(i * P, (i + 1) * P)
                    last = pe.matmul(bank(l, h, 1)[:, b], PR[h][:, b], XT[h][:, b], start=True, stop=True)
                last.then_inc(xp_done, 1)

        def scalar(act, t):
            l = t + 1
            for h in range(2):
                act.wait_ge(p_done, 2 * t + h + 1)
                if l >= 2:
                    act.wait_ge(xp_done, 2 * (t - 1) + h + 1)
                act.activation(PR[h], bank(l, h, "p"), ACT.Copy).then_inc(p_copied, 1)

        def vector(dve, t):
            l = t + 1
            for h in range(2):
                dve.wait_ge(xp_done, 2 * t + h + 1)
                if l < LEVELS - 1:
                    dve.tensor_tensor(X[h], X[h], bank(l, h, 0), ALU.add)
                dve.tensor_tensor(XT[h], XT[h], bank(l, h, 1), ALU.add).then_inc(x_ready, 1)

        return Work(LEVELS - 1, tensor, scalar, vector, gpsimd)

    def apply_inverse(self):
        k, b4 = self.k, self.banks
        made, masked, ta_done, tv_done, copied = (k.sem() for _ in range(5))
        self.a = dict(masked=masked, tv_done=tv_done, copied=copied)

        def tensor(pe, t):
            if t == 0:
                pe.wait_ge(self.i["x_ready"], 2 * (LEVELS - 1))
                pe.wait_ge(self.i["p_copied"], 2 * (LEVELS - 1))
                for h in range(2):
                    for i in range(TB):
                        b, cols = slice(i * P, (i + 1) * P), slice(i * P + 64 * h, i * P + 64 * h + 64)
                        last = pe.matmul(b4[0][HALF[h], b], self.tokA[:, cols], self.XT[h][:, b], start=True, stop=True)
                last.then_inc(ta_done, 1)
                for h in range(2):
                    for i in range(TB):
                        b, cols = slice(i * P, (i + 1) * P), slice(i * P + 64 * h, i * P + 64 * h + 64)
                        last = pe.matmul(b4[1][:, cols], self.XT[h][:, b], self.av[:, cols], start=True, stop=True)
                last.then_inc(tv_done, 1)
            else:
                h = t - 1
                if h == 1:
                    pe.wait_ge(copied, 2)
                for n, left in enumerate((self.bt, self.kt)):
                    for i in range(TB):
                        b = slice(i * P, (i + 1) * P)
                        last = pe.matmul(b4[2 - 2 * h + n][:, b], left[HALF[h], b], self.rt[HALF[h], b], start=True, stop=True)
                    last.then_inc(made, 1)

        def scalar(act, t):
            if t == 0:
                act.wait_ge(ta_done, 1)
                act.activation(self.TA, b4[0], ACT.Copy).then_inc(copied, 1)
                act.wait_ge(tv_done, 1)
                act.activation(self.av, b4[1], ACT.Copy).then_inc(copied, 1)

        def vector(dve, t):
            if t >= 1:
                h = t - 1
                for n, dst in enumerate((self.RB[h], self.RK[h])):
                    dve.wait_ge(made, 2 * h + n + 1)
                    dve.tensor_tensor(blocks(dst), blocks(b4[2 - 2 * h + n]), spread(k.c("upincl")), ALU.mult).then_inc(masked, 1)

        return Work(3, tensor, scalar, vector)

    def chunks(self):
        k, b4 = self.k, self.banks
        cleared, v_copied, sa_done, sa_ready, state_done, state_ready, sa_copied = (k.sem() for _ in range(7))
        SA, SAz, Vz, S, tokV = self.SA, self.SAz, self.Vz, self.S, self.tokV
        self.c = dict(sa_copied=sa_copied, sa_ready=sa_ready, state_ready=state_ready)

        def gpsimd(pool, n):
            if n == 0:
                pool.wait_ge(self.i["xp_done"], 2 * (LEVELS - 1))
                pool.wait_ge(self.a["tv_done"], 1)
                pool.memset(S(0), 0.0).then_inc(cleared, 1)
                for p in range(2):
                    pool.wait_ge(cleared, 2 * p + 1)
                    pool.memset(SAz[p][HALF[1 - p]], 0.0).then_inc(cleared, 1)
                    pool.memset(Vz[p][HALF[1 - p]], 0.0).then_inc(cleared, 1)

        def scalar(act, n):
            if n == 0:
                for p in range(2):
                    act.activation(Vz[p][HALF[p]], tokV[HALF[p]], ACT.Copy).then_inc(v_copied, 1)
            i, p = n // 2, n % 2
            act.wait_ge(sa_ready, n + 1)
            act.activation(SA[HALF[p], i * P:(i + 1) * P], SAz[p][HALF[p], i * P:(i + 1) * P], ACT.Copy).then_inc(sa_copied, 1)

        def tensor(pe, n):
            i, p = n // 2, n % 2
            b = slice(i * P, (i + 1) * P)
            if n == 0:
                pe.wait_ge(cleared, 5)
                pe.wait_ge(self.a["masked"], 4)
                pe.wait_ge(self.a["copied"], 2)
                pe.wait_ge(v_copied, 2)
            if n >= 1:
                pe.wait_ge(state_ready, n)
            if n >= 2:
                pe.wait_ge(sa_ready, n - 1)
            pe.matmul(b4[n % 2][:, 0:P], self.TA[:, b], S(n), start=True, stop=True).then_inc(sa_done, 1)
            if n == NCHUNK - 1:
                return
            out = b4[2 + n % 2][:, 0:P]
            pe.matmul(out, k.c("ident"), S(n), start=True, stop=False)
            pe.matmul(out, self.tokK[:, b], Vz[p][:, b], start=False, stop=False)
            pe.wait_ge(sa_ready, n + 1)
            pe.matmul(out, self.tokB[:, b], SAz[p][:, b], start=False, stop=True).then_inc(state_done, 1)

        def vector(dve, n):
            i, p = n // 2, n % 2
            b = slice(i * P, (i + 1) * P)
            if n == 0:
                dve.wait_ge(cleared, 5)
                dve.wait_ge(self.a["copied"], 2)
            dve.wait_ge(sa_done, n + 1)
            dve.tensor_tensor(SAz[p][HALF[p], b], self.av[HALF[p], b], b4[n % 2][HALF[p], 0:P], ALU.add).then_inc(sa_ready, 1)
            if n == NCHUNK - 1:
                return
            dve.wait_ge(state_done, n + 1)
            dve.scalar_tensor_tensor(out=S(n + 1), in0=b4[2 + n % 2][:, 0:P], scalar=self.fexp[:, n:n + 1],
                                     in1=k.c("pair"), op0=ALU.mult, op1=ALU.mult).then_inc(state_ready, 1)

        return Work(NCHUNK, tensor, scalar, vector, gpsimd)

    def outputs(self):
        k, j, b4 = self.k, self.j, self.banks
        y_done, y_copied, mean_done, centred, squared, var_done, root, chain, scaled, affine = (k.sem() for _ in range(10))
        y, sq, rstd = self.key, self.SAz[0], self.SAz[1]
        self.o = dict(y_copied=y_copied, centred=centred, root=root, affine=affine)

        def tensor(pe, t):
            if t == 0:
                pe.wait_ge(self.c["sa_copied"], NCHUNK)
                pe.wait_ge(self.c["sa_ready"], NCHUNK)
                pe.wait_ge(self.c["state_ready"], NCHUNK - 1)
                for i in range(TB):
                    b = slice(i * P, (i + 1) * P)
                    for h in range(2):
                        cols = slice(i * P + 64 * h, i * P + 64 * h + 64)
                        pe.matmul(b4[0][HALF[h], b], self.SA[:, cols], self.RB[h][:, b], start=True, stop=False)
                        pe.matmul(b4[0][HALF[h], b], self.tokV[:, cols], self.RK[h][:, b], start=False, stop=True)
                    for n in (2 * i, 2 * i + 1):
                        chunk = slice(n * CHUNK, (n + 1) * CHUNK)
                        last = pe.matmul(b4[0][:, chunk], self.S(n), self.rt[:, chunk], start=False, stop=True,
                                         skip_group_check=True)
                last.then_inc(y_done, 1)
            if t == 1:
                pe.wait_ge(y_copied, 1)
                pe.matmul(b4[1], k.c("mean64"), y, start=True, stop=True).then_inc(mean_done, 1)
            if t == 2:
                pe.wait_ge(squared, 1)
                pe.matmul(b4[2], k.c("mean64"), sq, start=True, stop=True).then_inc(var_done, 1)

        def scalar(act, t):
            if t == 0:
                act.wait_ge(y_done, 1)
                act.activation(y, b4[0], ACT.Copy).then_inc(y_copied, 1)
            if t == 1:
                act.wait_ge(centred, 1)
                act.activation(sq, y, ACT.Square).then_inc(squared, 1)
            if t == 2:
                act.wait_ge(var_done, 1)
                act.activation(rstd, b4[2], ACT.Sqrt, bias=k.eps(64e-5)).then_inc(root, 1)
            if t == 3:
                act.wait_ge(scaled, 1)
                act.activation(y, y, ACT.Identity, scale=k.v("lnx_g", j), bias=k.v("lnx_b", j)).then_inc(affine, 1)

        chains = []

        def vector(dve, t):
            if t == 0:
                chains.append(Chain(dve, chain))
            ch = chains[0]
            if t == 1:
                dve.wait_ge(mean_done, 1)
                dve.tensor_tensor(y, y, b4[1], ALU.subtract).then_inc(centred, 1)
            if t == 3:
                dve.wait_ge(root, 1)
                ch.then(dve.reciprocal(rstd, rstd))
                dve.tensor_tensor(y, y, rstd, ALU.mult).then_inc(scaled, 1)
            if t == 4:
                dve.wait_ge(affine, 1)
                ch.then(dve.tensor_tensor(y, y, self.bonus, ALU.add))
                ch.then(dve.tensor_tensor(y, y, self.gate, ALU.mult))

        return Work(5, tensor, scalar, vector)



def squared_relu(k, first, rhs, out, rhs_ready=None, free=None, before=None):
    relu_done, squared, out_hi, out_lo = (k.sem() for _ in range(4))
    buf = [k.tile(0), k.tile(1)]

    def tensor(pe, t):
        if t < MLP_HALF:
            if t >= 8:
                pe.wait_ge(relu_done, t - 7)
            elif free is not None:
                free(pe, t)
            k.product(pe, k.bank(t % 8), first + t, rhs, rhs_ready=rhs_ready if t == 0 else None)

    def scalar(act, t):
        if t < MLP_HALF:
            act.wait_ge(k.unit_used, first + t + 1)
            if t >= 2:
                act.wait_ge(out_lo, t - 1)
            elif before is not None:
                act.wait_ge(before.out_lo, MLP_HALF)
            act.activation(buf[t % 2], k.bank(t % 8), ACT.Relu).then_inc(relu_done, 1)
            k.split_hi(act, first + t + AHEAD)
            act.wait_ge(squared, t + 1)
            act.activation(out.hi(t), buf[t % 2], ACT.Copy).then_inc(out_hi, 1)

    def vector(dve, t):
        if t < MLP_HALF:
            dve.wait_ge(relu_done, t + 1)
            dve.tensor_tensor(buf[t % 2], buf[t % 2], buf[t % 2], ALU.mult).then_inc(squared, 1)
            k.split_lo(dve, first + t + AHEAD)
            dve.wait_ge(out_hi, t + 1)
            dve.tensor_tensor(out.lo(t), buf[t % 2], out.hi(t).bitcast(F32), ALU.subtract).then_inc(out_lo, 1)

    w = Work(MLP_HALF, tensor, scalar, vector, end=first + MLP_HALF)
    w.relu_done, w.out_lo = relu_done, out_lo
    return w


def gated_ffn(k, l, half, first, h, factor, out, h_ready=None, free=None, before=None):
    g_scaled, base, conv1, conv2, tanh_done, left, finished, out_hi, out_lo = (k.sem() for _ in range(9))
    acc, th = [k.tile(0), k.tile(1)], [k.tile(2), k.tile(3)]

    def tensor(pe, f):
        if f >= 4:
            pe.wait_ge(finished, f - 3)
        elif free is not None:
            free(pe, f)
        for part in range(2):
            k.product(pe, k.bank(2 * (f % 4) + part), first + 2 * f + part, h,
                      rhs_ready=h_ready if f == 0 and part == 0 else None)

    def scalar(act, f):
        j = half * FFN_HALF + f
        act.wait_ge(g_scaled, f + 1)
        if f >= 2:
            act.wait_ge(out_lo, f - 1)
        elif before is not None:
            act.wait_ge(before.out_lo, FFN_HALF)
        act.activation(acc[f % 2], k.bank(2 * (f % 4)), ACT.Identity, scale=k.v("ffn_w", (3 * l + 2) * FFN_TILES + j),
                       bias=k.v("ffn_b", l * FFN_TILES + j)).then_inc(base, 1)
        k.split_hi(act, first + 2 * f + AHEAD)
        act.wait_ge(conv2, f + 1)
        act.activation(th[f % 2], acc[f % 2], ACT.Tanh, scale=0.5).then_inc(tanh_done, 1)
        k.split_hi(act, first + 2 * f + 1 + AHEAD)
        act.wait_ge(finished, f + 1)
        act.activation(out.hi(f), acc[f % 2], ACT.Copy).then_inc(out_hi, 1)

    def vector(dve, f):
        j = half * FFN_HALF + f
        g, u, a = k.bank(2 * (f % 4)), k.bank(2 * (f % 4) + 1), acc[f % 2]
        dve.wait_ge(k.unit_used, first + 2 * f + 1)
        dve.tensor_tensor(g, g, factor, ALU.mult).then_inc(g_scaled, 1)
        dve.wait_ge(base, f + 1)
        dve.scalar_tensor_tensor(out=a[:, 1:T], in0=g[:, 0:T - 1], scalar=k.v("ffn_w", (3 * l + 1) * FFN_TILES + j),
                                 in1=a[:, 1:T], op0=ALU.mult, op1=ALU.add).then_inc(conv1, 1)
        dve.wait_ge(conv1, f + 1)
        dve.scalar_tensor_tensor(out=a[:, 2:T], in0=g[:, 0:T - 2], scalar=k.v("ffn_w", 3 * l * FFN_TILES + j),
                                 in1=a[:, 2:T], op0=ALU.mult, op1=ALU.add).then_inc(conv2, 1)
        k.split_lo(dve, first + 2 * f + AHEAD)
        dve.wait_ge(tanh_done, f + 1)
        dve.scalar_tensor_tensor(out=a, in0=th[f % 2], scalar=1.0, in1=a, op0=ALU.add, op1=ALU.mult).then_inc(left, 1)
        k.split_lo(dve, first + 2 * f + 1 + AHEAD)
        dve.wait_ge(left, 2 * f + 1)
        dve.tensor_tensor(a, a, factor, ALU.mult).then_inc(left, 1)
        dve.wait_ge(left, 2 * f + 2)
        dve.wait_ge(k.unit_used, first + 2 * f + 2)
        dve.scalar_tensor_tensor(out=a, in0=a, scalar=0.5, in1=u, op0=ALU.mult, op1=ALU.mult).then_inc(finished, 1)
        dve.wait_ge(out_hi, f + 1)
        dve.tensor_tensor(out.lo(f), a, out.hi(f).bitcast(F32), ALU.subtract).then_inc(out_lo, 1)

    w = Work(FFN_HALF, tensor, scalar, vector, end=first + FFN_TILES)
    w.finished, w.out_lo = finished, out_lo
    return w



def head_norms(k, l, copied, loaded, lam_v, lam_p, sq, bank):
    squared, mean_done, root, inverse, cleared, normed, lam_sum, lam_exp, chain = (k.sem() for _ in range(9))
    src = [k.tile(4 * (n % 2) + n // 2) for n in range(8)]
    lam = k.small[:, 40:44]

    def gpsimd(pool, n):
        if n == 0:
            for h in range(4):
                pool.memset(k.tile(26 + h)[0:64], 0.0).then_inc(cleared, 1)

    def scalar(act, n):
        if n >= 1:
            act.wait_ge(mean_done, n)
            act.activation(sq[(n - 1) % 2], k.bank(bank), ACT.Sqrt, bias=k.eps(64e-6 if n % 2 else 1e-6)).then_inc(root, 1)
        if n < 8:
            act.wait_ge(copied, 3 * (n // 2) + n % 2 + 1)
            if n >= 2:
                act.wait_ge(normed, n - 1)
            act.activation(sq[n % 2], src[n], ACT.Square).then_inc(squared, 1)
        if n == 1:
            act.wait_ge(lam_sum, 2)
            act.activation(lam[:, 0:2], lam[:, 0:2], ACT.Exp).then_inc(lam_exp, 1)

    def tensor(pe, n):
        if n < 8:
            pe.wait_ge(squared, n + 1)
            if n >= 1:
                pe.wait_ge(root, n)
            pe.matmul(k.bank(bank), k.c("mean64" if n % 2 else "sum64"), sq[n % 2], start=True, stop=True).then_inc(mean_done, 1)

    chains = []

    def vector(dve, n):
        if n == 0:
            chains.append(Chain(dve, chain))
            ch = chains[0]
            dve.wait_ge(loaded, 80)
            lp = lam_v.rearrange("p (a b c) -> p a b c", a=2, b=2)
            ch.then(dve.tensor_tensor(lam_p.rearrange("p (a c) -> p a c", a=2), lp[:, :, 0, :], lp[:, :, 1, :], ALU.mult))
            dve.reduce_sum(lam[:, 0:1], lam_p[:, 0:64], AX_X).then_inc(lam_sum, 1)
            dve.reduce_sum(lam[:, 1:2], lam_p[:, 64:128], AX_X).then_inc(lam_sum, 1)
        ch = chains[0]
        if n >= 1:
            m, rs = n - 1, sq[(n - 1) % 2]
            dve.wait_ge(root, n)
            dve.reciprocal(rs, rs).then_inc(inverse, 1)
            dve.wait_ge(inverse, n)
            if m % 2 == 0:
                dve.scalar_tensor_tensor(out=src[m], in0=src[m], scalar=k.v("da_q_g", l), in1=rs,
                                         op0=ALU.mult, op1=ALU.mult).then_inc(normed, 1)
            else:
                up = slice(64, 128)
                ch(dve.scalar_tensor_tensor(out=k.tile(26 + m // 2)[up], in0=src[m][up], scalar=k.v("da_k_g", l)[up],
                                            in1=rs[up], op0=ALU.mult, op1=ALU.mult))
                ch.then(dve.scalar_tensor_tensor(out=src[m][0:64], in0=src[m][0:64], scalar=k.v("da_k_g", l)[0:64],
                                                 in1=rs[0:64], op0=ALU.mult, op1=ALU.mult))
                dve.memset(src[m][up], 0.0).then_inc(normed, 1)
        if n == 2:
            dve.wait_ge(lam_exp, 1)
            ch.then(dve.tensor_tensor(lam[:, 2:3], lam[:, 1:2], lam[:, 0:1], ALU.subtract))
            ch.then(dve.tensor_scalar(lam[:, 3:4], lam[:, 2:3], -LAM_INIT[l], None, ALU.add))

    w = Work(9, tensor, scalar, vector, gpsimd)
    w.normed, w.cleared, w.nlam = normed, cleared, lam[:, 3:4]
    return w


def tile_norms(k, jobs, sq, th, factors, banks, ready):
    squared, mean_done, root, tanh_done, chain, finished = (k.sem() for _ in range(6))
    N = len(jobs)

    def tensor(pe, n):
        if n < N:
            pe.wait_ge(squared, n + 1)
            if n >= 2:
                pe.wait_ge(root, n - 1)
            pe.matmul(k.bank(banks[n % 2]), k.c(jobs[n][1]), sq[n % 2], start=True, stop=True).then_inc(mean_done, 1)

    def scalar(act, n):
        if n < N:
            ready(act, n)
            if n >= 2:
                act.wait_ge(finished, n - 1)
            act.activation(sq[n % 2], jobs[n][0], ACT.Square).then_inc(squared, 1)
            if jobs[n][4] is not None:
                act.activation(th[n], jobs[n][4], ACT.Tanh, scale=0.5).then_inc(tanh_done, 1)
        if n >= 1:
            act.wait_ge(mean_done, n)
            act.activation(sq[(n - 1) % 2], k.bank(banks[(n - 1) % 2]), ACT.Sqrt, bias=k.eps(1e-6)).then_inc(root, 1)

    chains = []

    def vector(dve, n):
        if n == 0:
            chains.append(Chain(dve, chain))
            for m, (o, mean, gain, factor, gate) in enumerate(jobs):
                if factor != 1.0:
                    chains[0].then(dve.tensor_scalar(factors[:, m:m + 1], gain, factor, None, ALU.mult))
        else:
            ch = chains[0]
            o, mean, gain, factor, gate = jobs[n - 1]
            rs = sq[(n - 1) % 2]
            dve.wait_ge(root, n)
            ch.then(dve.reciprocal(rs, rs))
            last = dve.scalar_tensor_tensor(out=o, in0=o, scalar=gain if factor == 1.0 else factors[:, n - 1:n], in1=rs,
                                            op0=ALU.mult, op1=ALU.mult)
            if gate is not None:
                ch(last)
                dve.wait_ge(tanh_done, n)
                ch.then(dve.scalar_tensor_tensor(out=gate, in0=th[n - 1], scalar=1.0, in1=gate, op0=ALU.add, op1=ALU.mult))
                last = dve.scalar_tensor_tensor(out=o, in0=gate, scalar=0.5, in1=o, op0=ALU.mult, op1=ALU.mult)
            last.then_inc(finished, 1)

    w = Work(N + 1, tensor, scalar, vector)
    w.finished = finished
    return w


def turn_tiles(k, tiles, banks):
    turned, copied = k.sem(), k.sem()

    def tensor(pe, t):
        for i in range(TB):
            b = slice(i * P, (i + 1) * P)
            last = pe.transpose(k.bank(banks[t])[:, b], tiles[t][:, b], k.c("ident"))
        last.then_inc(turned, 1)

    def scalar(act, t):
        act.wait_ge(turned, t + 1)
        act.activation(tiles[t], k.bank(banks[t]), ACT.Copy).then_inc(copied, 1)

    w = Work(len(tiles), tensor, scalar)
    w.copied = copied
    return w


def retention(k, q, key, val, buf, values_turned):
    scores_done, decayed, out_done, copied = (k.sem() for _ in range(4))
    units = [(h, s) for h in range(4) for s in range(TB)]
    U = len(units)
    decay = k.c("decay")

    def tensor(pe, u):
        if u < U:
            h, s = units[u]
            if u >= 4:
                pe.wait_ge(decayed, u - 3)
            pe.matmul(k.bank(2 + u % 4)[:, 0:T - s * P], key[h // 2][HALF[h % 2], s * P:(s + 1) * P],
                      q[h // 2][HALF[h % 2], s * P:T], start=True, stop=True).then_inc(scores_done, 1)
        if u >= 2:
            v = u - 2
            h, s = units[v]
            if v == 0:
                pe.wait_ge(values_turned, 2)
            pe.wait_ge(decayed, v + 1)
            pe.matmul(k.bank(6 + h // 2)[HALF[h % 2], s * P:T], val[h // 2][:, s * P + 64 * (h % 2):s * P + 64 * (h % 2) + 64],
                      buf[v % 8][:, 0:T - s * P], start=(s == 0), stop=(s == TB - 1)).then_inc(out_done, 1)

    def vector(dve, u):
        if u < U:
            h, s = units[u]
            dve.wait_ge(scores_done, u + 1)
            if u >= 8:
                dve.wait_ge(out_done, u - 7)
            dve.tensor_tensor(buf[u % 8][:, 0:T - s * P], decay[:, h * T:h * T + T - s * P],
                              k.bank(2 + u % 4)[:, 0:T - s * P], ALU.mult).then_inc(decayed, 1)

    def scalar(act, u):
        if u in (9, U + 1):
            j = 0 if u == 9 else 1
            act.wait_ge(out_done, 8 * (j + 1))
            act.activation(q[j], k.bank(6 + j), ACT.Copy).then_inc(copied, 1)

    w = Work(U + 2, tensor, scalar, vector)
    w.copied, w.out_done = copied, out_done
    return w


def short_conv(k, l, b, c, x):
    chain, ready, tapped, done = (k.sem() for _ in range(4))

    def gpsimd(pool, t):
        if t < 2:
            pool.tensor_tensor(c[t], c[t], x[t], ALU.mult).then_inc(ready, 1)
        elif t < 4:
            j = t - 2
            pool.wait_ge(tapped, j + 1)
            pool.tensor_tensor(b[j], b[j], x[j], ALU.mult).then_inc(done, 1)

    chains = []

    def vector(dve, t):
        if t == 0:
            chains.append(Chain(dve, chain))
        if t in (1, 2):
            ch, j = chains[0], t - 1
            dve.wait_ge(ready, j + 1)
            ch.then(dve.tensor_scalar(x[j], c[j], k.v("conv_w", 6 * l + 4 + j), k.v("conv_b", 2 * l + j), ALU.mult, ALU.add))
            ch.then(dve.scalar_tensor_tensor(out=x[j][:, 1:T], in0=c[j][:, 0:T - 1], scalar=k.v("conv_w", 6 * l + 2 + j),
                                             in1=x[j][:, 1:T], op0=ALU.mult, op1=ALU.add))
            dve.scalar_tensor_tensor(out=x[j][:, 2:T], in0=c[j][:, 0:T - 2], scalar=k.v("conv_w", 6 * l + j),
                                     in1=x[j][:, 2:T], op0=ALU.mult, op1=ALU.add).then_inc(tapped, 1)

    w = Work(4, vector=vector, gpsimd=gpsimd)
    w.done = done
    return w


def load_constants(k, held, const_in):
    nc = k.nc
    k.begin()
    loaded = k.sem()
    with nc.Block() as block:
        @block.sync
        def _(sp):
            sp.dma_start(held[:, :], const_in[:, CONST_W - CONST_PARTS[2][1]:CONST_W]).then_inc(loaded, 16)
            sp.wait_ge(loaded, 16)
            k.sync_work(sp)


def gated_branches(k, l, first, h, factor, src, src_ready, branch, out, gt, part):
    src_hi, src_lo, scaled, tanh_done, chain, read, made = (k.sem() for _ in range(7))
    ks = [range(0, 4), range(4, 6), range(6, 8)]

    def tensor(pe, t):
        d = t // 2
        n = first + 4 * d
        if t % 2 == 0:
            for b in range(3):
                if d >= 1:
                    pe.wait_ge(tanh_done, 3 * (d - 1) + b + 1)
                k.product(pe, k.bank(2 + b), n + b, h)
            return
        if d >= 1:
            pe.wait_ge(read, 3 * d)
        pe.wait_ge(k.lo_ready, n + 4)
        if d == 0:
            pe.wait_ge(src_lo, DT)
        u = (n + 3) % AHEAD
        for b in range(3):
            for i in ks[b]:
                w, end = slice(i * P, (i + 1) * P), i == ks[b][-1]
                pe.matmul(k.bank(5 + b), k.w_hi[:, u, w], branch.hi(i), start=(i == ks[b][0]), stop=False)
                pe.matmul(k.bank(5 + b), k.w_hi[:, u, w], branch.lo(i), start=False, stop=False)
                last = pe.matmul(k.bank(5 + b), k.w_lo[:, u, w], branch.hi(i), start=False, stop=end)
        last.then_inc(k.unit_used, 1)

    def scalar(act, t):
        d = t // 2
        n = first + 4 * d
        if t % 2:
            k.split_hi(act, n + 3 + AHEAD)
            return
        if d == 0:
            for i in range(DT):
                src_ready(act, i)
                act.activation(branch.hi(i), src[i], ACT.Copy).then_inc(src_hi, 1)
        else:
            act.wait_ge(read, 3 * d)
        for b in range(3):
            k.split_hi(act, n + b + AHEAD)
            act.wait_ge(scaled, 3 * d + b + 1)
            act.activation(gt[:, b * T:(b + 1) * T], k.bank(2 + b), ACT.Tanh, scale=0.5,
                           bias=k.v("b_gate", 24 * l + 8 * b + d)).then_inc(tanh_done, 1)

    chains = []

    def vector(dve, t):
        d = t // 2
        n = first + 4 * d
        if t == 0:
            chains.append(Chain(dve, chain))
            split_tiles_lo(dve, src, branch, src_hi, src_lo)
        ch = chains[0]
        if t % 2 == 0:
            for b in range(3):
                dve.wait_ge(k.unit_used, n + b + 1)
                dve.tensor_tensor(k.bank(2 + b), k.bank(2 + b), factor, ALU.mult).then_inc(scaled, 1)
                k.split_lo(dve, n + b + AHEAD)
            dve.wait_ge(tanh_done, 3 * (d + 1))
            ch.then(dve.tensor_scalar(gt, gt, 0.5, 0.5, ALU.mult, ALU.add))
            return
        dve.wait_ge(k.unit_used, n + 4)
        for b in range(3):
            dve.tensor_tensor(part[b], gt[:, b * T:(b + 1) * T], k.bank(5 + b), ALU.mult).then_inc(read, 1)
        k.split_lo(dve, n + 3 + AHEAD)
        dve.wait_ge(read, 3 * (d + 1))
        ch.then(dve.tensor_tensor(part[0], part[0], part[1], ALU.add))
        dve.tensor_tensor(out[d], part[0], part[2], ALU.add).then_inc(made, 1)
        dve.wait_ge(made, d + 1)

    w = Work(2 * DT, tensor, scalar, vector, end=first + 4 * DT)
    w.made = made
    return w


def epilogue(k, out):
    nc = k.nc
    k.begin()
    with nc.Block() as block:
        @block.sync
        def _(sp):
            sp.dma_start(out, k.xT[:, :, :]).then_inc(k.out_stored, 16)
            sp.wait_ge(k.out_stored, 16)


def program(nc, wts, x_in, const_in, mask_in, vec_in, onehot_in, relb_in, lora_in, lam_in, out, bias_dram):
    with ExitStack() as ctx:
        k = Core(nc, ctx, wts)
        first_block = ExitStack()
        first_const = k.open_constants(first_block, 1)
        with ExitStack() as phase:
            prologue(k, phase, first_const, x_in, const_in, mask_in, vec_in, onehot_in, relb_in, bias_dram)
        x = [k.x(d) for d in range(DT)]
        n = 0
        tiles = lambda a, b: [k.tile(t) for t in range(a, b)]

        def feed_forward(l, n):
            with ExitStack() as phase:
                k.open_part(phase, LOW, 3)
                xs, hidden = k.halves(phase, DT), k.halves(phase, MLP_HALF)
                k.begin()
                ln = layer_norm(k, "ln1_g", "ln1_b", l, 0, xs)
                up, down = [None, None], [None, None]
                schedule = ticks(ln)
                for half in range(2):
                    if half == 0:
                        up[0] = squared_relu(k, n, xs, hidden, rhs_ready=ln.out_lo)
                    else:
                        up[1] = squared_relu(k, n, xs, hidden, before=up[0],
                                             free=lambda pe, t: pe.wait_ge(down[0].added, t + 1))
                    n += MLP_HALF
                    down[half] = project_residual(
                        k, n, None, hidden, ALPHA if half == 0 else 1.0, units=2, rhs_ready=up[half].out_lo,
                        sums="x" if half else None, acc=k.tile(2), free=lambda pe, t, half=half: pe.wait_ge(up[half].relu_done, MLP_HALF - 7 + t))
                    n += 2 * DT
                    schedule += ticks(up[half]) + ticks(down[half])
                run(k, schedule)
            return n

        with ExitStack() as phase:
            k.open_part(phase, LOW)
            k.open_part(phase, MID)
            k.open_part(phase, EXTRA)
            with ExitStack() as inner:
                k.begin()
                keys, values = [k.tile(31 + 2 * (h % 2)) for h in range(4)], [k.tile(32 + 2 * (h % 2)) for h in range(4)]

                def place_of(c):
                    if c < 15:
                        return k.tile(c if c < 12 else 12 + c)
                    part, head = divmod(c - 15, 4)
                    return (k.tile(12 + head), keys[head], values[head])[part]

                place = [place_of(c) for c in AB_ORDER]
                mix = [c for c in AB_ORDER if c < 15]
                at = [AB_ORDER.index(c) for c in mix]
                v_at = [AB_ORDER.index(23 + h) for h in range(4)]
                lora_loaded, seen = k.sem(), []

                def load_loras(sp):
                    sp.dma_start(k.tile(41, 4), lora_in).then_inc(lora_loaded, 16)

                def set_free(act, t):
                    for h in (2, 3):
                        if AB_ORDER[t] == 19 + h:
                            act.wait_ge(seen[0].out_done, TB * (h - 1))

                proj = project(k, n, x, k.halves(inner, DT), place, turned=[t for t, c in enumerate(AB_ORDER) if 15 <= c < 23],
                               free=set_free)
                shift = rwkv_shift(k, [place_of(c) for c in mix], mix, proj.copied, at, [k.tile(35), k.tile(36), k.tile(45)])
                loras = rwkv_loras(k, shift.mixed, lora_loaded, tiles(41, 45), (3, 4))
                pairs = [Pair(k, j) for j in range(4)]
                scales = rwkv_scales(k, pairs, shift.mixed, loras, tiles(39, 45), (3, 4))
                causal = lambda i, j: [(k.m("ident"), k.m("causal"))] if i == j else []

                def head_ready(pe, h):
                    pe.wait_ge(proj.roped, 2 * h + 2)
                    pe.wait_ge(proj.copied, v_at[h] + 1)

                moba = attention(k, [([(k.tile(12 + h), keys[h], lambda i: 0, causal)], values[h], k.tile(12 + h))
                                     for h in range(4)], P ** -0.5, [k.tile(37)], k.tile(38), (5, 6, 7), ready=head_ready)
                seen.append(moba)
                scale_at = [14, 15, 17, 18, 18, 19, 20, 21, 22, 23, 24, 25, 25, 26, 26, 27]
                run(k, behind(proj, [(shift, lambda u: at[u] + 1), (loras, lambda u: 6 + (u + 1) // 2),
                                     (moba, lambda u: v_at[u // TB] + 2 + u % TB if u < 4 * TB else 0),
                                     (scales, lambda u: scale_at[u])]),
                    load_loras)
                n += 27
            with ExitStack() as inner:
                k.open_part(inner, EXT)
                for j, pair in enumerate(pairs):
                    pair.open((31, 47)[j % 2], 4 * (j % 2))

                def rest_of(pair, same_stage):
                    return (ticks(pair.invert(same_stage)) + ticks(pair.apply_inverse()) + ticks(pair.chunks())
                            + ticks(pair.outputs()))

                k.begin()
                first = [ticks(pair.matrices()) + rest_of(pair, True) for pair in pairs[0:2]]
                second = [ticks(pairs[j].matrices(before=pairs[j - 2])) for j in (2, 3)]
                both, after = braid(*first), braid(*second)
                run(k, both[:-4] + after[:2] + both[-4:-2] + after[2:4] + both[-2:] + after[4:])
                k.begin()
                run(k, braid(*(rest_of(pair, False) for pair in pairs[2:4])))
            with ExitStack() as inner:
                k.begin()
                run(k, ticks(project_residual(k, n, tiles(4, 8) + tiles(12, 16), k.halves(inner, DT), ALPHA, sums="x", acc=k.tile(0))))
                n += DT
        n = feed_forward(0, n)

        def near(i, j):
            return [(k.m("ident"), k.m("causal" if i == j else "band"))]

        def every(name):
            return lambda i, j: [(k.m("ident"), k.m(name + "causal" if i == j else name))]

        zero, band = lambda i: 0, lambda i: max(i - 1, 0) * P
        with ExitStack() as phase:
            k.open_part(phase, LOW)
            k.open_part(phase, MID)
            with ExitStack() as inner:
                k.begin()
                xs = k.halves(inner, DT)
                ln = layer_norm(k, "ln2_g", "ln2_b", 0, MID + 4, xs)
                sets = [[k.tile(8 + 5 * c + b) for b in range(5)] for c in range(3)]
                seen = []

                def set_free(act, t):
                    h = t // 5
                    if h >= 3 and t % 5 == 0:
                        act.wait_ge(seen[0].out_done, TB * (h - 2))

                proj = project(k, n, None, xs, [sets[h % 3][b] for h in range(8) for b in range(5)],
                               turned=[t for t in range(40) if t % 5 < 4], free=set_free,
                               rhs_ready=ln.out_lo)

                def head_ready(pe, h):
                    pe.wait_ge(proj.roped, 4 * h + 4)
                    pe.wait_ge(proj.copied, 5 * h + 5)

                heads = []
                for h in range(8):
                    q0, q1, q2, key, val = sets[h % 3]
                    heads.append(([(q1, key, zero, every("four")), (q2, key, zero, every("sixteen")), (q0, key, band, near)],
                                  val, k.tile(h)))
                dilated = attention(k, heads, P ** -0.5, [k.tile(MID + g) for g in range(3)], k.tile(MID + 3), (3, 4, 5, 6, 7),
                                    ready=head_ready)
                seen.append(dilated)
                n += 40

                def output_ready(act, h, n=n):
                    if h == 0:
                        act.wait_ge(k.unit_used, n)
                    act.wait_ge(dilated.out_copied, TB * (h + 1))

                split = split_work(k, tiles(0, 8), xs, output_ready)
                down = project_residual(k, n, None, xs, ALPHA, rhs_ready=split.out_lo, sums="x", acc=k.tile(8), early=3)
                n += DT
                schedule = ticks(ln) + behind(proj, [(dilated, lambda u: 5 * (u // TB) + 6 + u % TB)])
                rest = ticks(split)
                fill = [rest[0:2], rest[2:4], rest[4:7], [(down.early, 0)], [(down.early, 1)], [(down.early, 2)]]
                last = schedule[-6:]
                schedule = schedule[:-6] + [e for t in range(6) for e in [last[t]] + fill[t]] + rest[7:]
                run(k, schedule + ticks(down))
        n = feed_forward(1, n)
        first_block.close()

        second_const = k.open_constants(ctx, 2)
        with ExitStack() as phase:
            k.open_part(phase, LOW, 3)
            k.begin()
            constants_loaded = k.sem()

            def load_constants(sp):
                sp.dma_start(second_const[:, :], const_in[:, CONST_W - CONST_PARTS[2][1]:CONST_W]).then_inc(constants_loaded, 16)
                sp.wait_ge(constants_loaded, 16)

            run(k, ticks(layer_norm(k, "ln2_g", "ln2_b", 1, 0)), load_constants)
        for l in range(DEPTH):
            with ExitStack() as phase:
                k.open_part(phase, LOW)
                k.open_part(phase, MID, 4)
                with ExitStack() as mixing:
                    h = k.halves(mixing, DT)
                    rstd = k.space(mixing, 1)[:, 0, :]
                    with ExitStack() as inner:
                        k.open_part(inner, MID + 4, 12)
                        k.begin()
                        bias_loaded = k.sem()
                        lam_v, lam_p = k.tile(39)[:, 0:256], k.tile(39)[:, 256:384]

                        def load_bias(sp):
                            sp.dma_start(lam_v, lam_in[l]).then_inc(bias_loaded, 16)
                            with nc.allow_non_contiguous_dma(reason="one Toeplitz tile per row shift"):
                                for head in range(4):
                                    toeplitz = bass.AP(bias_dram.tensor, head * (T + P), [[1, P], [P, TB], [1, P]])
                                    sp.dma_start(blocks(k.tile(30 + head)), toeplitz).then_inc(bias_loaded, 16)

                        norm = rms_norm(k, "norm_mix_g", l, h, [k.tile(34), k.tile(35)], rstd, l > 0)
                        place = [k.tile(b + a) for a in range(4) for b in (0, 4, 8)] + [k.tile(t) for t in MIX_ORDER]
                        proj = project(k, n, None, h, place, turned=[12 + t for t, c in enumerate(MIX_ORDER) if c < 16], cos="cos2", sin="sin2", rows=P,
                                       rhs_ready=norm.out_lo, factor=rstd)
                        heads = head_norms(k, l, proj.copied, bias_loaded, lam_v, lam_p, [k.tile(37), k.tile(38)], 3)

                        def relative(head):
                            return lambda i, j: ([(k.tile(30 + head)[:, (i - j) * P:(i - j + 1) * P], k.c("flip"))]
                                                 + ([(k.m("ident"), k.m("causal"))] if i == j else []))

                        def head_ready(pe, a):
                            pe.wait_ge(heads.cleared, 4)
                            pe.wait_ge(bias_loaded, 80)
                            pe.wait_ge(heads.normed, 2 * a + 2)
                            pe.wait_ge(proj.copied, 3 * a + 3)

                        diff = attention(k, [([(k.tile(a), k.tile(4 + a), zero, relative(a)),
                                               (k.tile(a), k.tile(26 + a), zero, relative(a))], k.tile(8 + a), k.tile(a))
                                             for a in range(4)], 1.0, [k.tile(34), k.tile(35)], k.tile(36), (4, 5, 6, 7),
                                         ready=head_ready, difference=heads.nlam)
                        run(k, ticks(norm) + behind(proj, [(heads, lambda u: 3 * (u // 2) + u % 2 + 1),
                                                           (diff, lambda u: 5 + (5 * u + 3) // 4)]), load_bias)
                        n += 26
                    k.begin()
                    turn = turn_tiles(k, tiles(16, 18), (0, 1))
                    conv = short_conv(k, l, tiles(20, 22), tiles(22, 24), tiles(24, 26))
                    ret = retention(k, tiles(12, 14), tiles(14, 16), tiles(16, 18), tiles(4, 12), turn.copied)
                    def diff_ready(act, a):
                        if a == 0:
                            act.wait_ge(turn.copied, 2)

                    diff_norms = tile_norms(k, [(k.tile(a), "mean128", k.v("subln_g", l), 1.0 - LAM_INIT[l], None) for a in range(4)],
                                            tiles(26, 28), None, k.small[:, 44:48], (0, 1), diff_ready)

                    def ret_ready(act, a):
                        act.wait_ge(ret.copied, a + 1)
                        if a == 0:
                            act.wait_ge(diff_norms.finished, 4)
                            act.wait_ge(conv.done, 2)

                    ret_norms = tile_norms(k, [(k.tile(12 + a), "mean64", k.v("ret_g", l), 1.0, k.tile(18 + a)) for a in range(2)],
                                           tiles(26, 28), tiles(24, 26), None, (0, 1), ret_ready)

                    def src_ready(act, i):
                        if i < 4:
                            act.wait_ge(diff_norms.finished, i + 1)
                        elif i < 6:
                            act.wait_ge(ret_norms.finished, i - 3)
                        else:
                            act.wait_ge(conv.done, i - 5)

                    gates = gated_branches(k, l, n, h, rstd, tiles(0, 4) + tiles(12, 14) + tiles(20, 22), src_ready,
                                           k.halves(mixing, DT), tiles(4, 12), k.tile(14, 3), tiles(17, 20))
                    schedule = ticks(turn) + behind(ret, [(conv, lambda u: 2 * u), (diff_norms, lambda u: 4 * u + 3)])
                    n += 4 * DT

                    def y_ready(act, i, n=n):
                        if i == 0:
                            act.wait_ge(k.unit_used, n - 1)
                        act.wait_ge(gates.made, i + 1)

                    split = split_work(k, tiles(4, 12), h, y_ready)
                    down = project_residual(k, n, None, h, 1.0, rhs_ready=split.out_lo, sums="squares", acc=k.tile(2),
                                            sq=tiles(0, 2), early=2)
                    gate_ticks, splits = ticks(gates), ticks(split)
                    run(k, schedule + ticks(ret_norms) + gate_ticks[:-1] + splits[:-1] + gate_ticks[-1:] + splits[-1:]
                        + ticks(down.early) + ticks(down))
                    n += DT
            with ExitStack() as phase:
                k.open_part(phase, LOW, 5)
                h, act = k.halves(phase, DT), k.halves(phase, FFN_HALF)
                k.begin()
                norm = rms_norm(k, "norm_ffn_g", l, h, None, k.tile(4), True)
                schedule = ticks(norm)
                up, down = [None, None], [None, None]
                for half in range(2):
                    if half == 0:
                        up[0] = gated_ffn(k, l, 0, n, h, k.tile(4), act, h_ready=norm.out_lo)
                    else:
                        up[1] = gated_ffn(k, l, 1, n, h, k.tile(4), act, before=up[0],
                                          free=lambda pe, f: pe.wait_ge(down[0].added, 2 * f + 2))
                    n += FFN_TILES

                    def up_left(pe, t, half=half):
                        last = max(f for f in range(FFN_HALF) if f % 4 == t // 2)
                        pe.wait_ge(up[half].finished, last + 1)

                    down[half] = project_residual(k, n, None, act, 1.0, units=2, rhs_ready=up[half].out_lo, free=up_left,
                                                  sums="squares" if half and l + 1 < DEPTH else None, acc=k.tile(0), sq=tiles(2, 4))
                    n += 2 * DT
                    schedule += ticks(up[half]) + ticks(down[half])
                run(k, schedule)
        assert n == len(UNITS)
        epilogue(k, out)



def pack_weights(i):
    def unit(w):
        if w.shape[1] < P:
            w = np.concatenate([w, np.zeros((w.shape[0], P - w.shape[1]), w.dtype)], 1)
        return w.reshape(-1, P, P).transpose(1, 0, 2).reshape(P, -1)

    def split(w):
        return [unit(w[:, c:c + P]) for c in range(0, w.shape[1], P)]

    def mlp(w1, w2):
        half = MLP_HALF * P
        return [u for h in range(2) for u in split(w1[:, h * half:(h + 1) * half]) + split(w2[h * half:(h + 1) * half])]

    ends = AB_TILES[1:15] + [1824] + AB_TILES[16:] + [i["ab_w_in"].shape[2]]
    ab = [unit(i["ab_w_in"][0][:, a:b]) for a, b in zip(AB_TILES, ends)]
    def paired(units):
        order = np.concatenate([np.arange(16), np.arange(32, 48), np.arange(16, 32), np.arange(48, P)])
        return [u.reshape(P, -1, P)[:, :, order].reshape(P, -1) for u in units]

    ab[15:23] = paired(ab[15:23])
    g = [ab[c] for c in AB_ORDER]
    g += split(i["ab_w_out"][0]) + mlp(i["mlp_w1"][0], i["mlp_w2"][0])
    c = split(i["c_w_in"][0])
    c[0:32] = paired(c[0:32])
    g += [c[8 * part + h] for h in range(8) for part in range(5)] + split(i["c_w_out"][0]) + mlp(i["mlp_w1"][1], i["mlp_w2"][1])
    for l in range(DEPTH):
        w = i["w_in_2"][l]
        branch = np.concatenate([i["w_branch_da_2"][l], i["w_branch_ret_2"][l], i["w_branch_sc_2"][l]], 0)
        mix = split(w[:, 0:3328])
        g += [mix[4 * part + a] for a in range(4) for part in range(3)] + [mix[c] for c in MIX_ORDER]
        for d in range(DT):
            g += [unit(w[:, 3328 + b * D + d * P:3328 + b * D + (d + 1) * P]) for b in range(3)]
            g.append(unit(branch[:, d * P:(d + 1) * P]))
        g += split(i["w_out_2"][l])
        f, o = i["w_ffn_in_2"][l], i["w_ffn_out_2"][l]
        inner = FFN_TILES * P
        for h in range(2):
            rows = slice(h * FFN_HALF * P, (h + 1) * FFN_HALF * P)
            g += [unit(f[:, s + c * P:s + (c + 1) * P]) for c in range(h * FFN_HALF, (h + 1) * FFN_HALF) for s in (0, inner)]
            g += split(o[rows])
    return np.concatenate(g, 1)


def pack_vectors(i):
    def cols(v):
        v = np.asarray(v).reshape(-1)
        pad = -len(v) % P
        return np.concatenate([v, np.zeros(pad, v.dtype)]).reshape(-1, P).T

    def twice(v):
        return np.concatenate([v, v], -1)

    def dw(w):
        return w

    parts = {
        "w0": i["ab_w0"], "a0": i["ab_a0"], "b_gate": i["b_gate_2"], "mix": i["ab_shift_mix"], "k_k": i["ab_k_k"],
        "k_a": i["ab_k_a"], "r_k": i["ab_r_k"], "lnx_g": i["ab_lnx_g"], "lnx_b": i["ab_lnx_b"],
        "ln1_g": i["ln1_g"], "ln1_b": i["ln1_b"], "ln2_g": i["ln2_g"], "ln2_b": i["ln2_b"],
        "norm_mix_g": i["norm_mix_g_2"], "norm_ffn_g": i["norm_ffn_g_2"],
        "da_q_g": twice(i["da_q_norm_g_2"]), "da_k_g": twice(i["da_k_norm_g_2"]), "subln_g": i["da_subln_g_2"],
        "ret_g": twice(i["ret_norm_g_2"]), "conv_w": dw(i["sc_conv_w_2"]), "conv_b": i["sc_conv_b_2"],
        "ffn_w": dw(i["ffn_conv_w_2"]), "ffn_b": i["ffn_conv_b_2"],
    }
    out = [cols(parts[name]) for name, _ in vector_entries()]
    return np.concatenate(out, 1)


def build(nc, shapes):
    ap = {n: nc.dram_tensor("in_" + n, s, mybir.dt.from_np(np.dtype(d)), kind="ExternalInput").ap() for n, (s, d) in shapes.items()}
    out = nc.dram_tensor("out", (P, DT, T), F32, kind="ExternalOutput").ap()
    bias_dram = nc.dram_tensor("bias_by_distance", (4, T + P), F32, kind="Internal").ap()
    program(nc, ap["weights"], ap["x"], ap["const"], ap["mask"], ap["vectors"], ap["onehot"], ap["rel_bias"],
            ap["lora"], [ap["lam0"], ap["lam1"]], out, bias_dram)




def kernel(**inputs):
    import concourse.bacc as bacc
    from concourse.bass_utils import run_bass_kernel_spmd as run

    i = {n: np.asarray(a) for n, a in inputs.items()}
    const, mask, onehot = constants()
    z = np.zeros((64, 512), np.float32)
    gup = i["ab_g_up"][0]
    lora = np.concatenate([np.concatenate([i["ab_w_up"][0], z], 0), np.concatenate([z, i["ab_a_up"][0]], 0),
                           gup[0:P], np.concatenate([gup[P:], np.zeros((2 * P - gup.shape[0], 512), np.float32)], 0)], 1)
    arrays = {
        "weights": pack_weights(i),
        "x": np.ascontiguousarray(i["x"][0].T.reshape(DT, P, T).transpose(1, 0, 2)),
        "const": const, "mask": mask, "vectors": np.ascontiguousarray(pack_vectors(i)), "onehot": onehot,
        "rel_bias": np.ascontiguousarray(i["rel_bias_2"]), "lora": lora,
        "lam0": np.ascontiguousarray(np.broadcast_to(i["da_lambda_2"][0].reshape(1, 256), (P, 256))),
        "lam1": np.ascontiguousarray(np.broadcast_to(i["da_lambda_2"][1].reshape(1, 256), (P, 256))),
    }
    nc = bacc.Bacc("TRN2", target_bir_lowering=False, num_devices=1)
    build(nc, {n: (a.shape, a.dtype) for n, a in arrays.items()})
    got = run(nc, [{"in_" + n: a for n, a in arrays.items()}], core_ids=[0]).results[0]["out"]
    return np.ascontiguousarray(got.transpose(1, 0, 2).reshape(D, T).T).reshape(1, T, D)
```
